# Optimizing a Trainium2 kernel written in Bass

```python
import jax, jax.numpy as jnp
from jax import lax
import numpy as np

D_MODEL = 1024
BATCH = 1
SEQ = 128
DEPTH = 1
DEC_BATCH = 1
DEC_SEQ = 1024
PAST_LEN = 256

GRID_W = 64
CONV_W = D_MODEL // 2
DN_HEADS = 4
DK = 128
DV = 128
QK_W = DN_HEADS * DK
V_W = DN_HEADS * DV
D_MIX = CONV_W + V_W
D_FF = ((8 * D_MODEL // 3 + 127) // 128) * 128
CHUNK = 64
EPS = 1e-6
IN_COLS = 3 * CONV_W + 2 * QK_W + 2 * V_W + 4 * DN_HEADS

kernel_name = "hybrid_conv_gdn_diffusion_step"

def rmsnorm(x, w):
    xf = x.astype(jnp.float32)
    y = xf * lax.rsqrt(jnp.mean(xf * xf, axis=-1, keepdims=True) + EPS)
    return (y * w.astype(jnp.float32)).astype(x.dtype)

def l2norm(x):
    return x * lax.rsqrt(jnp.sum(x * x, axis=-1, keepdims=True) + EPS)

def row_conv3(u, w, row_len):
    b, l, ch = u.shape
    rows = l // row_len
    u4 = u.reshape(b, rows, row_len, ch)
    up = jnp.pad(u4, ((0, 0), (0, 0), (1, 1), (0, 0)))
    y = w[0] * up[:, :, :-2] + w[1] * up[:, :, 1:-1] + w[2] * up[:, :, 2:]
    return y.reshape(b, l, ch)

def grid_conv3x3(u, w, row_len):
    b, l, ch = u.shape
    rows = l // row_len
    u4 = u.reshape(b, rows, row_len, ch)
    y = lax.conv_general_dilated(u4, w[:, :, None, :], (1, 1), 'SAME',
                                 dimension_numbers=('NHWC', 'HWIO', 'NHWC'),
                                 feature_group_count=ch)
    return y.reshape(b, l, ch)

def chunked_gated_delta(q, k, v, beta, log_alpha, s0):
    b, l, h, dk = q.shape
    dv = v.shape[-1]
    n = l // CHUNK

    def blk(t):
        return jnp.moveaxis(t.reshape((b, n, CHUNK, h) + t.shape[3:]), 3, 1)

    q, k, v, beta = blk(q), blk(k), blk(v), blk(beta)
    g = jnp.cumsum(blk(log_alpha), axis=-1)
    idx = jnp.arange(CHUNK)
    strict = idx[:, None] > idx[None, :]
    incl = idx[:, None] >= idx[None, :]
    diff = g[..., :, None] - g[..., None, :]
    dec_strict = jnp.where(strict, jnp.exp(jnp.where(strict, diff, 0.0)), 0.0)
    dec_incl = jnp.where(incl, jnp.exp(jnp.where(incl, diff, 0.0)), 0.0)
    kb = k * beta[..., None]
    vb = v * beta[..., None]
    a_mat = jnp.eye(CHUNK, dtype=jnp.float32) + jnp.einsum('bhnid,bhnjd->bhnij', kb, k) * dec_strict
    u_val = lax.linalg.triangular_solve(a_mat, vb, left_side=True, lower=True, unit_diagonal=True)
    w_key = lax.linalg.triangular_solve(a_mat, kb * jnp.exp(g)[..., None], left_side=True,
                                        lower=True, unit_diagonal=True)
    qk = jnp.einsum('bhnid,bhnjd->bhnij', q, k) * dec_incl
    q_dec = q * jnp.exp(g)[..., None]
    g_last = g[..., -1:]
    k_end = k * jnp.exp(g_last - g)[..., None]
    chunk_decay = jnp.exp(g_last)[..., None]
    xs = tuple(jnp.moveaxis(t, 2, 0) for t in (u_val, w_key, qk, q_dec, k_end, chunk_decay))

    def step(s, inp):
        u_c, w_c, qk_c, qd_c, ke_c, dl_c = inp
        v_new = u_c - jnp.einsum('bhcd,bhde->bhce', w_c, s)
        o_c = jnp.einsum('bhcd,bhde->bhce', qd_c, s) + jnp.einsum('bhij,bhje->bhie', qk_c, v_new)
        s = s * dl_c + jnp.einsum('bhcd,bhce->bhde', ke_c, v_new)
        return s, o_c

    s_final, o = lax.scan(step, s0.astype(jnp.float32), xs)
    o = jnp.moveaxis(jnp.moveaxis(o, 0, 2), 1, 3).reshape(b, l, h, dv)
    return o, s_final

def mixer(h, row_len, s0_f, s0_b, w_in, conv_a_w, qkv_conv_w, a_log, dt_bias, o_norm_w, w_out):
    b, l, _ = h.shape
    z = h @ w_in
    cuts = [CONV_W, 2 * CONV_W, 3 * CONV_W, 3 * CONV_W + 2 * QK_W + V_W,
            3 * CONV_W + 2 * QK_W + 2 * V_W, 3 * CONV_W + 2 * QK_W + 2 * V_W + 2 * DN_HEADS]
    cb, cc, cx, qkv, gate, b_logit, a_in = jnp.split(z, cuts, axis=-1)
    y_conv = cb * row_conv3(cc * cx, conv_a_w, row_len)
    qkv = jax.nn.silu(row_conv3(qkv, qkv_conv_w, row_len)).astype(jnp.float32)
    q, k, v = jnp.split(qkv, [QK_W, 2 * QK_W], axis=-1)
    q = l2norm(q.reshape(b, l, DN_HEADS, DK)) * (DK ** -0.5)
    k = l2norm(k.reshape(b, l, DN_HEADS, DK))
    v = v.reshape(b, l, DN_HEADS, DV)
    beta = jax.nn.sigmoid(b_logit.astype(jnp.float32)).reshape(b, l, 2, DN_HEADS)
    log_alpha = -jnp.exp(a_log.astype(jnp.float32)) * jax.nn.softplus(
        a_in.astype(jnp.float32).reshape(b, l, 2, DN_HEADS) + dt_bias.astype(jnp.float32))
    o_f, s_f = chunked_gated_delta(q, k, v, beta[:, :, 0], log_alpha[:, :, 0], s0_f)
    rev = lambda t: t[:, ::-1]
    o_b, s_b = chunked_gated_delta(rev(q), rev(k), rev(v), rev(beta[:, :, 1]),
                                   rev(log_alpha[:, :, 1]), s0_b)
    o = o_f + rev(o_b)
    o = rmsnorm(o, o_norm_w) * jax.nn.silu(gate.astype(jnp.float32).reshape(b, l, DN_HEADS, DV))
    y = jnp.concatenate([y_conv, o.reshape(b, l, V_W).astype(h.dtype)], axis=-1) @ w_out
    return y, s_f, s_b

def conv_glu(h, row_len, w_up, ffn_conv_w, w_down):
    u, gt = jnp.split(h @ w_up, 2, axis=-1)
    gt = grid_conv3x3(gt, ffn_conv_w, row_len)
    return (jax.nn.gelu(gt) * u) @ w_down

def block(x, mod, row_len, s0_f, s0_b, norm1_w, w_in, conv_a_w, qkv_conv_w, a_log, dt_bias,
          o_norm_w, w_out, norm2_w, w_up, ffn_conv_w, w_down):
    shift1, scale1, gate1, shift2, scale2, gate2 = jnp.split(mod, 6, axis=-1)
    h = rmsnorm(x, norm1_w) * (1 + scale1) + shift1
    y, s_f, s_b = mixer(h, row_len, s0_f, s0_b, w_in, conv_a_w, qkv_conv_w, a_log, dt_bias,
                        o_norm_w, w_out)
    x = x + gate1 * y
    h = rmsnorm(x, norm2_w) * (1 + scale2) + shift2
    x = x + gate2 * conv_glu(h, row_len, w_up, ffn_conv_w, w_down)
    return x, s_f, s_b

def setup_inputs(seed: int = 0) -> dict:
    key = jax.random.key(seed)
    ks = jax.random.split(key, 24)
    nrm = lambda k, shape, s: jax.random.normal(k, shape, jnp.float32) * s
    dt = jnp.exp(jax.random.uniform(ks[10], (DEPTH, 2, DN_HEADS), jnp.float32,
                                    np.log(1e-3), np.log(1e-1)))
    return {
        "x_prompt": nrm(ks[0], (BATCH, SEQ, D_MODEL), 1.0),
        "x_sample": nrm(ks[1], (DEC_BATCH, DEC_SEQ, D_MODEL), 1.0),
        "state_deltanet": nrm(ks[2], (DEC_BATCH, DEPTH, 2, DN_HEADS, DK, DV), 0.3),
        "c": nrm(ks[3], (DEC_BATCH, D_MODEL), 1.0),
        "c_ctx": nrm(ks[4], (D_MODEL,), 1.0),
        "w_ada": nrm(ks[5], (DEPTH, D_MODEL, 6 * D_MODEL), 0.5 * D_MODEL ** -0.5),
        "b_ada": nrm(ks[6], (DEPTH, 6 * D_MODEL), 0.02),
        "norm1_w": 1.0 + nrm(ks[7], (DEPTH, D_MODEL), 0.02),
        "w_in": nrm(ks[8], (DEPTH, D_MODEL, IN_COLS), D_MODEL ** -0.5),
        "conv_a_w": nrm(ks[9], (DEPTH, 3, CONV_W), 0.5),
        "qkv_conv_w": nrm(ks[11], (DEPTH, 3, 2 * QK_W + V_W), 0.5),
        "a_log": jnp.log(jax.random.uniform(ks[12], (DEPTH, 2, DN_HEADS), jnp.float32, 1.0, 16.0)),
        "dt_bias": dt + jnp.log(-jnp.expm1(-dt)),
        "o_norm_w": 1.0 + nrm(ks[13], (DEPTH, DV), 0.02),
        "w_out": nrm(ks[14], (DEPTH, D_MIX, D_MODEL), D_MIX ** -0.5),
        "norm2_w": 1.0 + nrm(ks[15], (DEPTH, D_MODEL), 0.02),
        "w_up": nrm(ks[16], (DEPTH, D_MODEL, 2 * D_FF), D_MODEL ** -0.5),
        "ffn_conv_w": nrm(ks[17], (DEPTH, 3, 3, D_FF), 1.0 / 3.0),
        "w_down": nrm(ks[18], (DEPTH, D_FF, D_MODEL), D_FF ** -0.5),
        "final_norm_w": 1.0 + nrm(ks[19], (D_MODEL,), 0.02),
    }

def reference(x_prompt, x_sample, state_deltanet, c, c_ctx, w_ada, b_ada, norm1_w, w_in,
              conv_a_w, qkv_conv_w, a_log, dt_bias, o_norm_w, w_out, norm2_w, w_up,
              ffn_conv_w, w_down, final_norm_w):
    b_ctx, ctx_len, _ = x_prompt.shape
    xp = x_prompt
    xs = x_sample
    zero_state = jnp.zeros((b_ctx, DN_HEADS, DK, DV), jnp.float32)
    ctx_states = []
    for l in range(DEPTH):
        layer_w = (norm1_w[l], w_in[l], conv_a_w[l], qkv_conv_w[l], a_log[l], dt_bias[l],
                   o_norm_w[l], w_out[l], norm2_w[l], w_up[l], ffn_conv_w[l], w_down[l])
        mod_ctx = jax.nn.silu(c_ctx) @ w_ada[l] + b_ada[l]
        xp, s_f, s_b = block(xp, mod_ctx, ctx_len, zero_state, zero_state, *layer_w)
        ctx_states.append(jnp.stack([s_f, s_b], axis=1))
        mod_lat = (jax.nn.silu(c) @ w_ada[l] + b_ada[l])[:, None, :]
        xs, _, _ = block(xs, mod_lat, GRID_W, state_deltanet[:, l, 0], state_deltanet[:, l, 1],
                         *layer_w)
    y_prompt = rmsnorm(xp, final_norm_w)
    y_sample = rmsnorm(xs, final_norm_w)
    new_state_deltanet = jnp.stack(ctx_states, axis=1)
    return (y_prompt, y_sample, new_state_deltanet)


_drawn_inputs = setup_inputs


def setup_inputs(seed=0):
    import zlib

    import numpy as np

    out = dict(_drawn_inputs(seed))
    spreads = {}
    factors = {'state_deltanet': 2.838, 'o_norm_w': 22.394, 'norm2_w': 8.0, 'final_norm_w': 8.153}
    for name, (base, spread) in spreads.items():
        noise = np.random.default_rng([zlib.crc32(name.encode()), seed]).standard_normal(out[name].shape)
        drawn = base * np.exp(spread * noise) if base else spread * noise
        out[name] = __import__('jax').numpy.asarray(drawn.astype(out[name].dtype))
    for name, factor in factors.items():
        out[name] = (out[name] * factor).astype(out[name].dtype)
    return out
```

```python
import numpy as np

import concourse.bass as bass
from concourse import mybir
from concourse.alu_op_type import AluOpType as ALU

F32 = mybir.dt.float32
F32R = mybir.dt.float32r
I32 = mybir.dt.int32
ACT = mybir.ActivationFunctionType

P = 128
D = 1024
KT = D // P
LAT, CTX = 1024, 128
T = LAT + CTX
TW = 384
NT = T // TW
GRID = 64
ROWS = LAT // GRID
H = 4
TT_ = T // P
CH = 64
DFF = 2816
FB = DFF // P
EPS = 1e-6

C_BADA, C_N1, C_N2, C_NF, C_CA, C_QK, C_ON, C_C, C_CC, C_FFN = 0, 48, 56, 64, 72, 84, 120, 121, 129, 137
C_DTB = C_FFN + 9 * FB
C_ALOG = C_DTB + 2 * H
C_IND = C_ALOG + 2 * H
C_MAT = C_IND + 2
MATS = ["ident", "ones", "UI", "LI", "US", "LS", "CB0", "CB1", "L1", "U1"]
N_CONST = C_MAT + len(MATS) * P
LEVELS = (2, 4, 8, 16, 32)

N_ADA = 48
N_QKV, N_AB, N_CONV, N_GATE = 12, 1, 12, 4
N_Z = N_QKV + N_AB + N_CONV + N_GATE
N_OUT = 8
GROUPS = 5
RAW = 4
U_CONV = N_QKV + N_AB
U_GATE = U_CONV + N_CONV
U_OUT = N_Z
U_FFN = U_OUT + N_OUT
U_TAIL = U_FFN + 1 + 12 * GROUPS
N_SPLIT = U_TAIL + 5
B_FFN = U_FFN
B_TAIL = B_FFN + 1 + 16 * GROUPS
N_UNITS = N_ADA + N_SPLIT


def constants():
    p, f = np.meshgrid(np.arange(P), np.arange(P), indexing="ij")
    same = (p // CH) == (f // CH)
    m = {"ident": p == f, "ones": p >= 0, "UI": same & (p <= f), "LI": same & (p >= f),
         "US": same & (p < f), "LS": same & (p > f), "CB0": p < CH, "CB1": p >= CH}

    def level(s):
        return ((p // s) % 2 == 1) & (f // s == p // s - 1)
    m["L1"], m["U1"] = level(1), level(1).T
    mats = np.concatenate([m[k].astype(np.float32) for k in MATS], 1)
    preds = np.concatenate([x.astype(np.int32) for s in LEVELS for x in (level(s), level(s).T)], 1)
    ind = np.stack([np.arange(P) < CH, np.arange(P) >= CH], 1).astype(np.float32)
    return mats, preds, ind


class Tally:

    def __init__(self, sem):
        self.sem, self.n, self.i, self.per, self.n0 = sem, 0, None, 0, 0

    def inc(self, ins):
        ins.then_inc(self.sem, 1)
        self.n += 1
        return self.n

    def value(self, n=None):
        n = self.n if n is None else n
        return n if self.i is None else self.i * self.per + n

    def enter(self, i, per):
        self.i, self.per, self.n0 = i, per, self.n

    def leave(self, count):
        assert self.n - self.n0 == self.per, (self.n - self.n0, self.per)
        self.n = self.n0 + count * self.per
        self.i = None


def build(nc, const, preds, xT, s0, wts, y_out, s_out, yc_d, g_d):
    BLK = T * 4
    base = 16512
    at = [base]

    def place(name, shape, dt, off=None):
        n = 4
        for s in shape[1:]:
            n *= s
        if off is None:
            off = at[0]
            at[0] += (n + 31) // 32 * 32
        return nc.alloc_sbuf_tensor_at(name, shape, dt, offset=off)

    cst = place("cst", [P, N_CONST], F32)
    prd = place("prd", [P, 2 * len(LEVELS), P], I32)
    mod = place("mod", [P, 48, 2], F32)
    sc1 = place("sc1", [P, KT, 2], F32)
    sc2 = place("sc2", [P, KT, 2], F32)
    scT = place("scT", [P, KT, 2], F32)
    wqk = place("wqk", [P, 36], F32)
    onw = place("onw", [P, 1], F32)
    biases = place("biases", [P, 3], F32)
    dots = place("dots", [P, 160], F32)
    raw = place("raw", [P, RAW, D], F32)
    wH = place("wH", [P, 2, D], F32R)
    wL = place("wL", [P, 2, D], F32R)
    R0 = at[0]

    def blk(n):
        return R0 + n * BLK

    assert blk(35) < 229344
    hH = place("hH", [P, KT, T], F32R, blk(0))
    hL = place("hL", [P, KT, T], F32R, blk(8))
    X = place("X", [P, KT, T], F32, blk(16))
    QKV = place("QKV", [P, 12, T], F32, blk(16))
    sq = place("sq", [P, 2, T], F32, blk(28))
    rstd = place("rstd", [P, T], F32, blk(30))
    ub = place("ub", [P, 2, T], F32, blk(31))
    modrow = place("modrow", [2, 2, D], F32, blk(33))
    ZS, ZC = ROWS * (GRID + 2), CTX + 2
    zp = place("zp", [P, ZS + ZC], F32, blk(28))
    acc = place("acc", [P, T], F32, blk(30))
    ccb = place("ccb", [P, T], F32, blk(31))
    tb = place("tb", [P, T], F32, blk(32))
    abT = place("abT", [2 * 2 * H, T], F32, blk(33))
    oT = place("oT", [P, H, T], F32, blk(28))
    off = [blk(32)]

    def tail_place(name, shape, dt=F32):
        n = 4
        for s in shape[1:]:
            n *= s
        o = off[0]
        off[0] += n
        assert off[0] <= 229344, name
        return place(name, shape, dt, o)

    SC = tail_place("SC", [P, TT_, 2, 32])
    la = tail_place("la", [P, TT_, 8])
    gA = tail_place("gA", [P, TT_, 8])
    gB = tail_place("gB", [P, TT_, 8])
    gC = tail_place("gC", [P, TT_, 8])
    dl = []
    doff = [blk(0), blk(16), 0]

    def dplace(name, shape):
        n = 4
        for s in shape[1:]:
            n *= s
        if doff[0] + n <= doff[1]:
            o = doff[0]
            doff[0] += n
            return place(name, shape, F32, o)
        return tail_place(name, shape)

    for d in range(2):
        b = {}
        b["nrm"] = dplace(f"nrm{d}", [P, 8, P])
        o = doff[0] - 4096
        b["T"] = place(f"T{d}", [P, H, P], F32, o)
        b["TT"] = place(f"TT{d}", [P, H, P], F32, o + 2048)
        b["qk"] = dplace(f"qk{d}", [P, 8, P])
        for nm in ("v", "X", "D", "E", "ET", "QD", "A", "AT", "kbg", "ke0", "ke1", "vb", "vnew", "Sa", "Sb"):
            b[nm] = dplace(f"{nm}{d}", [P, H, P])
        b["sc"] = dplace(f"sc_{d}", [P, 32])
        dl.append(b)
    osq = place("osq", [P, 2, T], F32, blk(24))
    ors = place("ors", [P, T], F32, blk(26))
    ogt = place("ogt", [P, 2, T], F32, blk(32))
    om = place("om", [P, T], F32, blk(27))
    pH = place("pH", [P, 4, T], F32R, blk(24))
    pL = place("pL", [P, 4, T], F32R, blk(28))
    GS = (ROWS + 2) * (GRID + 2)
    G = place("G", [P, GS + ZC], F32, blk(32))
    fa = place("fa", [P, 2, T], F32, blk(32) + ((GS + ZC) * 4 + 31) // 32 * 32)
    sq2 = place("sq2", [P, 2, T], F32, blk(24))
    rstd2 = place("rstd2", [P, T], F32, blk(26))
    ub2 = place("ub2", [P, 2, T], F32, blk(27))
    sq3 = place("sq3", [P, 2, T], F32, blk(0))
    rstd3 = place("rstd3", [P, T], F32, blk(2))
    yb = place("yb", [P, 2, T], F32, blk(3))

    ps = nc.alloc_psum_tensor("ps", [P, 8, 512], F32)

    def mat(name):
        k = C_MAT + MATS.index(name) * P
        return cst[:, k:k + P]

    def pred(level, upper):
        return prd[:, 2 * level + upper, :]

    def bank3(side, n):
        return ps[:, 3 * side + n, 0:TW]

    names = ("cst_in prd_in x_in x_in1 s0_in0 s0_in1 st_out0 st_out1 bias_set z_init ffn_init oz "
             "wh_ready wl_ready ada_used modrow_ready modps_ready mod_ready sc_ready sq_ready "
             "sq_used rstd_ready u_ready hH_ready hL_ready blk_done side_free0 side_free1 conv_step "
             "conv_done tanh_done qkv_done yc_out gate_out abt_ready g_act g_dve g_pe sc_tab dpe dact ddve "
             "dpool x2_in yc_in0 yc_in1 gt_in0 gt_in1 o_sq o_st o_rs o_m mixH mixL fc_done gelu_done "
             "pH_ready pL_ready y_ready y_out0 y_out1 dve_step act_step").split()
    s = {n: nc.alloc_semaphore(n) for n in names}
    raw_in = [nc.alloc_semaphore(f"raw_in{k}") for k in range(RAW)]
    side_free = [s["side_free0"], s["side_free1"]]

    dot = [0]

    def plain(eng):
        dot[0] += 1
        o = dots[0:1, dot[0]:dot[0] + 1]
        if eng is nc.gpsimd:
            nc.gpsimd.tensor_tensor(o, biases[0:1, 0:1], biases[0:1, 0:1], ALU.add)
        else:
            nc.vector.memset(o, 0.0)

    def units(eng, lo, hi, body):
        n = (hi - lo) // 4
        if n > 1:
            with eng.Fori(0, n) as i:
                for u in range(4):
                    body(i * 4 + (lo + u), lo + u, i)
        else:
            n = 0
        for w in range(lo + 4 * n, hi):
            body(w, w, 0)

    def landed(w4, i):
        return (i + (w4 // RAW + 1)) * 16

    ORDER = [("act", "sq"), ("pool", "sc"), ("pool", "v"), ("pool", "dg"), ("pe", "nrm"), ("pe", "gb"),
             ("act", "lnq"), ("act", "lnk"), ("act", "eq"), ("act", "ek"), ("act", "eg"),
             ("dve", "qk"), ("dve", "D"), ("act", "r1"), ("act", "e1"), ("act", "r2"), ("act", "e2"),
             ("pe", "kk"), ("pe", "qkT"), ("pe", "trk"), ("pe", "trv"),
             ("pool", "em"), ("pool", "eb"), ("pool", "pm"), ("pool", "qd"),
             ("dve", "A"), ("pe", "trA"), ("act", "AT"), ("dve", "PT"), ("dve", "kbg"), ("dve", "ke0"),
             ("dve", "ke1"), ("dve", "vb"), ("pool", "t0"), ("pool", "t1"), ("pool", "tt0"), ("pool", "tt1")]
    for l in range(5):
        ORDER += [("pe", f"x{l}"), ("act", f"xc{l}")]
        if l < 4:
            ORDER += [("pe", f"y{l}"), ("dve", f"cp{l}")]
        ORDER += [("pe", f"yt{l}"), ("dve", f"cpt{l}")]
    ORDER += [("pe", "u"), ("pe", "wT"), ("act", "uc"), ("act", "wc")]
    for k in range(2):
        ORDER += [("pool", f"sd{k}"), ("pe", f"ws{k}"), ("dve", f"vn{k}"), ("pe", f"ds{k}"), ("pe", f"o{k}"),
                  ("dve", f"su{k}"), ("dve", f"oa{k}")]
    STEP = {}
    for e in ("pe", "act", "dve", "pool"):
        names_e = [n for en, n in ORDER if en == e]
        STEP[e] = {(n, d): 2 * k + d + 1 for k, n in enumerate(names_e) for d in range(2)}
    NSTEP = {e: len(v) for e, v in STEP.items()}
    SEM = {"pe": s["dpe"], "act": s["dact"], "dve": s["ddve"], "pool": s["dpool"]}

    with nc.Block() as block:

        @block.sync
        def _(sp):
            sp.dma_start(cst[:], const).then_inc(s["cst_in"], 16)

            def load(w, w4, i):
                sp.dma_start(raw[:, w4 % RAW, :], wts[w]).then_inc(raw_in[w4 % RAW], 16)

            for w in range(RAW):
                load(w, w, 0)
            sp.dma_start(X[:, 0:4, :], xT[:, 0:4, :]).then_inc(s["x_in"], 16)

            def after_ada(w, w4, i):
                sp.wait_ge(s["ada_used"], w - RAW + 1)
                load(w, w4, i)

            def after_split(w, w4, i):
                sp.wait_ge(s["wl_ready"], w - RAW - N_ADA + 1)
                load(w, w4, i)

            units(sp, RAW, N_ADA + RAW, after_ada)
            ahead = N_ADA + U_OUT + 2 + RAW
            units(sp, N_ADA + RAW, ahead, after_split)
            for e in ("pe", "act", "dve", "pool"):
                sp.wait_ge(SEM[e], TT_ * NSTEP[e])
            for d in range(2):
                sp.dma_start(s_out[:, d, :, :], dl[d]["Sa"][:]).then_inc(s[f"st_out{d}"], 16)
            for j in range(2):
                sp.dma_start(ogt[:, j, :], yc_d[:, j, :]).then_inc(s[f"yc_in{j}"], 16)
            for d in range(2):
                sp.wait_ge(s[f"st_out{d}"], 16)
            sp.dma_start(X[:], xT).then_inc(s["x2_in"], 16)
            for j in range(2, 4):
                sp.wait_ge(s["mixL"], j - 1)
                sp.dma_start(ogt[:, j % 2, :], yc_d[:, j, :]).then_inc(s[f"yc_in{j % 2}"], 16)
            for h in range(H):
                if h < 2:
                    sp.wait_ge(s["mixL"], h + 3)
                else:
                    sp.wait_ge(s["o_m"], h - 1)
                sp.dma_start(ogt[:, h % 2, :], g_d[:, h, :]).then_inc(s[f"gt_in{h % 2}"], 16)
            units(sp, ahead, N_UNITS, after_split)
            for b in range(KT):
                sp.wait_ge(s["y_ready"], b + 1)
                sp.dma_start(y_out[:, b, :], yb[:, b % 2, :]).then_inc(s[f"y_out{b % 2}"], 16)
            for k in range(2):
                sp.wait_ge(s[f"y_out{k}"], 16 * KT // 2)

        def delta(eng, me, stages):
            def iteration(it, first):
                def after(e, name, d, back=0):
                    if back and first:
                        return
                    eng.wait_ge(SEM[e], it * NSTEP[e] + (STEP[e][name, d] - back * NSTEP[e])
                                if not back else (it - 1) * NSTEP[e] + STEP[e][name, d])
                for e, name in ORDER:
                    if e == me:
                        for d in range(2):
                            last = stages(name, d, it, after)
                            last.then_inc(SEM[me], 1)
            return iteration

        def tiles(it):
            if isinstance(it, int) and it == TT_ - 1:
                return (it, it)
            return (it, (TT_ - 2) - it)

        def tok(it, d):
            return bass.ds(tiles(it)[d] * P, P) if not isinstance(it, int) else \
                slice(tiles(it)[d] * P, tiles(it)[d] * P + P)

        def bh(ap):
            return ap.unsqueeze(1).broadcast_to([P, H, P])

        def bc(ap):
            return ap.unsqueeze(2).broadcast_to([P, H, P])

        NB, GG, BG, ET0, ET1, CD0, CD1, BT = range(0, 32, 4)
        MA = ("LS", "US")
        MP = ("UI", "LI")
        ONE = (("L1", "U1"), ("U1", "L1"))

        def delta_run(eng, stages, me, between):
            run = delta(eng, me, stages)
            run(0, True)
            with eng.Fori(1, TT_ - 1) as it:
                run(it, False)
            between()
            run(TT_ - 1, False)

        def delta_pool(pool):
            def stages(name, d, it, after):
                b = dl[d]
                gp = nc.gpsimd
                sc = b["sc"]
                if name == "sc":
                    if isinstance(it, int) and it == 0:
                        pool.wait_ge(s["sc_tab"], 1)
                    after("dve", "vb", d, 1)
                    after("pool", "sd1", d, 1)
                    plain(pool)
                    return gp.tensor_copy(sc[:], SC[:, bass.ds(tiles(it)[d], 1), d, :] if not isinstance(it, int)
                                          else SC[:, tiles(it)[d]:tiles(it)[d] + 1, d, :])
                if name == "v":
                    after("dve", "vn1", d, 1)
                    plain(pool)
                    return gp.tensor_copy(b["v"][:], QKV[:, 8:12, tok(it, d)])
                if name == "dg":
                    after("pe", "u", d, 1)
                    after("pool", "sc", d)
                    return gp.tensor_tensor(b["X"][:], bh(mat("ident")), bc(sc[:, GG:GG + 4]), ALU.mult)
                if name == "em":
                    after("act", "e1", d)
                    return gp.tensor_tensor(b["E"][:], b["E"][:], bh(mat(MA[d])), ALU.mult)
                if name == "eb":
                    after("pool", "em", d)
                    return gp.tensor_tensor(b["E"][:], b["E"][:], bc(sc[:, NB:NB + 4]), ALU.mult)
                if name == "pm":
                    after("act", "e2", d)
                    return gp.tensor_tensor(b["ET"][:], b["ET"][:], bh(mat(MP[d])), ALU.mult)
                if name == "qd":
                    after("dve", "qk", d)
                    after("act", "eg", d)
                    return gp.tensor_tensor(b["QD"][:], b["QD"][:], b["qk"][:, 0:4, :], ALU.mult)
                if name == "t0":
                    after("dve", "qk", d)
                    after("dve", "A", d)
                    return gp.tensor_tensor(b["T"][:], b["A"][:], bh(mat(ONE[d][0])), ALU.mult)
                if name == "t1":
                    after("pool", "t0", d)
                    return gp.tensor_tensor(b["T"][:], b["T"][:], bh(mat("ident")), ALU.add)
                if name == "tt0":
                    after("act", "AT", d)
                    return gp.tensor_tensor(b["TT"][:], b["AT"][:], bh(mat(ONE[d][1])), ALU.mult)
                if name == "tt1":
                    after("pool", "tt0", d)
                    return gp.tensor_tensor(b["TT"][:], b["TT"][:], bh(mat("ident")), ALU.add)
                k = int(name[2])
                c = k if d == 0 else 1 - k
                cur = b["Sa"] if k == 0 else b["Sb"]
                cd = (CD0, CD1)[c]
                if k == 0:
                    after("dve", "su1", d, 1)
                    if isinstance(it, int) and it == TT_ - 1:
                        pool.wait_ge(s["oz"], 3)
                else:
                    after("dve", "su0", d)
                after("act", "r2", d)
                return gp.tensor_tensor(b["D"][:], cur[:], bc(sc[:, cd:cd + 4]), ALU.mult)
            pool.wait_ge(s["sc_tab"], 1)
            for d in range(2):
                pool.dma_start(dl[d]["Sa"][:], s0[:, d, :, :]).then_inc(s[f"s0_in{d}"], 16)
            for d in range(2):
                pool.wait_ge(s[f"s0_in{d}"], 16)
            delta_run(pool, stages, "pool", lambda: None)

        def delta_act(act):
            def stages(name, d, it, after):
                b = dl[d]
                A = nc.scalar.activation
                pb = 4 * d
                if name == "sq":
                    if isinstance(it, int) and it == 0 and d == 0:
                        act.wait_ge(s["qkv_done"], N_QKV)
                        act.wait_ge(s["gate_out"], 16 * N_GATE)
                        act.wait_ge(side_free[(N_Z - 1) % 2], (N_Z - 1) // 2 + 1)
                    after("pe", "wT", d, 1)
                    return A(b["nrm"][:], QKV[:, 0:8, tok(it, d)], ACT.Square)
                if name in ("lnq", "lnk"):
                    k = name == "lnk"
                    after("pe", "nrm", d)
                    return A(b["nrm"][:, 4 * k:4 * k + 4, :], ps[:, pb + k, :].rearrange("p (h n) -> p h n", h=H),
                             ACT.Ln, bias=biases[:, 0:1])
                if name in ("eq", "ek"):
                    k = name == "ek"
                    after("act", "lnk" if k else "lnq", d)
                    v = b["nrm"][:, 4 * k:4 * k + 4, :]
                    return A(v, v, ACT.Exp, scale=-0.5, bias=(0.0 if k else biases[:, 1:2]))
                if name == "eg":
                    after("pe", "gb", d)
                    after("pe", "o1", d, 1)
                    return A(b["QD"][:], ps[:, pb + 2, :].rearrange("p (h n) -> p h n", h=H), ACT.Exp)
                if name == "r1":
                    after("dve", "D", d)
                    return A(b["E"][:], b["D"][:], ACT.Relu)
                if name == "e1":
                    after("act", "r1", d)
                    return A(b["E"][:], b["E"][:], ACT.Exp, scale=-1.0)
                if name == "r2":
                    after("pe", "o1", d, 1)
                    return A(b["ET"][:], b["D"][:], ACT.Relu, scale=-1.0)
                if name == "e2":
                    after("act", "r2", d)
                    return A(b["ET"][:], b["ET"][:], ACT.Exp, scale=-1.0)
                if name == "AT":
                    after("pe", "trA", d)
                    return A(b["AT"][:], ps[:, pb + 3, :].rearrange("p (h n) -> p h n", h=H), ACT.Copy)
                if name[:2] == "xc":
                    after("pe", "x" + name[2:], d)
                    return A(b["X"][:], ps[:, pb, :].rearrange("p (h n) -> p h n", h=H), ACT.Copy)
                if name == "uc":
                    after("pe", "u", d)
                    return A(b["v"][:], ps[:, pb, :].rearrange("p (h n) -> p h n", h=H), ACT.Copy)
                if name == "wc":
                    after("pe", "wT", d)
                    after("pool", "t0", d)
                    return A(b["A"][:], ps[:, pb + 3, :].rearrange("p (h n) -> p h n", h=H), ACT.Copy)
            delta_run(act, stages, "act", lambda: None)

        def delta_dve(dve):
            V = nc.vector
            dve.wait_ge(s["prd_in"], 16)

            def stages(name, d, it, after):
                b = dl[d]
                sc = b["sc"]
                pb = 4 * d

                def bank(k):
                    return ps[:, pb + k, :].rearrange("p (h n) -> p h n", h=H)
                if name == "qk":
                    after("act", "ek", d)
                    after("act", "eq", d)
                    after("pe", "trk", d, 1)
                    after("pool", "qd", d, 1)
                    plain(dve)
                    return V.tensor_tensor(b["qk"][:], QKV[:, 0:8, tok(it, d)], b["nrm"][:], ALU.mult)
                if name == "D":
                    after("act", "eg", d)
                    after("pool", "sc", d)
                    after("dve", "su1", d, 1)
                    return V.tensor_tensor(b["D"][:], bank(2), bc(sc[:, GG:GG + 4]), ALU.subtract)
                if name == "A":
                    after("pe", "kk", d)
                    after("pool", "eb", d)
                    after("pe", "ws1", d, 1)
                    return V.tensor_tensor(b["A"][:], bank(3), b["E"][:], ALU.mult)
                if name == "PT":
                    after("pe", "qkT", d)
                    after("pool", "pm", d)
                    return V.tensor_tensor(b["ET"][:], bank(0), b["ET"][:], ALU.mult)
                if name in ("kbg", "ke0", "ke1"):
                    after("pe", "trk", d)
                    f = {"kbg": BG, "ke0": ET0, "ke1": ET1}[name]
                    if name == "kbg":
                        after("pe", "wT", d, 1)
                    else:
                        after("pe", "ds1", d, 1)
                    return V.tensor_tensor(b[name][:], bank(1), bc(sc[:, f:f + 4]), ALU.mult)
                if name == "vb":
                    after("pe", "trv", d)
                    return V.tensor_tensor(b["vb"][:], bank(2), bc(sc[:, BT:BT + 4]), ALU.mult)
                if name[:3] == "cpt":
                    l = int(name[3])
                    after("pe", f"yt{l}", d)
                    after("pool", "tt1", d)
                    if l:
                        after("dve", f"cpt{l - 1}", d)
                    plain(dve)
                    return V.copy_predicated(b["TT"][:], bh(pred(l, 1 - d)), bank(2))
                if name[:2] == "cp":
                    l = int(name[2])
                    after("pe", f"y{l}", d)
                    after("pool", "t1", d)
                    if l:
                        after("dve", f"cp{l - 1}", d)
                    plain(dve)
                    return V.copy_predicated(b["T"][:], bh(pred(l, d)), bank(1))
                k = int(name[2])
                c = k if d == 0 else 1 - k
                if name[:2] == "vn":
                    after("pe", f"ws{k}", d)
                    after("act", "uc", d)
                    r = slice(CH * c, CH * c + CH)
                    return V.tensor_tensor(b["vnew"][r], b["v"][r], bank(1)[r], ALU.subtract)
                if name[:2] == "su":
                    after("pe", f"ds{k}", d)
                    after("pool", f"sd{k}", d)
                    new = b["Sb"] if k == 0 else b["Sa"]
                    return V.tensor_tensor(new[:], b["D"][:], bank(0), ALU.add)
                after("pe", f"o{k}", d)
                t = tiles(it)[d]
                cols = slice(t * P + c * CH, t * P + c * CH + CH) if isinstance(it, int) else \
                    bass.ds(t * P + c * CH, CH)
                if d:
                    after("dve", f"oa{k}", 0)
                elif k:
                    after("dve", "oa0", 1)
                else:
                    after("dve", "oa1", 1, 1)
                plain(dve)
                return V.tensor_tensor(oT[:, :, cols], oT[:, :, cols],
                                       ps[:, pb + 2, 0:H * CH].rearrange("p (h n) -> p h n", h=H), ALU.add)

            def between():
                dve.wait_ge(s["ddve"], (TT_ - 1) * NSTEP["dve"])
                dve.wait_ge(s["dpe"], (TT_ - 1) * NSTEP["pe"])
                dve.wait_ge(s["dpool"], (TT_ - 1) * NSTEP["pool"])
                V.memset(dl[0]["Sa"][:], 0.0)
                V.memset(dl[1]["Sa"][:], 0.0).then_inc(s["oz"], 1)
            delta_run(dve, stages, "dve", between)

        def delta_pe(pe):
            M = nc.tensor.matmul

            def stages(name, d, it, after):
                b = dl[d]
                pb = 4 * d

                def bank(k, h):
                    return ps[:, pb + k, h * P:h * P + P]

                def four(k, left, right):
                    for h in range(H):
                        last = M(bank(k, h), left(h), right(h), start=True, stop=True)
                    return last
                if name == "nrm":
                    after("act", "sq", d)
                    after("dve", "su1", d, 1)
                    after("dve", "vn1", d, 1)
                    for k in range(2):
                        last = M(ps[:, pb + k, :], mat("ones"), b["nrm"][:, 4 * k:4 * k + 4, :].rearrange("p a n -> p (a n)"),
                                 start=True, stop=True)
                    return last
                if name == "gb":
                    after("pool", "dg", d)
                    after("dve", "oa1", d, 1)
                    return M(ps[:, pb + 2, :], mat("ones"), b["X"][:].rearrange("p a n -> p (a n)"),
                             start=True, stop=True)
                if name == "kk":
                    after("dve", "qk", d)
                    after("act", "wc", d, 1)
                    return four(3, lambda h: b["qk"][:, 4 + h, :], lambda h: b["qk"][:, 4 + h, :])
                if name == "qkT":
                    after("act", "lnk", d)
                    return four(0, lambda h: b["qk"][:, 4 + h, :], lambda h: b["qk"][:, h, :])
                if name == "trk":
                    for h in range(H):
                        last = nc.tensor.transpose(bank(1, h), b["qk"][:, 4 + h, :], mat("ident"))
                    return last
                if name == "trv":
                    after("pool", "v", d)
                    after("dve", "D", d)
                    for h in range(H):
                        last = nc.tensor.transpose(bank(2, h), b["v"][:, h, :], mat("ident"))
                    return last
                if name == "trA":
                    after("dve", "A", d)
                    for h in range(H):
                        last = nc.tensor.transpose(bank(3, h), b["A"][:, h, :], mat("ident"))
                    return last
                if name[0] == "x":
                    l = int(name[1])
                    if l == 0:
                        after("act", "AT", d)
                        after("pool", "t1", d)
                        after("dve", "PT", d)
                    else:
                        after("dve", f"cp{l - 1}", d)
                    return four(0, lambda h: b["AT"][:, h, :], lambda h: b["T"][:, h, :])
                if name[:2] == "yt":
                    l = int(name[2])
                    after("act", f"xc{l}", d)
                    if l == 0:
                        after("pool", "tt1", d)
                        after("dve", "vb", d)
                    else:
                        after("dve", f"cpt{l - 1}", d)
                    return four(2, lambda h: b["X"][:, h, :], lambda h: b["TT"][:, h, :])
                if name[0] == "y":
                    l = int(name[1])
                    after("act", f"xc{l}", d)
                    if l == 0:
                        after("pool", "tt1", d)
                        after("dve", "ke1", d)
                    else:
                        after("dve", f"cpt{l - 1}", d)
                    return four(1, lambda h: b["TT"][:, h, :], lambda h: b["X"][:, h, :])
                if name == "u":
                    after("dve", "cpt4", d)
                    after("dve", "vb", d)
                    return four(0, lambda h: b["TT"][:, h, :], lambda h: b["vb"][:, h, :])
                if name == "wT":
                    after("dve", "kbg", d)
                    return four(3, lambda h: b["kbg"][:, h, :], lambda h: b["TT"][:, h, :])
                k = int(name[-1])
                c = k if d == 0 else 1 - k
                cur = b["Sa"] if k == 0 else b["Sb"]
                if name[:2] == "ws":
                    after("act", "wc", d)
                    if k == 0:
                        after("dve", "su1", d, 1)
                        if isinstance(it, int) and it == TT_ - 1:
                            pe.wait_ge(s["oz"], 3)
                    else:
                        after("dve", "su0", d)
                    return four(1, lambda h: b["A"][:, h, :], lambda h: cur[:, h, :])
                if name[:2] == "ds":
                    after("dve", f"vn{k}", d)
                    after("act", "uc", d)
                    ke = b["ke0"] if c == 0 else b["ke1"]
                    return four(0, lambda h: ke[:, h, :], lambda h: b["vnew"][:, h, :])
                after("pool", "qd", d)
                if k:
                    after("dve", "oa0", d)
                for h in range(H):
                    out = ps[:, pb + 2, h * CH:h * CH + CH]
                    M(out, cur[:, h, :], b["QD"][:, h, c * CH:c * CH + CH], start=True, stop=False)
                    last = M(out, b["vnew"][:, h, :], b["ET"][:, h, c * CH:c * CH + CH], start=False, stop=True)
                return last
            delta_run(pe, stages, "pe", lambda: None)

        @block.gpsimd
        def _(pool):
            pool.dma_start(X[:, 4:8, :], xT[:, 4:8, :]).then_inc(s["x_in1"], 16)
            pool.dma_start(prd[:], preds).then_inc(s["prd_in"], 16)

            def low(u, u4):
                pool.wait_ge(s["wh_ready"], u + 1)
                nc.gpsimd.tensor_tensor(wL[:, u4 % 2, :], raw[:, u4 % RAW, :],
                                        wH[:, u4 % 2, :].bitcast(F32), ALU.subtract).then_inc(s["wl_ready"], 1)

            low(0, 0)
            low(1, 1)
            units(pool, 2, U_CONV + 2, lambda u, u4, i: low(u, u4))
            for j in range(4):
                for k in range(3):
                    w = U_CONV + 3 * j + k
                    low(w + 2, w + 2)
                pool.wait_ge(side_free[w % 2], w // 2 + 1)
                pool.dma_start(yc_d[:, j, :], ccb[:]).then_inc(s["yc_out"], 16)
            for g in range(N_GATE):
                w = U_GATE + g
                low(w + 2, w + 2)
                pool.wait_ge(side_free[w % 2], w // 2 + 1)
                pool.dma_start(g_d[:, g, :], acc[:]).then_inc(s["gate_out"], 16)

            pool.wait_ge(s["gate_out"], 16 * N_GATE)
            delta_pool(pool)
            for k in range(KT):
                pool.wait_ge(s["mixH"], k + 1)
                src = ogt[:, k % 2, :] if k < 4 else om[:]
                nc.gpsimd.tensor_tensor(hL[:, k, :], src, hH[:, k, :].bitcast(F32),
                                        ALU.subtract).then_inc(s["mixL"], 1)
            units(pool, U_OUT + 2, U_FFN + 2, lambda u, u4, i: low(u, u4))

            def p_low(f, slot, cnt):
                pool.wait_ge(s["pH_ready"], cnt)
                nc.gpsimd.tensor_tensor(pL[:, slot, :], fa[:, f % 2, :], pH[:, slot, :].bitcast(F32),
                                        ALU.subtract).then_inc(s["pL_ready"], 1)

            low(U_FFN + 2, U_FFN + 2)
            with pool.Fori(0, GROUPS) as g:
                u0 = U_FFN + 1
                for f in range(4):
                    low(g * 12 + (u0 + 2 * f + 2), u0 + 2 * f + 2)
                    low(g * 12 + (u0 + 2 * f + 3), u0 + 2 * f + 3)
                    p_low(f, f, g * 4 + (f + 1))
                for j in range(4):
                    low(g * 12 + (u0 + 8 + j + 2), u0 + 8 + j + 2)
            for u in range(U_TAIL + 2, N_SPLIT - 1):
                low(u, u)
            p_low(0, 0, 4 * GROUPS + 1)
            low(N_SPLIT - 1, N_SPLIT - 1)
            p_low(1, 1, 4 * GROUPS + 2)

        @block.scalar
        def _(act):
            A = nc.scalar.activation
            act.wait_ge(s["cst_in"], 16)
            act.wait_ge(s["bias_set"], 1)
            for k, col in enumerate((C_C, C_CC)):
                last = A(scT[:, :, k], cst[:, col:col + KT], ACT.Tanh, scale=0.5)
            last.then_inc(s["act_step"], 1)

            def ada_rows(m):
                act.wait_ge(s["ada_used"], 8 * m + 8)
                if m >= 2:
                    act.wait_ge(s["modps_ready"], m - 1)
                for j in range(2):
                    last = A(modrow[:, m % 2, 512 * j:512 * j + 512], ps[0:2, 4 + 2 * (m % 2) + j, :], ACT.Copy)
                last.then_inc(s["modrow_ready"], 1)

            astep = Tally(s["act_step"])
            astep.n = 1

            def norm_stats(k, sqb, rs, side):
                for b in range(KT):
                    if k == 0:
                        act.wait_ge(s["x_in"] if b < 4 else s["x_in1"], 16)
                    else:
                        xb = (U_OUT, B_TAIL + 3)[k - 1] + b
                        act.wait_ge(side_free[xb % 2], xb // 2 + 1)
                    if b >= 2:
                        act.wait_ge(s["sq_used"], 8 * k + b - 1)
                    A(sqb[:, b % 2, :], X[:, b, :], ACT.Square).then_inc(s["sq_ready"], 1)
                act.wait_ge(s["sq_used"], 8 * k + KT)
                for n in range(NT):
                    last = A(rs[:, n * TW:n * TW + TW], bank3(side, n), ACT.Ln, scale=1.0 / D, bias=biases[:, 0:1])
                astep.inc(last)
                act.wait_ge(s["act_step"], astep.value())
                A(rs[:], rs[:], ACT.Exp, scale=-0.5).then_inc(s["rstd_ready"], 1)

            def norm_high(k, ubuf, shift):
                act.wait_ge(s["mod_ready"], 2)
                for b in range(KT):
                    act.wait_ge(s["u_ready"], 8 * k + b + 1)
                    A(hH[:, b, 0:LAT], ubuf[:, b % 2, 0:LAT], ACT.Identity, bias=mod[:, shift * 8 + b, 0:1])
                    A(hH[:, b, LAT:T], ubuf[:, b % 2, LAT:T], ACT.Identity,
                      bias=mod[:, shift * 8 + b, 1:2]).then_inc(s["hH_ready"], 1)

            ada_rows(0)
            ada_rows(1)
            norm_stats(0, sq, rstd, 0)
            norm_high(0, ub, 0)
            for m in range(2, 6):
                ada_rows(m)

            def high(u, u4, i, done=None):
                act.wait_ge(raw_in[u4 % RAW], landed(u4 + N_ADA, i))
                A(wH[:, u4 % 2, :], raw[:, u4 % RAW, :], ACT.Copy).then_inc(s["wh_ready"], 1)

            high(0, 0, 0)
            high(1, 1, 0)

            def evac_rows(side, dst_s, dst_c, row):
                per = TW // GRID
                for n in range(NT):
                    rows = min(per, ROWS - n * per)
                    A(dst_s[:, row + n * per:row + n * per + rows, 1:GRID + 1],
                      bank3(side, n)[:, 0:rows * GRID].rearrange("p (r c) -> p r c", c=GRID), ACT.Copy)
                return A(dst_c[:, 1:CTX + 1], bank3(side, NT - 1)[:, LAT - (NT - 1) * TW:TW], ACT.Copy)

            zs = zp[:, 0:ZS].rearrange("p (r c) -> p r c", c=GRID + 2)
            zc = zp[:, ZS:ZS + ZC]

            act.wait_ge(s["z_init"], 1)

            def qkv_block(b, b4, i):
                act.wait_ge(s["blk_done"], b + 1)
                high(b + 2, b4 + 2, i)
                if b4:
                    act.wait_ge(s["conv_done"], b)
                evac_rows(b4 % 2, zs, zc, 0).then_inc(side_free[b4 % 2], 1)
                act.wait_ge(s["conv_done"], b + 1)
                if b4:
                    act.wait_ge(s["qkv_done"], b)
                A(tb[:], acc[:], ACT.Tanh).then_inc(s["tanh_done"], 1)

            for b in range(4):
                qkv_block(b, b, 0)
            with act.Fori(1, 3) as i:
                for u in range(4):
                    qkv_block(i * 4 + u, 4 + u, i - 1)

            b = N_QKV
            act.wait_ge(s["blk_done"], b + 1)
            high(b + 2, b + 2, 0)
            for n in range(NT):
                last = A(abT[:, n * TW:n * TW + TW], bank3(b % 2, n)[0:16], ACT.Copy)
            last.then_inc(side_free[b % 2], 1)
            for j in range(4):
                for k in range(3):
                    b = U_CONV + 3 * j + k
                    act.wait_ge(s["blk_done"], b + 1)
                    high(b + 2, b + 2, 0)
                    if k == 0:
                        if j:
                            act.wait_ge(s["yc_out"], 16 * j)
                        for n in range(NT):
                            last = A(ccb[:, n * TW:n * TW + TW], bank3(b % 2, n), ACT.Copy)
                        last.then_inc(side_free[b % 2], 1)
            for g in range(N_GATE):
                b = U_GATE + g
                act.wait_ge(s["blk_done"], b + 1)
                high(b + 2, b + 2, 0)
                act.wait_ge(side_free[(b - 2) % 2], (b - 2) // 2 + 1)
                act.wait_ge(s["qkv_done"], N_QKV)
                if g:
                    act.wait_ge(side_free[(b - 1) % 2], (b - 1) // 2 + 1)
                for n in range(NT):
                    last = A(tb[:, n * TW:n * TW + TW], bank3(b % 2, n), ACT.Tanh, scale=0.5)
                last.then_inc(s["tanh_done"], 1)

            act.wait_ge(s["abt_ready"], 1)
            act.wait_ge(s["tanh_done"], N_QKV + N_GATE)
            act.wait_ge(side_free[(N_Z - 1) % 2], (N_Z - 1) // 2 + 1)
            ab = ps[:, 6, 0:TT_ * 16].rearrange("p (t c) -> p t c", c=16)
            A(gA[:], ab[:, :, 0:8], ACT.Exp, scale=-1.0).then_inc(s["g_act"], 1)
            act.wait_ge(s["g_dve"], 2)
            A(gC[:], gC[:], ACT.Exp, scale=-1.0).then_inc(s["g_act"], 1)
            act.wait_ge(s["g_act"], 2)
            A(gC[:], gC[:], ACT.Ln, bias=biases[:, 2:3])
            A(cst[:, C_ALOG:C_ALOG + 8], cst[:, C_ALOG:C_ALOG + 8], ACT.Exp).then_inc(s["g_act"], 1)
            act.wait_ge(s["g_pe"], 1)

            def gp(k):
                return ps[:, 7, 72 * k:72 * k + 72].rearrange("p (t d h) -> p t d h", d=2, h=H)

            def field(f):
                return SC[:, :, :, f:f + 4]

            v4 = lambda t: t[:].rearrange("p t (d h) -> p t d h", d=2)
            act.wait_ge(s["g_dve"], 5)
            A(field(GG), gp(0), ACT.Copy)
            A(v4(gB), gp(0), ACT.Exp)
            A(v4(gC), gp(1), ACT.Exp)
            A(field(CD0), gp(2), ACT.Exp)
            A(field(CD1), gp(3), ACT.Exp).then_inc(s["g_act"], 1)

            delta_act(act)

            for j in range(4):
                act.wait_ge(s[f"yc_in{j % 2}"], 16 * (j // 2 + 1))
                A(hH[:, j, :], ogt[:, j % 2, :], ACT.Copy).then_inc(s["mixH"], 1)
            act.wait_ge(s["ddve"], TT_ * NSTEP["dve"])
            for h in range(H):
                A(osq[:, h % 2, :], oT[:, h, :], ACT.Square).then_inc(s["o_sq"], 1)
                act.wait_ge(s["o_st"], h + 1)
                if h:
                    act.wait_ge(s["dve_step"], h)
                for n in range(NT):
                    last = A(ors[:, n * TW:n * TW + TW], bank3((h + 1) % 2, n), ACT.Ln, scale=1.0 / P,
                             bias=biases[:, 0:1])
                astep.inc(last)
                act.wait_ge(s["act_step"], astep.value())
                A(ors[:], ors[:], ACT.Exp, scale=-0.5).then_inc(s["o_rs"], 1)
                act.wait_ge(s["o_m"], h + 1)
                A(hH[:, 4 + h, :], om[:], ACT.Copy).then_inc(s["mixH"], 1)

            def out_unit(b, b4, i):
                act.wait_ge(s["blk_done"], b + 1)
                high(b + 2, b4 + 2, i)
            units(act, U_OUT, U_FFN, lambda u, u4, i: out_unit(u, u4, i))
            norm_stats(1, sq2, rstd2, 1)
            norm_high(1, ub2, 3)

            gs = G[:, 0:GS].rearrange("p (r c) -> p r c", c=GRID + 2)
            gc = G[:, GS:GS + ZC]
            act.wait_ge(s["ffn_init"], 1)

            def gt_block(f, side):
                if not isinstance(f, int) or f:
                    act.wait_ge(s["fc_done"], f)
                evac_rows(side, gs, gc, 1).then_inc(side_free[side], 1)

            def gelu(f, f4):
                act.wait_ge(s["fc_done"], f + 1)
                A(fa[:, f4 % 2, :], fa[:, f4 % 2, :], ACT.Gelu_apprx_tanh).then_inc(s["gelu_done"], 1)

            def p_high(f, f4, slot, side, nfree):
                act.wait_ge(side_free[side], nfree)
                A(pH[:, slot, :], fa[:, f4 % 2, :], ACT.Copy).then_inc(s["pH_ready"], 1)

            act.wait_ge(s["blk_done"], B_FFN + 1)
            high(U_FFN + 2, U_FFN + 2, 0)
            gt_block(0, B_FFN % 2)
            with act.Fori(0, GROUPS) as g:
                ub0, b0 = U_FFN + 1, B_FFN + 1
                for f in range(4):
                    act.wait_ge(s["blk_done"], g * 16 + (b0 + 2 * f + 1))
                    high(g * 12 + (ub0 + 2 * f + 2), ub0 + 2 * f + 2, g * 3)
                    gelu(g * 4 + f, f)
                    gt_block(g * 4 + (f + 1), (b0 + 2 * f) % 2)
                    act.wait_ge(s["blk_done"], g * 16 + (b0 + 2 * f + 2))
                    high(g * 12 + (ub0 + 2 * f + 3), ub0 + 2 * f + 3, g * 3)
                    p_high(g * 4 + f, f, f, (b0 + 2 * f + 1) % 2, g * 8 + ((b0 + 2 * f + 1) // 2 + 1))
                for j in range(4):
                    act.wait_ge(s["blk_done"], g * 16 + (b0 + 8 + 2 * j + 2))
                    high(g * 12 + (ub0 + 8 + j + 2), ub0 + 8 + j + 2, g * 3)
            f0 = 4 * GROUPS
            act.wait_ge(s["blk_done"], B_TAIL + 1)
            high(U_TAIL + 2, U_TAIL + 2, 0)
            gelu(f0, f0)
            gt_block(f0 + 1, B_TAIL % 2)
            act.wait_ge(s["blk_done"], B_TAIL + 2)
            high(U_TAIL + 3, U_TAIL + 3, 0)
            p_high(f0, f0, 0, (B_TAIL + 1) % 2, (B_TAIL + 1) // 2 + 1)
            gelu(f0 + 1, f0 + 1)
            act.wait_ge(s["blk_done"], B_TAIL + 3)
            high(U_TAIL + 4, U_TAIL + 4, 0)
            p_high(f0 + 1, f0 + 1, 1, (B_TAIL + 2) % 2, (B_TAIL + 2) // 2 + 1)
            norm_stats(2, sq3, rstd3, 1)

        @block.vector
        def _(dve):
            V = nc.vector
            V.memset(biases[:, 0:1], EPS)
            V.memset(biases[:, 1:2], -0.5 * float(np.log(P)))
            V.memset(biases[:, 2:3], 1.0).then_inc(s["bias_set"], 1)
            dve.wait_ge(s["cst_in"], 16)
            V.tensor_scalar(wqk[:], cst[:, C_QK:C_QK + 36], 0.5, None, ALU.mult)
            V.tensor_scalar(onw[:], cst[:, C_ON:C_ON + 1], 0.5, None, ALU.mult).then_inc(s["oz"], 1)
            dve.wait_ge(s["act_step"], 1)
            dve.wait_ge(s["oz"], 1)
            for k, col in enumerate((C_C, C_CC)):
                last = V.scalar_tensor_tensor(scT[:, :, k], scT[:, :, k], 1.0, cst[:, col:col + KT], ALU.add, ALU.mult)
            last.then_inc(s["sc_ready"], 1)
            dve.wait_ge(s["sc_ready"], 1)
            V.tensor_scalar(scT[:], scT[:], 0.5, None, ALU.mult).then_inc(s["sc_ready"], 1)

            def add_bias(lo, hi, n):
                dve.wait_ge(s["modps_ready"], hi)
                V.tensor_tensor(mod[:, 8 * lo:8 * hi, :],
                                ps[:, 3, 16 * lo:16 * hi].rearrange("p (b k) -> p b k", k=2),
                                cst[:, C_BADA + 8 * lo:C_BADA + 8 * hi].unsqueeze(2).broadcast_to([P, 8 * (hi - lo), 2]),
                                ALU.add).then_inc(s["mod_ready"], 1)
                dve.wait_ge(s["mod_ready"], n)

            def scale_of(dst, row, col):
                V.scalar_tensor_tensor(dst[:], mod[:, 8 * row:8 * row + 8, :], 1.0,
                                       cst[:, col:col + 8].unsqueeze(2).broadcast_to([P, 8, 2]),
                                       ALU.add, ALU.mult).then_inc(s["mod_ready"], 1)

            def norm_apply(k, scl, ubuf, rs, shift):
                dve.wait_ge(s["rstd_ready"], k + 1)

                def u_of(b):
                    if b >= 2:
                        dve.wait_ge(s["hL_ready"], 8 * k + b - 1)
                    for which, (lo, hi) in enumerate(((0, LAT), (LAT, T))):
                        last = V.scalar_tensor_tensor(ubuf[:, b % 2, lo:hi], X[:, b, lo:hi], scl[:, b, which:which + 1],
                                                      rs[:, lo:hi], ALU.mult, ALU.mult)
                    last.then_inc(s["u_ready"], 1)
                u_of(0)
                for b in range(KT):
                    if b + 1 < KT:
                        u_of(b + 1)
                    dve.wait_ge(s["hH_ready"], 8 * k + b + 1)
                    dve.wait_ge(s["u_ready"], 8 * k + b + 1)
                    for which, (lo, hi) in enumerate(((0, LAT), (LAT, T))):
                        last = V.scalar_tensor_tensor(hL[:, b, lo:hi], ubuf[:, b % 2, lo:hi],
                                                      mod[:, shift * 8 + b, which:which + 1],
                                                      hH[:, b, lo:hi].bitcast(F32), ALU.add, ALU.subtract)
                    last.then_inc(s["hL_ready"], 1)

            add_bias(0, 2, 1)
            scale_of(sc1, 1, C_N1)
            dve.wait_ge(s["mod_ready"], 2)
            norm_apply(0, sc1, ub, rstd, 0)
            add_bias(2, 6, 3)
            scale_of(sc2, 4, C_N2)
            dve.wait_ge(s["hL_ready"], 8)
            V.memset(zp[:], 0.0).then_inc(s["z_init"], 1)

            zs = zp[:, 0:ZS].rearrange("p (r c) -> p r c", c=GRID + 2)
            zc = zp[:, ZS:ZS + ZC]
            step = Tally(s["dve_step"])
            acs = acc[:, 0:LAT].rearrange("p (r c) -> p r c", c=GRID)
            def conv3(chain, w, done):
                for tap, first in ((1, True), (0, False), (2, False)):
                    for dst, src in ((acs, zs[:, :, tap:tap + GRID]), (acc[:, LAT:T], zc[:, tap:tap + CTX])):
                        if first:
                            last = V.tensor_scalar(dst, src, w(tap), None, ALU.mult)
                        else:
                            last = V.scalar_tensor_tensor(dst, src, w(tap), dst, ALU.mult, ALU.add)
                    if tap != 2:
                        chain.inc(last)
                        dve.wait_ge(chain.sem, chain.value())
                last.then_inc(done, 1)

            def qkv_block(b, b4, chain):
                dve.wait_ge(side_free[b4 % 2], b4 // 2 + 1 if isinstance(b, int) else chain.i * 2 + b4 // 2 + 1)
                if b4:
                    dve.wait_ge(s["qkv_done"], b)
                col = (lambda t: wqk[:, t * 12 + b:t * 12 + b + 1]) if isinstance(b, int) else \
                    (lambda t: wqk[:, bass.ds(b + t * 12, 1)])
                conv3(chain, col, s["conv_done"])
                dve.wait_ge(s["tanh_done"], b + 1)
                dst = QKV[:, b, :] if isinstance(b, int) else QKV[:, bass.ds(b, 1), :]
                src = (lambda t: t[:]) if isinstance(b, int) else (lambda t: t[:].unsqueeze(1))
                V.scalar_tensor_tensor(dst, src(tb), 1.0, src(acc), ALU.add, ALU.mult).then_inc(s["qkv_done"], 1)

            chain = Tally(s["conv_step"])
            for b in range(4):
                qkv_block(b, b, chain)
            with dve.Fori(1, 3) as i:
                chain.enter(i - 1, 8)
                for u in range(4):
                    qkv_block(i * 4 + u, 4 + u, chain)
                chain.leave(2)
            for j in range(4):
                b = U_CONV + 3 * j
                dve.wait_ge(side_free[b % 2], b // 2 + 1)
                b += 1
                dve.wait_ge(s["blk_done"], b + 1)
                dve.wait_ge(s["conv_done"], N_QKV + j)
                per = TW // GRID
                for n in range(NT):
                    rows = min(per, ROWS - n * per)
                    V.tensor_tensor(zs[:, n * per:n * per + rows, 1:GRID + 1],
                                    bank3(b % 2, n)[:, 0:rows * GRID].rearrange("p (r c) -> p r c", c=GRID),
                                    ccb[:, n * TW:n * TW + rows * GRID].rearrange("p (r c) -> p r c", c=GRID), ALU.mult)
                V.tensor_tensor(zc[:, 1:CTX + 1], bank3(b % 2, NT - 1)[:, TW - CTX:TW], ccb[:, LAT:T],
                                ALU.mult).then_inc(side_free[b % 2], 1)
                dve.wait_ge(side_free[b % 2], b // 2 + 1)
                dve.wait_ge(s["qkv_done"], N_QKV)
                if j:
                    dve.wait_ge(side_free[(b - 2) % 2], (b - 2) // 2 + 1)
                conv3(chain, lambda t: cst[:, C_CA + 4 * t + j:C_CA + 4 * t + j + 1], s["conv_done"])
                b += 1
                dve.wait_ge(s["blk_done"], b + 1)
                dve.wait_ge(s["conv_done"], N_QKV + j + 1)
                for n in range(NT):
                    last = V.tensor_tensor(ccb[:, n * TW:n * TW + TW], bank3(b % 2, n), acc[:, n * TW:n * TW + TW],
                                           ALU.mult)
                last.then_inc(side_free[b % 2], 1)
            for g in range(N_GATE):
                b = U_GATE + g
                dve.wait_ge(s["tanh_done"], N_QKV + g + 1)
                if g:
                    dve.wait_ge(s["gate_out"], 16 * g)
                else:
                    dve.wait_ge(side_free[(b - 1) % 2], (b - 1) // 2 + 1)
                for n in range(NT):
                    last = V.scalar_tensor_tensor(acc[:, n * TW:n * TW + TW], tb[:, n * TW:n * TW + TW], 1.0,
                                                  bank3(b % 2, n), ALU.add, ALU.mult)
                last.then_inc(side_free[b % 2], 1)

            ab = ps[:, 6, 0:TT_ * 16].rearrange("p (t c) -> p t c", c=16)
            dve.wait_ge(s["g_act"], 1)
            b8 = lambda col: cst[:, col:col + 8].unsqueeze(1).broadcast_to([P, TT_, 8])
            V.tensor_tensor(gB[:], ab[:, :, 8:16], b8(C_DTB), ALU.add).then_inc(s["g_dve"], 1)
            dve.wait_ge(s["g_dve"], 1)
            V.scalar_tensor_tensor(gC[:], gB[:], -1.0, gB[:], ALU.mult, ALU.max)
            V.tensor_scalar(gA[:], gA[:], 1.0, None, ALU.add).then_inc(s["g_dve"], 1)
            dve.wait_ge(s["g_dve"], 2)
            dve.wait_ge(s["g_act"], 3)
            V.reciprocal(gA[:], gA[:])
            V.scalar_tensor_tensor(la[:], gB[:], 0.0, gC[:], ALU.max, ALU.add).then_inc(s["g_dve"], 1)
            dve.wait_ge(s["g_dve"], 3)
            V.scalar_tensor_tensor(la[:], la[:], -1.0, b8(C_ALOG), ALU.mult, ALU.mult).then_inc(s["g_dve"], 1)
            dve.wait_ge(s["g_dve"], 4)
            v4 = lambda t: t[:].rearrange("p t (d h) -> p t d h", d=2)

            def field(f):
                return SC[:, :, :, f:f + 4]
            V.tensor_scalar(field(NB), v4(gA), -1.0, None, ALU.mult)
            V.tensor_copy(field(BT), v4(gA)).then_inc(s["g_dve"], 1)
            dve.wait_ge(s["g_act"], 4)
            V.tensor_tensor(field(BG), v4(gA), v4(gB), ALU.mult)
            V.tensor_scalar(field(ET0), v4(gC), cst[:, C_IND:C_IND + 1], None, ALU.mult)
            V.tensor_scalar(field(ET1), v4(gC), cst[:, C_IND + 1:C_IND + 2], None, ALU.mult).then_inc(s["sc_tab"], 1)
            dve.wait_ge(s["gate_out"], 16 * N_GATE)
            for d in range(2):
                V.memset(dl[d]["vnew"][:], 0.0)
            V.memset(oT[:], 0.0).then_inc(s["oz"], 1)
            dve.wait_ge(s["oz"], 2)
            delta_dve(dve)

            for h in range(H):
                dve.wait_ge(s["o_rs"], h + 1)
                if h:
                    dve.wait_ge(s["mixL"], 4 + h)
                step.inc(V.tensor_tensor(om[:], oT[:, h, :], ors[:], ALU.mult))
                dve.wait_ge(s["dve_step"], step.value())
                dve.wait_ge(s[f"gt_in{h % 2}"], 16 * (h // 2 + 1))
                V.scalar_tensor_tensor(om[:], om[:], onw[:, 0:1], ogt[:, h % 2, :], ALU.mult,
                                       ALU.mult).then_inc(s["o_m"], 1)

            def residual(b, side, ob, gate):
                xs = (lambda lo, hi: X[:, ob, lo:hi])
                for n in range(NT):
                    lo, hi = n * TW, min((n + 1) * TW, LAT)
                    last = V.scalar_tensor_tensor(xs(lo, hi), bank3(side, n)[:, 0:hi - lo], mod[:, gate * 8 + ob, 0:1],
                                                  xs(lo, hi), ALU.mult, ALU.add)
                last = V.scalar_tensor_tensor(xs(LAT, T), bank3(side, NT - 1)[:, TW - CTX:TW],
                                              mod[:, gate * 8 + ob, 1:2], xs(LAT, T), ALU.mult, ALU.add)
                last.then_inc(side_free[side], 1)

            dve.wait_ge(s["x2_in"], 16)
            for ob in range(KT):
                b = U_OUT + ob
                dve.wait_ge(s["blk_done"], b + 1)
                residual(b, b % 2, ob, 2)
            dve.wait_ge(side_free[(U_FFN - 1) % 2], (U_FFN - 1) // 2 + 1)
            norm_apply(1, sc2, ub2, rstd2, 3)
            dve.wait_ge(s["hL_ready"], 16)
            V.memset(G[:], 0.0).then_inc(s["ffn_init"], 1)

            gs = G[:, 0:GS].rearrange("p (r c) -> p r c", c=GRID + 2)
            gc = G[:, GS:GS + ZC]
            fch = Tally(s["dve_step"])
            fch.n = step.n

            def conv9(f, f4, side, nfree):
                dve.wait_ge(side_free[side], nfree)
                dst = fa[:, f4 % 2, 0:LAT].rearrange("p (r c) -> p r c", c=GRID)
                dctx = fa[:, f4 % 2, LAT:T]
                w = (lambda t: cst[:, C_FFN + FB * t + f:C_FFN + FB * t + f + 1]) if isinstance(f, int) else \
                    (lambda t: cst[:, bass.ds(f + (C_FFN + FB * t), 1)])
                first = True
                for dy in range(3):
                    for dx in range(3):
                        src = gs[:, dy:dy + ROWS, dx:dx + GRID]
                        if first:
                            V.tensor_scalar(dst, src, w(3 * dy + dx), None, ALU.mult) if dy != 1 else None
                            last = V.tensor_scalar(dctx, gc[:, 0:CTX], w(3), None, ALU.mult)
                            first = False
                        else:
                            last = V.scalar_tensor_tensor(dst, src, w(3 * dy + dx), dst, ALU.mult, ALU.add)
                            if dy == 1 and dx:
                                last = V.scalar_tensor_tensor(dctx, gc[:, dx:dx + CTX], w(3 + dx), dctx,
                                                              ALU.mult, ALU.add)
                        if (dy, dx) == (2, 2):
                            last.then_inc(s["fc_done"], 1)
                        else:
                            fch.inc(last)
                            dve.wait_ge(s["dve_step"], fch.value())

            def product(f, f4, side, ndone):
                dve.wait_ge(s["gelu_done"], f + 1)
                dve.wait_ge(s["blk_done"], ndone)
                for n in range(NT):
                    last = V.tensor_tensor(fa[:, f4 % 2, n * TW:n * TW + TW], fa[:, f4 % 2, n * TW:n * TW + TW],
                                           bank3(side, n), ALU.mult)
                last.then_inc(side_free[side], 1)

            conv9(0, 0, B_FFN % 2, B_FFN // 2 + 1)

            def group(g, dyn):
                b0 = B_FFN + 1
                for f in range(4):
                    fi = g * 4 + f
                    bg = b0 + 2 * f
                    if dyn or f:
                        dve.wait_ge(s["pL_ready"], g * 4 + f)
                    conv9(g * 4 + (f + 1), f + 1, bg % 2, g * 8 + (bg // 2 + 1))
                    product(fi, f, (bg + 1) % 2, g * 16 + (bg + 2))
                for ob in range(KT):
                    b = b0 + 8 + ob
                    dve.wait_ge(s["blk_done"], g * 16 + (b + 1))
                    residual(b, b % 2, ob, 5)
            group(0, False)
            with dve.Fori(1, GROUPS) as g:
                fch.enter(g - 1, 32)
                group(g, True)
                fch.leave(GROUPS - 1)
            f0 = 4 * GROUPS
            dve.wait_ge(s["pL_ready"], f0)
            conv9(f0 + 1, f0 + 1, B_TAIL % 2, B_TAIL // 2 + 1)
            product(f0, f0, (B_TAIL + 1) % 2, B_TAIL + 2)
            product(f0 + 1, f0 + 1, (B_TAIL + 2) % 2, B_TAIL + 3)
            for ob in range(KT):
                b = B_TAIL + 3 + ob
                dve.wait_ge(s["blk_done"], b + 1)
                residual(b, b % 2, ob, 5)
            dve.wait_ge(side_free[(B_TAIL + 10) % 2], (B_TAIL + 10) // 2 + 1)
            dve.wait_ge(s["rstd_ready"], 3)
            for b in range(KT):
                if b >= 2:
                    dve.wait_ge(s[f"y_out{b % 2}"], 16 * (b // 2))
                V.scalar_tensor_tensor(yb[:, b % 2, :], X[:, b, :], cst[:, C_NF + b:C_NF + b + 1], rstd3[:],
                                       ALU.mult, ALU.mult).then_inc(s["y_ready"], 1)

        @block.tensor
        def _(pe):
            M = nc.tensor.matmul

            def ada(m):
                for kt in range(KT):
                    u = 8 * m + kt
                    pe.wait_ge(raw_in[u % RAW], (u // RAW + 1) * 16)
                    for j in range(2):
                        last = M(ps[0:2, 4 + 2 * (m % 2) + j, :], scT[:, kt, :], raw[:, u % RAW, 512 * j:512 * j + 512],
                                 start=(kt == 0), stop=(kt == KT - 1))
                    last.then_inc(s["ada_used"], 1)

            def turn(m):
                pe.wait_ge(s["modrow_ready"], m + 1)
                for b in range(KT):
                    last = M(ps[:, 3, 16 * m + 2 * b:16 * m + 2 * b + 2], modrow[:, m % 2, P * b:P * b + P],
                             mat("ident")[0:2, 0:2], start=True, stop=True)
                last.then_inc(s["modps_ready"], 1)

            def stats(k, sqb, side):
                for b in range(KT):
                    pe.wait_ge(s["sq_ready"], 8 * k + b + 1)
                    for n in range(NT):
                        last = M(bank3(side, n), mat("ones"), sqb[:, b % 2, n * TW:n * TW + TW],
                                 start=(b == 0), stop=(b == KT - 1))
                    last.then_inc(s["sq_used"], 1)

            pe.wait_ge(s["sc_ready"], 2)
            ada(0)
            ada(1)
            turn(0)
            turn(1)
            stats(0, sq, 0)
            for m in range(2, 6):
                ada(m)
                if m >= 3:
                    turn(m - 1)
            turn(5)
            pe.wait_ge(s["mod_ready"], 3)

            def product_block(slot, side, kts, left, right, ready):
                for k in range(kts):
                    ready(k)
                    rh, rl = right(k)
                    for w, lo in ((wH, False), (wL, True)):
                        lhs = left(w, k)
                        for n in range(NT):
                            c = slice(n * TW, n * TW + TW)
                            last = M(bank3(side, n), lhs, rh[:, c], start=(k == 0 and not lo),
                                     stop=(lo and k == kts - 1))
                            if not lo:
                                M(bank3(side, n), lhs, rl[:, c], start=False, stop=False)
                last.then_inc(s["blk_done"], 1)

            def model_block(u, u4, free, ready):
                pe.wait_ge(s["wl_ready"], u + 1)
                if free[1] is not None:
                    pe.wait_ge(side_free[free[0]], free[1])
                product_block(u4 % 2, free[0], KT, lambda w, k: w[:, u4 % 2, k * P:k * P + P],
                              lambda k: (hH[:, k, :], hL[:, k, :]), ready)

            h1_ready = lambda k: pe.wait_ge(s["hL_ready"], k + 1)
            for u in range(4):
                model_block(u, u, (u % 2, u // 2 or None), h1_ready)
            units(pe, 4, N_Z, lambda u, u4, i: model_block(u, u4, (u4 % 2, i * 2 + u4 // 2), h1_ready))
            pe.wait_ge(side_free[N_QKV % 2], N_QKV // 2 + 1)
            for t in range(TT_):
                last = M(ps[:, 6, 16 * t:16 * t + 16], abT[:, t * P:t * P + P], mat("ident")[0:16, 0:16],
                         start=True, stop=True)
            last.then_inc(s["abt_ready"], 1)
            pe.wait_ge(s["g_dve"], 4)
            for d in range(2):
                for k, m in enumerate((("UI", "LS"), ("LI", "US"))[d]):
                    M(ps[:, 7, 72 * k:72 * k + 72].rearrange("p (t c) -> p t c", c=8)[:, :, 4 * d:4 * d + 4],
                      mat(m), la[:, :, 4 * d:4 * d + 4], start=True, stop=True)
            for k in range(2):
                last = M(ps[:, 7, 144 + 72 * k:216 + 72 * k], mat(f"CB{k}"), la[:].rearrange("p t c -> p (t c)"),
                         start=True, stop=True)
            last.then_inc(s["g_pe"], 1)

            delta_pe(pe)

            for h in range(H):
                side = (h + 1) % 2
                pe.wait_ge(s["o_sq"], h + 1)
                if h >= 2:
                    pe.wait_ge(s["o_rs"], h - 1)
                for n in range(NT):
                    last = M(bank3(side, n), mat("ones"), osq[:, h % 2, n * TW:n * TW + TW], start=True, stop=True)
                last.then_inc(s["o_st"], 1)
            pe.wait_ge(s["o_rs"], 3)
            units(pe, U_OUT, U_FFN, lambda u, u4, i: model_block(
                u, u4, (u4 % 2, i * 2 + u4 // 2),
                lambda k: pe.wait_ge(s["mixL"], k + 1)))
            pe.wait_ge(side_free[1], (B_FFN - 2) // 2 + 1)
            stats(1, sq2, 1)
            pe.wait_ge(s["rstd_ready"], 2)
            model_block(U_FFN, U_FFN, (B_FFN % 2, B_FFN // 2), lambda k: pe.wait_ge(s["hL_ready"], 9 + k))

            def down(u, u4, b, bdyn, fis, width, p0):
                pe.wait_ge(s["wl_ready"], u + 1)
                for o in range(width):
                    pe.wait_ge(side_free[(b + o) % 2], bdyn + (b + o) // 2)
                    product_block(u4 % 2, (b + o) % 2, fis,
                                  lambda w, k: w[:, u4 % 2, (k * width + o) * P:(k * width + o) * P + P],
                                  lambda k: (pH[:, k, :], pL[:, k, :]),
                                  lambda k: pe.wait_ge(s["pL_ready"], p0 + (k + 1)))

            no_wait = lambda k: None
            with pe.Fori(0, GROUPS) as g:
                for k in range(8):
                    u, b = U_FFN + 1 + k, B_FFN + 1 + k
                    model_block(g * 12 + u, u, (b % 2, g * 8 + b // 2), no_wait)
                for j in range(4):
                    u, b = U_FFN + 9 + j, B_FFN + 9 + 2 * j
                    down(g * 12 + u, u, b, g * 8, 4, 2, g * 4)
            for k in range(3):
                model_block(U_TAIL + k, U_TAIL + k, ((B_TAIL + k) % 2, (B_TAIL + k) // 2), no_wait)
            for j in range(2):
                down(U_TAIL + 3 + j, U_TAIL + 3 + j, B_TAIL + 3 + 4 * j, 0, 2, 4, 4 * GROUPS)
            pe.wait_ge(side_free[1], (B_TAIL + 9) // 2 + 1)
            stats(2, sq3, 1)


def kernel(x_prompt, x_sample, state_deltanet, c, c_ctx, w_ada, b_ada, norm1_w, w_in, conv_a_w, qkv_conv_w,
           a_log, dt_bias, o_norm_w, w_out, norm2_w, w_up, ffn_conv_w, w_down, final_norm_w):
    import concourse.bacc as bacc
    from concourse.bass_utils import run_bass_kernel_spmd

    f = lambda a: np.asarray(a, dtype=np.float32)
    cols = lambda a: f(a).reshape(-1, P).T
    mats, preds, ind = constants()
    rep = lambda a: np.broadcast_to(f(a).reshape(1, -1), (P, 2 * H))
    const = np.ascontiguousarray(np.concatenate([
        cols(b_ada), cols(norm1_w), cols(norm2_w), cols(final_norm_w), cols(conv_a_w), cols(qkv_conv_w),
        cols(o_norm_w), cols(c), cols(c_ctx), cols(ffn_conv_w), rep(dt_bias), rep(a_log), ind, mats], 1))
    assert const.shape[1] == N_CONST
    tok = np.concatenate([f(x_sample)[0], f(x_prompt)[0]], 0)
    xT = np.ascontiguousarray(tok.T.reshape(KT, P, T).transpose(1, 0, 2))
    s0 = np.ascontiguousarray(f(state_deltanet)[0, 0].transpose(2, 0, 1, 3))

    def unit(w):
        k, n = w.shape
        return w.reshape(k // P, P, n).transpose(1, 0, 2).reshape(P, -1)

    wa, wi, wo, wu, wd = (f(a)[0] for a in (w_ada, w_in, w_out, w_up, w_down))
    cw = D // 2
    us = [wa[k * P:k * P + P, m * D:m * D + D] for m in range(6) for k in range(KT)]
    blk = lambda lo: unit(wi[:, lo:lo + P])
    q0 = 3 * cw
    us += [blk(q0 + b * P) for b in range(N_QKV)]
    g0 = q0 + 3 * H * P
    ab0 = g0 + H * P
    us.append(unit(np.concatenate([wi[:, ab0:ab0 + 4 * H], wi[:, ab0 - P + 4 * H:ab0]], 1)))
    for j in range(4):
        us += [blk(cw + j * P), blk(2 * cw + j * P), blk(j * P)]
    us += [blk(g0 + b * P) for b in range(N_GATE)]
    us += [unit(wo[:, b * P:b * P + P]) for b in range(KT)]
    gt = lambda b: unit(wu[:, DFF + b * P:DFF + b * P + P])
    up = lambda b: unit(wu[:, b * P:b * P + P])
    us.append(gt(0))
    for g in range(GROUPS):
        for b in range(4 * g, 4 * g + 4):
            us += [gt(b + 1), up(b)]
        us += [unit(wd[4 * g * P:4 * (g + 1) * P, j * 256:j * 256 + 256]) for j in range(4)]
    b = 4 * GROUPS
    us += [gt(b + 1), up(b), up(b + 1)]
    us += [unit(wd[b * P:(b + 2) * P, j * 512:j * 512 + 512]) for j in range(2)]
    assert len(us) == N_UNITS
    wts = np.stack(us)

    nc = bacc.Bacc("TRN2", target_bir_lowering=False, num_devices=1)
    ins = {"const": const, "preds": preds.reshape(P, -1, P), "xT": xT, "s0": s0, "wts": wts}
    dts = {"preds": I32}
    args = [nc.dram_tensor(k, v.shape, dts.get(k, F32), kind="ExternalInput").ap() for k, v in ins.items()]
    y = nc.dram_tensor("y", (P, KT, T), F32, kind="ExternalOutput").ap()
    st = nc.dram_tensor("st", (P, 2, H, P), F32, kind="ExternalOutput").ap()
    yc = nc.dram_tensor("yc", (P, 4, T), F32, kind="Internal").ap()
    gd = nc.dram_tensor("gd", (P, 4, T), F32, kind="Internal").ap()
    build(nc, *args, y, st, yc, gd)
    r = run_bass_kernel_spmd(nc, [ins], core_ids=[0]).results[0]
    yt = r["y"].transpose(1, 0, 2).reshape(D, T).T
    return (np.ascontiguousarray(yt[LAT:])[None], np.ascontiguousarray(yt[:LAT])[None],
            np.ascontiguousarray(r["st"].transpose(1, 2, 0, 3))[None, None])
```

```python
import numpy as np

import concourse.bass as bass
from concourse import mybir
from concourse.alu_op_type import AluOpType as ALU

F32 = mybir.dt.float32
F32R = mybir.dt.float32r
I32 = mybir.dt.int32
ACT = mybir.ActivationFunctionType

P = 128
D = 1024
KT = D // P
LAT, CTX = 1024, 128
T = LAT + CTX
TW = 384
NT = T // TW
GRID = 64
ROWS = LAT // GRID
H = 4
TT_ = T // P
CH = 64
DFF = 2816
FB = DFF // P
EPS = 1e-6

C_BADA, C_N1, C_N2, C_NF, C_CA, C_QK, C_ON, C_C, C_CC, C_FFN = 0, 48, 56, 64, 72, 84, 120, 121, 129, 137
C_DTB = C_FFN + 9 * FB
C_ALOG = C_DTB + 2 * H
C_IND = C_ALOG + 2 * H
C_MAT = C_IND + 2
MATS = ["ident", "ones", "UI", "LI", "US", "LS", "CB0", "CB1", "E0", "E1", "I0", "I1", "D32", "OU", "OL"]
C_SUB = C_MAT + len(MATS) * P
Q = 32
N_CONST = C_SUB + 3 * Q
LEVELS = (2, 4, 8, 16)
BIG = 1e30

N_ADA = 48
N_QKV, N_AB, N_CONV, N_GATE = 12, 1, 12, 4
N_Z = N_QKV + N_AB + N_CONV + N_GATE
N_OUT = 8
GROUPS = 5
RAW = 4
U_CONV = N_QKV + N_AB
U_GATE = U_CONV + N_CONV
U_OUT = N_Z
U_FFN = U_OUT + N_OUT
U_TAIL = U_FFN + 1 + 12 * GROUPS
N_SPLIT = U_TAIL + 5
B_FFN = U_FFN
B_TAIL = B_FFN + 1 + 16 * GROUPS
B_NORM = 16
N_UNITS = N_ADA + N_SPLIT


def constants():
    p, f = np.meshgrid(np.arange(P), np.arange(P), indexing="ij")
    same = (p // CH) == (f // CH)
    m = {"ident": p == f, "ones": p >= 0, "UI": same & (p <= f), "LI": same & (p >= f),
         "US": same & (p < f), "LS": same & (p > f), "CB0": p < CH, "CB1": p >= CH}
    m["E0"], m["E1"] = (np.where(m[k], 0.0, BIG) for k in ("LS", "US"))
    m["I0"], m["I1"] = (np.where(m[k], 0.0, -BIG) for k in ("UI", "LI"))
    m["D32"] = p // Q == f // Q
    m["OU"], m["OL"] = m["US"] & ~m["D32"], m["LS"] & ~m["D32"]

    def level(s):
        return ((p // s) % 2 == 1) & (f // s == p // s - 1)

    def compact(x):
        return np.concatenate([x[q:q + Q, q:q + Q] for q in range(0, P, Q)], 0)
    sub = [compact(p == f), -1.0 * compact(level(1)), -1.0 * compact(level(1).T)]
    mats = np.concatenate([m[k].astype(np.float32) for k in MATS] + [x.astype(np.float32) for x in sub], 1)
    preds = np.concatenate([compact(x).astype(np.int32) for s in LEVELS for x in (level(s), level(s).T)], 1)
    ind = np.stack([np.arange(P) < CH, np.arange(P) >= CH], 1).astype(np.float32)
    return mats, preds, ind


class Tally:

    def __init__(self, sem):
        self.sem, self.n, self.i, self.per, self.n0 = sem, 0, None, 0, 0

    def inc(self, ins):
        ins.then_inc(self.sem, 1)
        self.n += 1
        return self.n

    def value(self, n=None):
        n = self.n if n is None else n
        return n if self.i is None else self.i * self.per + n

    def enter(self, i, per):
        self.i, self.per, self.n0 = i, per, self.n

    def leave(self, count):
        assert self.n - self.n0 == self.per, (self.n - self.n0, self.per)
        self.n = self.n0 + count * self.per
        self.i = None


def build(nc, const, preds, xT, s0, wts, y_out, s_out, yc_d, g_d):
    BLK = T * 4
    base = 16512
    at = [base]

    def place(name, shape, dt, off=None):
        n = 4
        for s in shape[1:]:
            n *= s
        if off is None:
            off = at[0]
            at[0] += (n + 31) // 32 * 32
        return nc.alloc_sbuf_tensor_at(name, shape, dt, offset=off)

    cst = place("cst", [P, N_CONST], F32)
    prd = place("prd", [P, 2 * len(LEVELS), Q], I32)
    mod = place("mod", [P, 48, 2], F32)
    sc1 = place("sc1", [P, KT, 2], F32)
    sc2 = place("sc2", [P, KT, 2], F32)
    scT = place("scT", [P, KT, 2], F32)
    wqk = place("wqk", [P, 36], F32)
    onw = place("onw", [P, 1], F32)
    biases = place("biases", [P, 3], F32)
    dots = place("dots", [P, 160], F32)
    raw = place("raw", [P, RAW, D], F32)
    wH = place("wH", [P, 2, D], F32R)
    wL = place("wL", [P, 2, D], F32R)
    R0 = at[0]

    def blk(n):
        return R0 + n * BLK

    assert blk(35) < 229344
    hH = place("hH", [P, KT, T], F32R, blk(0))
    hL = place("hL", [P, KT, T], F32R, blk(8))
    X = place("X", [P, KT, T], F32, blk(16))
    QKV = place("QKV", [P, 12, T], F32, blk(16))
    sq = place("sq", [P, 2, T], F32, blk(28))
    rstd = place("rstd", [P, T], F32, blk(30))
    ub = place("ub", [P, 2, T], F32, blk(31))
    ss = place("ss", [P, T], F32, blk(15))
    ZS, ZC = ROWS * (GRID + 2), CTX + 2
    zp = place("zp", [P, ZS + ZC], F32, blk(28))
    acc = place("acc", [P, T], F32, blk(30))
    ccb = place("ccb", [P, T], F32, blk(31))
    tb = place("tb", [P, T], F32, blk(32))
    abT = place("abT", [2 * 2 * H, T], F32, blk(33))
    modrow = place("modrow", [2, 2, D], F32, blk(33))
    ycH = place("ycH", [P, T], F32R, blk(32))
    ycL = place("ycL", [P, T], F32R, blk(31))
    qn = place("qn", [P, T], F32, blk(34))
    oT = place("oT", [P, H, T], F32, blk(28))
    off = [blk(32)]

    def tail_place(name, shape, dt=F32):
        n = 4
        for s in shape[1:]:
            n *= s
        o = off[0]
        off[0] += n
        assert off[0] <= 229344, name
        return place(name, shape, dt, o)

    SC = tail_place("SC", [P, TT_, 2, 32])
    la = tail_place("la", [P, TT_, 8])
    gA = tail_place("gA", [P, TT_, 8])
    gB = tail_place("gB", [P, TT_, 8])
    gC = tail_place("gC", [P, TT_, 8])
    gL = tail_place("gL", [P, TT_, 8])
    dl = []
    doff = [blk(0), blk(16), 0]

    def dplace(name, shape):
        n = 4
        for s in shape[1:]:
            n *= s
        if doff[0] + n <= doff[1]:
            o = doff[0]
            doff[0] += n
            return place(name, shape, F32, o)
        return tail_place(name, shape)

    for d in range(2):
        b = {}
        b["qkv"] = dplace(f"dqkv{d}", [P, 12, P])
        for nm in ("R1", "R2", "A", "AT", "AT32", "TT", "kbg", "ke", "QD", "PT", "U", "W", "vnew"):
            b[nm] = dplace(f"{nm}{d}", [P, H, P])
        for nm in ("Sa", "Sb"):
            b[nm] = tail_place(f"{nm}{d}", [P, H, P])
        b["QE"], b["Xf"], b["vb"] = b["kbg"], b["A"], b["R1"]
        for nm in ("T", "Tt", "X"):
            b[nm] = dplace(f"{nm}{d}", [P, H, Q])
        b["sc"] = dplace(f"sc_{d}", [P, 32])
        b["cd"] = dplace(f"cd{d}", [P, 8])
        dl.append(b)
    osq = place("osq", [P, H, T], F32, blk(4))
    ors = place("ors", [P, H, T], F32, blk(12))
    og = place("og", [P, H, T], F32, blk(24))
    pH = place("pH", [P, 4, T], F32R, blk(24))
    pL = place("pL", [P, 4, T], F32R, blk(28))
    GS = (ROWS + 2) * (GRID + 2)
    G = place("G", [P, GS + ZC], F32, blk(32))
    fa = place("fa", [P, 2, T], F32, blk(32) + ((GS + ZC) * 4 + 31) // 32 * 32)
    sq2 = place("sq2", [P, 2, T], F32, blk(24))
    rstd2 = place("rstd2", [P, T], F32, blk(26))
    ub2 = place("ub2", [P, 2, T], F32, blk(27))
    ss2 = place("ss2", [P, T], F32, blk(29))
    ss3 = place("ss3", [P, T], F32, blk(5))
    sq3 = place("sq3", [P, 2, T], F32, blk(0))
    rstd3 = place("rstd3", [P, T], F32, blk(2))
    yb = place("yb", [P, 2, T], F32, blk(3))

    ps = nc.alloc_psum_tensor("ps", [P, 8, 512], F32)

    def mat(name):
        k = C_MAT + MATS.index(name) * P
        return cst[:, k:k + P]

    def pred(level, upper):
        return prd[:, 2 * level + upper, :]

    def bank3(side, n):
        return ps[:, 3 * side + n, 0:TW]

    names = ("cst_in prd_in x_in x_in1 s0_in0 s0_in1 st_out0 st_out1 bias_set z_init ffn_init oz "
             "wh_ready wl_ready ada_used modrow_ready modps_ready mod_ready qs_ready qs_done qs_read qr_ready qm_done sc_ready sq_ready "
             "sq_used st_done rstd_ready u_ready hH_ready hL_ready blk_done side_free0 side_free1 conv_step "
             "conv_done tanh_done qkv_done yc_out0 yc_out1 yc_high yc_low gate_out abt_ready g_act g_dve g_pe sc_tab pre_pe pre_act pre_dve "
             "pre_pool scan_pe scan_dve scan_pool x2_in yH_in0 yH_in1 yL_in0 yL_in1 gt_in o_sq o_st o_ln o_rs o_m mixH mixL fc_done gelu_done "
             "pH_ready pL_ready y_ready y_out0 y_out1 dve_step act_step").split()
    s = {n: nc.alloc_semaphore(n) for n in names}
    raw_in = [nc.alloc_semaphore(f"raw_in{k}") for k in range(RAW)]
    side_free = [s["side_free0"], s["side_free1"]]

    dot = [0]

    def plain(eng):
        dot[0] += 1
        o = dots[0:1, dot[0]:dot[0] + 1]
        if eng is nc.gpsimd:
            nc.gpsimd.tensor_tensor(o, biases[0:1, 0:1], biases[0:1, 0:1], ALU.add)
        elif eng is nc.scalar:
            nc.scalar.activation(o, biases[0:1, 0:1], ACT.Copy)
        else:
            nc.vector.memset(o, 0.0)

    def units(eng, lo, hi, body):
        n = (hi - lo) // 4
        if n > 1:
            with eng.Fori(0, n) as i:
                for u in range(4):
                    body(i * 4 + (lo + u), lo + u, i)
        else:
            n = 0
        for w in range(lo + 4 * n, hi):
            body(w, w, 0)

    def landed(w4, i):
        return (i + (w4 // RAW + 1)) * 16

    ORDER = {
        "pe": ["gb", "kk", "WS0", "qkT", "O0", "DS0", "trA", "WS1", "x0", "DS1", "O1",
               "y0", "trk", "x1", "y1", "trv", "x2", "y2", "x3", "y3", "x4", "yt", "u", "wT"],
        "act": ["cp", "eg", "e1", "e2", "nc", "at", "xc0", "kbg", "xc1", "ke", "xc2", "xc3", "uc", "wc"],
        "dve": ["g1", "VN0", "g2", "a", "SU0", "t0", "t1", "at32", "VN1", "tr", "ex", "SU1", "OA", "pt"]
               + [f"{k}{l}" for l in range(4) for k in ("cp", "tr", "ex")] + ["vb", "xf", "ca"],
        "pool": ["CD", "sc", "qd", "off"],
    }
    STEP, N_STEP = {}, {}
    for e, order in ORDER.items():
        for scan in (False, True):
            part = [n for n in order if n.isupper() == scan]
            N_STEP[e, scan] = 2 * len(part)
            STEP.update({(e, n, d): 2 * k + d + 1 for k, n in enumerate(part) for d in range(2)})
    SEM = {(e, scan): s[("scan_" if scan else "pre_") + e] for e in ORDER for scan in (False, True)
           if N_STEP[e, scan]}

    with nc.Block() as block:

        @block.sync
        def _(sp):
            sp.dma_start(cst[:], const).then_inc(s["cst_in"], 16)

            def load(w, w4, i):
                sp.dma_start(raw[:, w4 % RAW, :], wts[w]).then_inc(raw_in[w4 % RAW], 16)

            for w in range(RAW):
                load(w, w, 0)
            sp.dma_start(X[:, 0:4, :], xT[:, 0:4, :]).then_inc(s["x_in"], 16)

            def after_ada(w, w4, i):
                sp.wait_ge(s["ada_used"], w - RAW + 1)
                load(w, w4, i)

            def after_split(w, w4, i):
                sp.wait_ge(s["wl_ready"], w - RAW - N_ADA + 1)
                load(w, w4, i)

            units(sp, RAW, N_ADA + RAW, after_ada)
            ahead = N_ADA + U_OUT + 2 + RAW
            units(sp, N_ADA + RAW, ahead, after_split)
            for d in range(2):
                sp.wait_ge(SEM["act", False], (TT_ - 1) * N_STEP["act", False] + STEP["act", "cp", d])
            sp.dma_start(og[:], g_d).then_inc(s["gt_in"], 16)
            sp.dma_start(X[:], xT).then_inc(s["x2_in"], 16)
            sp.wait_ge(SEM["dve", True], TT_ * N_STEP["dve", True])
            for d in range(2):
                sp.dma_start(s_out[:, d, :, :], dl[d]["Sa"][:]).then_inc(s[f"st_out{d}"], 16)
            units(sp, ahead, N_UNITS, after_split)
            for b in range(KT):
                sp.wait_ge(s["y_ready"], b + 1)
                sp.dma_start(y_out[:, b, :], yb[:, b % 2, :]).then_inc(s[f"y_out{b % 2}"], 16)
            for k in range(2):
                sp.wait_ge(s[f"y_out{k}"], 16 * KT // 2)
                sp.wait_ge(s[f"st_out{k}"], 16)

        def delta_run(eng, me, stage, between=None):
            def run(tile, parts):
                for name in ORDER[me]:
                    scan = name.isupper()
                    if scan not in parts:
                        continue
                    t = tile if scan else (tile[0], tile[1] + 1)
                    for d in range(2):
                        def after(e, of, dd, back=0):
                            if isinstance(t[0], int) and t[1] < back:
                                return
                            n = N_STEP[e, of.isupper()]
                            eng.wait_ge(SEM[e, of.isupper()], t[0] * n + ((t[1] - back) * n + STEP[e, of, dd]))
                        stage(name, d, t, after).then_inc(SEM[me, scan], 1)
            run((0, -1), (False,))
            run((0, 0), (False, True))
            with eng.Fori(1, TT_ - 2) as i:
                run((i, 0), (False, True))
            run((0, TT_ - 2), (False, True))
            if between:
                between()
            run((0, TT_ - 1), (True,))

        def is_context(t):
            return isinstance(t[0], int) and t[1] == TT_ - 1

        def place_of(t, d):
            i, o = t
            if isinstance(i, int):
                return o if o == TT_ - 1 or d == 0 else TT_ - 2 - o
            return i + o if d == 0 else (TT_ - 2 - o) - i

        def cols_of(t, d, lo, n):
            x = place_of(t, d)
            return slice(x * P + lo, x * P + lo + n) if isinstance(x, int) else bass.ds(x * P + lo, n)

        def at_of(x):
            return slice(x, x + 1) if isinstance(x, int) else bass.ds(x, 1)

        def bh(ap):
            return ap.unsqueeze(1).broadcast_to([P, H, ap.shape[-1]])

        def bc(ap, n=P):
            return ap.unsqueeze(2).broadcast_to([P, H, n])

        def heads(k):
            return ps[:, k, :].rearrange("p (h n) -> p h n", h=H)

        def small(k):
            first = ps[:, k, 0:1]
            return bass.AP(first.tensor, first.offset, [first.ap[0], [P + Q, H], [1, Q]])

        def blocks(ap):
            return ap.rearrange("p h (b n) -> p h b n", n=Q)

        def spread(ap):
            return ap.unsqueeze(2).broadcast_to([P, H, P // Q, Q])

        def mask4(m):
            return mat(m).rearrange("p (b n) -> p b n", n=Q).unsqueeze(1).broadcast_to([P, H, P // Q, Q])

        def rows(k, d):
            c = k if d == 0 else 1 - k
            return c, slice(CH * c, CH * c + CH)

        GG, NG, GE, BG, BT, KE, CD0, CD1 = range(0, 32, 4)

        def delta_pool(pool):
            gp = nc.gpsimd

            def stage(name, d, t, after):
                b = dl[d]
                if name == "sc":
                    after("dve", "vb", d, 1)
                    after("act", "ke", d, 1)
                    plain(pool)
                    return gp.tensor_copy(b["sc"][:].unsqueeze(1), SC[:, at_of(place_of(t, d)), d, :])
                if name == "CD":
                    after("dve", "SU1", d, 1)
                    plain(pool)
                    return gp.tensor_copy(b["cd"][:].unsqueeze(1), SC[:, at_of(place_of(t, d)), d, CD0:CD0 + 8])
                if name == "qd":
                    after("act", "eg", d)
                    after("act", "cp", d)
                    after("pe", "O1", d, 1)
                    return gp.tensor_tensor(b["QD"][:], b["QE"][:], b["qkv"][:, 0:H, :], ALU.mult)
                after("act", "at", d)
                return gp.tensor_tensor(b["AT"][:], b["AT"][:], bh(mat(("OU", "OL")[d])), ALU.mult)
            pool.wait_ge(s["sc_tab"], 1)
            for d in range(2):
                pool.dma_start(dl[d]["Sa"][:], s0[:, d, :, :]).then_inc(s[f"s0_in{d}"], 16)
            for d in range(2):
                pool.wait_ge(s[f"s0_in{d}"], 16)
            delta_run(pool, "pool", stage)

        def delta_act(act):
            A = nc.scalar.activation
            act.wait_ge(s["qkv_done"], N_QKV)
            act.wait_ge(s["gate_out"], 16 * N_GATE)
            act.wait_ge(side_free[(N_Z - 1) % 2], (N_Z - 1) // 2 + 1)

            def stage(name, d, t, after):
                b = dl[d]
                sc = b["sc"]
                P0, P1 = 4 * d, 4 * d + 1
                if name == "cp":
                    after("pe", "trv", d, 1)
                    after("pool", "qd", d, 1)
                    plain(act)
                    return A(b["qkv"][:], QKV[:, :, cols_of(t, d, 0, P)], ACT.Copy)
                if name == "eg":
                    after("pe", "gb", d)
                    after("pe", "wT", d, 1)
                    return A(b["QE"][:], heads(P0), ACT.Exp)
                if name in ("e1", "e2"):
                    r, scale, f = (b["R1"], -1.0, GE) if name == "e1" else (b["R2"], 1.0, NG)
                    after("dve", "g1" if name == "e1" else "g2", d)
                    for h in range(H):
                        last = A(r[:, h, :], r[:, h, :], ACT.Exp, scale=scale, bias=sc[:, f + h:f + h + 1])
                    return last
                if name == "nc":
                    after("dve", "a", d)
                    after("pe", "y3", d, 1)
                    for q in range(0, P, Q):
                        last = A(b["X"][q:q + Q], b["A"][q:q + Q, :, q:q + Q], ACT.Copy)
                    return last
                if name == "at":
                    after("dve", "at32", d)
                    after("pe", "x4", d, 1)
                    return A(b["AT"][:], heads(P1), ACT.Copy, scale=-1.0)
                if name == "kbg":
                    after("pe", "trk", d)
                    after("pool", "qd", d)
                    for h in range(H):
                        last = A(b["kbg"][:, h, :], ps[:, P0, h * P:h * P + P], ACT.Copy, scale=sc[:, BG + h:BG + h + 1])
                    return last
                if name == "ke":
                    after("pe", "DS1", d, 1)
                    for h in range(H):
                        last = A(b["ke"][:, h, :], ps[:, P0, h * P:h * P + P], ACT.Copy, scale=sc[:, KE + h:KE + h + 1])
                    return last
                if name[:2] == "xc":
                    after("pe", "x" + name[2:], d)
                    return A(b["X"][:], small(P1), ACT.Copy, scale=-1.0)
                if name == "uc":
                    after("pe", "u", d)
                    after("dve", "VN1", d, 1)
                    return A(b["U"][:], heads(P0), ACT.Copy)
                after("pe", "wT", d)
                after("pe", "WS1", d, 1)
                return A(b["W"][:], heads(P1), ACT.Copy)
            delta_run(act, "act", stage)

        def delta_dve(dve):
            V = nc.vector
            dve.wait_ge(s["prd_in"], 16)

            def stage(name, d, t, after):
                b = dl[d]
                sc = b["sc"]
                P0, P1, S0, S1 = range(4 * d, 4 * d + 4)
                if name == "g1":
                    after("act", "eg", d)
                    after("pe", "u", d, 1)
                    return V.tensor_tensor(b["R1"][:], heads(P0), bh(mat(f"E{d}")), ALU.add)
                if name == "g2":
                    after("dve", "pt", d, 1)
                    return V.tensor_tensor(b["R2"][:], heads(P0), bh(mat(f"I{d}")), ALU.add)
                if name == "a":
                    after("pe", "kk", d)
                    after("act", "e1", d)
                    after("pe", "yt", d, 1)
                    return V.tensor_tensor(b["A"][:], heads(P1), b["R1"][:], ALU.mult)
                if name == "pt":
                    after("pe", "qkT", d)
                    after("act", "e2", d)
                    after("pe", "O1", d, 1)
                    return V.tensor_tensor(b["PT"][:], heads(P0), b["R2"][:], ALU.mult)
                if name == "at32":
                    after("pe", "trA", d)
                    after("pe", "x3", d, 1)
                    return V.tensor_tensor(b["AT32"][:], heads(P1), bh(mat("D32")), ALU.mult)
                if name == "t0":
                    after("act", "nc", d)
                    after("pe", "x4", d, 1)
                    after("dve", "tr3", d, 1)
                    k = C_SUB + Q * (1 + d)
                    return V.tensor_tensor(b["T"][:], b["X"][:], bh(cst[:, k:k + Q]), ALU.mult)
                if name == "t1":
                    after("dve", "t0", d)
                    return V.tensor_tensor(b["T"][:], b["T"][:], bh(cst[:, C_SUB:C_SUB + Q]), ALU.add)
                if name[:2] == "tr":
                    if name == "tr":
                        after("dve", "t1", d)
                        after("dve", "ex3", d, 1)
                    else:
                        after("dve", "cp" + name[2:], d)
                        after("dve", "ex" + ("" if name == "tr0" else str(int(name[2]) - 1)), d)
                    return V.transpose(b["Tt"][:].rearrange("p h n -> p (h n)"), b["T"][:].rearrange("p h n -> p (h n)"))
                if name[:2] == "ex":
                    after("dve", "tr" + name[2:], d)
                    if name == "ex":
                        after("pe", "u", d, 1)
                        after("pe", "wT", d, 1)
                    else:
                        after("pe", "y" + name[2:], d)
                    return V.tensor_tensor(blocks(b["TT"][:]), spread(b["Tt"][:]), mask4("D32"), ALU.mult)
                if name[:2] == "cp":
                    l = int(name[2])
                    after("pe", f"y{l}", d)
                    after("dve", "tr" if l == 0 else f"tr{l - 1}", d)
                    plain(dve)
                    return V.copy_predicated(b["T"][:], bh(prd[:, 2 * l + d, :]), small(P1))
                if name == "vb":
                    after("pe", "trv", d)
                    after("dve", "a", d)
                    return V.tensor_tensor(b["vb"][:], heads(P0), bc(sc[:, BT:BT + 4]), ALU.mult)
                if name == "xf":
                    after("pe", "x4", d)
                    after("pe", "trA", d)
                    return V.tensor_tensor(blocks(b["Xf"][:]), spread(small(P1)), mask4(("OL", "OU")[d]), ALU.mult)
                if name == "ca":
                    after("pe", "yt", d)
                    after("dve", "ex3", d)
                    return V.tensor_tensor(b["TT"][:], b["TT"][:], heads(P1), ALU.add)
                if name == "OA":
                    after("pe", "O1", d)
                    after("dve", "OA", 1 - d, 1 - d)
                    plain(dve)
                    oc = cols_of(t, d, 0, P)
                    return V.tensor_tensor(oT[:, :, oc], oT[:, :, oc], heads(S0), ALU.add)
                k = int(name[2])
                c, r = rows(k, d)
                cur, new = (b["Sa"], b["Sb"]) if k == 0 else (b["Sb"], b["Sa"])
                if name[:2] == "VN":
                    after("pe", f"WS{k}", d)
                    after("act", "uc", d)
                    if k == 0:
                        after("pe", "O1", d, 1)
                    return V.tensor_tensor(b["vnew"][r], b["U"][r], heads(S1)[r], ALU.subtract)
                if name[:2] == "SU":
                    after("pe", f"DS{k}", d)
                    if k:
                        after("dve", "SU0", d)
                    else:
                        after("dve", "SU1", d, 1)
                        if is_context(t):
                            dve.wait_ge(s["oz"], 3)
                    after("pe", f"O{1 - k}", d, 1 - k)
                    after("pool", "CD", d)
                    for h in range(H):
                        last = V.scalar_tensor_tensor(new[:, h, :], cur[:, h, :], b["cd"][:, 4 * c + h:4 * c + h + 1],
                                                      ps[:, S1, h * P:h * P + P], ALU.mult, ALU.add)
                    return last

            def between():
                for d in range(2):
                    dve.wait_ge(SEM["dve", True], (TT_ - 1) * N_STEP["dve", True])
                    dve.wait_ge(SEM["pe", True], (TT_ - 1) * N_STEP["pe", True])
                V.memset(dl[0]["Sa"][:], 0.0)
                V.memset(dl[1]["Sa"][:], 0.0).then_inc(s["oz"], 1)
            delta_run(dve, "dve", stage, between)

        def delta_pe(pe):
            M = nc.tensor.matmul

            def stage(name, d, t, after):
                b = dl[d]
                P0, P1, S0, S1 = range(4 * d, 4 * d + 4)

                def four(k, left, right, rows=slice(0, P)):
                    for h in range(H):
                        last = M(ps[:, k, h * P:h * P + P], left[rows, h, :],
                                 right[rows, h, :], start=True, stop=True)
                    return last

                def four_small(k, left, right):
                    for h in range(H):
                        last = M(ps[:, k, h * P:h * P + P], left[:, h, :], right.rearrange("p h n -> p (h n)"),
                                 start=True, stop=True)
                    return last

                def turn(k, x, h0=0):
                    for h in range(H):
                        last = nc.tensor.transpose(ps[:, k, h * P:h * P + P], x[:, h0 + h, :], mat("ident"))
                    return last
                q, k_ = b["qkv"][:, 0:H, :], b["qkv"][:, H:2 * H, :]
                if name == "gb":
                    after("pool", "sc", d)
                    after("act", "uc", d, 1)
                    for h in range(H):
                        last = nc.tensor.transpose(ps[:, P0, h * P:h * P + P],
                                                   b["sc"][:, GG + h:GG + h + 1].broadcast_to([P, P]), mat("ident"))
                    return last
                if name == "kk":
                    after("act", "cp", d)
                    after("act", "wc", d, 1)
                    return four(P1, k_, k_)
                if name == "qkT":
                    after("dve", "g2", d)
                    return four(P0, k_, q)
                if name == "trA":
                    after("dve", "a", d)
                    return turn(P1, b["A"])
                if name == "trk":
                    after("dve", "pt", d)
                    return turn(P0, b["qkv"], H)
                if name == "trv":
                    after("act", "ke", d)
                    return turn(P0, b["qkv"], 2 * H)
                if name == "x4":
                    after("dve", "cp3", d)
                    after("pool", "off", d)
                    return four_small(P1, b["AT"], b["T"])
                if name[0] == "x":
                    after("dve", "t1" if name == "x0" else f"cp{int(name[1]) - 1}", d)
                    if name == "x0":
                        after("act", "at", d)
                    return four_small(P1, b["AT32"], b["T"])
                if name == "yt":
                    after("dve", "xf", d)
                    after("dve", "ex3", d)
                    return four(P1, b["Xf"], b["TT"])
                if name[0] == "y":
                    l = int(name[1])
                    after("act", f"xc{l}", d)
                    after("dve", "ex" if l == 0 else f"ex{l - 1}", d)
                    return four_small(P1, b["TT"], b["X"])
                if name == "u":
                    after("dve", "ca", d)
                    after("dve", "vb", d)
                    return four(P0, b["TT"], b["vb"])
                if name == "wT":
                    after("act", "kbg", d)
                    return four(P1, b["kbg"], b["TT"])
                k = int(name[-1])
                c, r = rows(k, d)
                cur = b["Sa"] if k == 0 else b["Sb"]
                if name[:2] == "WS":
                    after("act", "wc", d)
                    if k == 0:
                        after("dve", "SU1", d, 1)
                        if is_context(t):
                            pe.wait_ge(s["oz"], 3)
                    else:
                        after("dve", "SU0", d)
                    return four(S1, b["W"], cur)
                if name[:2] == "DS":
                    after("dve", f"VN{k}", d)
                    after("act", "ke", d)
                    return four(S1, b["ke"], b["vnew"], rows=r)
                if k == 0:
                    after("pool", "qd", d)
                    after("dve", "OA", d, 1)
                else:
                    after("dve", "pt", d)
                for h in range(H):
                    last = M(ps[:, S0, h * P + c * CH:h * P + c * CH + CH], cur[:, h, :],
                             b["QD"][:, h, c * CH:c * CH + CH], start=(k == 0 and h == 0), stop=False)
                for h in range(H if k else 0):
                    last = M(ps[:, S0, h * P:h * P + P], b["vnew"][:, h, :], b["PT"][:, h, :],
                             start=False, stop=(h == H - 1))
                return last
            delta_run(pe, "pe", stage)

        @block.gpsimd
        def _(pool):
            pool.dma_start(X[:, 4:8, :], xT[:, 4:8, :]).then_inc(s["x_in1"], 16)
            pool.dma_start(prd[:], preds).then_inc(s["prd_in"], 16)

            def low(u, u4):
                pool.wait_ge(s["wh_ready"], u + 1)
                nc.gpsimd.tensor_tensor(wL[:, u4 % 2, :], raw[:, u4 % RAW, :],
                                        wH[:, u4 % 2, :].bitcast(F32), ALU.subtract).then_inc(s["wl_ready"], 1)

            low(0, 0)
            low(1, 1)
            units(pool, 2, U_CONV + 2, lambda u, u4, i: low(u, u4))
            for j in range(4):
                for k in range(3):
                    w = U_CONV + 3 * j + k
                    low(w + 2, w + 2)
                pool.wait_ge(s["yc_high"], j + 1)
                nc.gpsimd.tensor_tensor(ycL[:], ccb[:], ycH[:].bitcast(F32), ALU.subtract).then_inc(s["yc_low"], 1)
                pool.dma_start(yc_d[:, j, :], ycH[:]).then_inc(s["yc_out0"], 16)
                pool.wait_ge(s["yc_low"], j + 1)
                pool.dma_start(yc_d[:, 4 + j, :], ycL[:]).then_inc(s["yc_out1"], 16)
            for g in range(N_GATE):
                w = U_GATE + g
                low(w + 2, w + 2)
                pool.wait_ge(side_free[w % 2], w // 2 + 1)
                pool.dma_start(g_d[:, g, :], acc[:]).then_inc(s["gate_out"], 16)

            pool.wait_ge(s["gate_out"], 16 * N_GATE)
            delta_pool(pool)
            for (e, scan), sem in SEM.items():
                pool.wait_ge(sem, TT_ * N_STEP[e, scan])
            for j in range(2):
                pool.dma_start(hH[:, 2 * j:2 * j + 2, :], yc_d[:, 2 * j:2 * j + 2, :]).then_inc(s[f"yH_in{j}"], 16)
                pool.dma_start(hL[:, 2 * j:2 * j + 2, :], yc_d[:, 4 + 2 * j:6 + 2 * j, :]).then_inc(s[f"yL_in{j}"], 16)
            for h in range(H):
                pool.wait_ge(s["mixH"], h + 1)
                nc.gpsimd.tensor_tensor(hL[:, 4 + h, :], oT[:, h, :], hH[:, 4 + h, :].bitcast(F32),
                                        ALU.subtract).then_inc(s["mixL"], 1)
            units(pool, U_OUT + 2, U_FFN + 2, lambda u, u4, i: low(u, u4))

            def p_low(f, slot, cnt):
                pool.wait_ge(s["pH_ready"], cnt)
                nc.gpsimd.tensor_tensor(pL[:, slot, :], fa[:, f % 2, :], pH[:, slot, :].bitcast(F32),
                                        ALU.subtract).then_inc(s["pL_ready"], 1)

            low(U_FFN + 2, U_FFN + 2)
            with pool.Fori(0, GROUPS) as g:
                u0 = U_FFN + 1
                for f in range(4):
                    low(g * 12 + (u0 + 2 * f + 2), u0 + 2 * f + 2)
                    low(g * 12 + (u0 + 2 * f + 3), u0 + 2 * f + 3)
                    p_low(f, f, g * 4 + (f + 1))
                for j in range(4):
                    low(g * 12 + (u0 + 8 + j + 2), u0 + 8 + j + 2)
            for u in range(U_TAIL + 2, N_SPLIT - 1):
                low(u, u)
            p_low(0, 0, 4 * GROUPS + 1)
            low(N_SPLIT - 1, N_SPLIT - 1)
            p_low(1, 1, 4 * GROUPS + 2)

        @block.scalar
        def _(act):
            A = nc.scalar.activation
            act.wait_ge(s["cst_in"], 16)
            act.wait_ge(s["bias_set"], 1)
            for k, col in enumerate((C_C, C_CC)):
                last = A(scT[:, :, k], cst[:, col:col + KT], ACT.Tanh, scale=0.5)
            last.then_inc(s["act_step"], 1)

            def ada_rows(m):
                act.wait_ge(s["ada_used"], 8 * m + 8)
                if m >= 2:
                    act.wait_ge(s["modps_ready"], m - 1)
                for j in range(2):
                    last = A(modrow[:, m % 2, 512 * j:512 * j + 512], ps[0:2, 4 + 2 * (m % 2) + j, :], ACT.Copy)
                last.then_inc(s["modrow_ready"], 1)

            astep = Tally(s["act_step"])
            astep.n = 1

            def square(k, b, sqb, total):
                if k == 0:
                    act.wait_ge(s["x_in"] if b < 4 else s["x_in1"], 16)
                else:
                    xb = (U_OUT, B_TAIL + 3)[k - 1] + b
                    act.wait_ge(side_free[xb % 2], xb // 2 + 1)
                if b >= 3:
                    act.wait_ge(s["sq_used"], 7 * k + b - 2)
                A(sqb[:, b % 2, :] if b else total[:], X[:, b, :], ACT.Square).then_inc(s["sq_ready"], 1)

            def norm_rstd(k, rs, side):
                act.wait_ge(s["st_done"], k + 1)
                for n in range(NT):
                    last = A(rs[:, n * TW:n * TW + TW], bank3(side, n), ACT.Ln, scale=1.0 / D, bias=biases[:, 0:1])
                astep.inc(last)
                act.wait_ge(s["act_step"], astep.value())
                A(rs[:], rs[:], ACT.Exp, scale=-0.5).then_inc(s["rstd_ready"], 1)

            def norm_high(k, ubuf, shift):
                act.wait_ge(s["mod_ready"], 2)
                for b in range(KT):
                    act.wait_ge(s["u_ready"], 8 * k + b + 1)
                    A(hH[:, b, 0:LAT], ubuf[:, b % 2, 0:LAT], ACT.Identity, bias=mod[:, shift * 8 + b, 0:1])
                    A(hH[:, b, LAT:T], ubuf[:, b % 2, LAT:T], ACT.Identity,
                      bias=mod[:, shift * 8 + b, 1:2]).then_inc(s["hH_ready"], 1)

            for b in range(KT):
                square(0, b, sq, ss)
            ada_rows(0)
            ada_rows(1)
            norm_rstd(0, rstd, 0)
            norm_high(0, ub, 0)
            for m in range(2, 6):
                ada_rows(m)

            def high(u, u4, i, done=None):
                act.wait_ge(raw_in[u4 % RAW], landed(u4 + N_ADA, i))
                A(wH[:, u4 % 2, :], raw[:, u4 % RAW, :], ACT.Copy).then_inc(s["wh_ready"], 1)

            high(0, 0, 0)
            high(1, 1, 0)

            def evac_rows(side, dst_s, dst_c, row):
                per = TW // GRID
                for n in range(NT):
                    rows = min(per, ROWS - n * per)
                    A(dst_s[:, row + n * per:row + n * per + rows, 1:GRID + 1],
                      bank3(side, n)[:, 0:rows * GRID].rearrange("p (r c) -> p r c", c=GRID), ACT.Copy)
                return A(dst_c[:, 1:CTX + 1], bank3(side, NT - 1)[:, LAT - (NT - 1) * TW:TW], ACT.Copy)

            zs = zp[:, 0:ZS].rearrange("p (r c) -> p r c", c=GRID + 2)
            zc = zp[:, ZS:ZS + ZC]

            act.wait_ge(s["z_init"], 1)

            def qkv_block(b, b4, i):
                act.wait_ge(s["blk_done"], b + 1)
                high(b + 2, b4 + 2, i)
                if b4:
                    act.wait_ge(s["conv_done"], b)
                evac_rows(b4 % 2, zs, zc, 0).then_inc(side_free[b4 % 2], 1)
                act.wait_ge(s["conv_done"], b + 1)
                if b4:
                    act.wait_ge(s["qkv_done"], b)
                A(tb[:], acc[:], ACT.Tanh).then_inc(s["tanh_done"], 1)

            for b in range(4):
                qkv_block(b, b, 0)
            with act.Fori(1, 3) as i:
                for u in range(4):
                    qkv_block(i * 4 + u, 4 + u, i - 1)

            def norm_qk(n):
                act.wait_ge(s["qkv_done"], N_QKV)
                if n:
                    act.wait_ge(s["qm_done"], n)
                A(qn[:], QKV[:, n, :], ACT.Square).then_inc(s["qs_ready"], 1)
                for j in range(NT):
                    act.wait_ge(s["qs_done"], NT * n + (j + 1 if j < 1 else NT))
                    A(qn[:, j * TW:j * TW + TW], ps[:, 6 + (NT * n + j) % 2, 0:TW], ACT.Ln,
                      bias=biases[:, 0:1]).then_inc(s["qs_read"], 1)
                act.wait_ge(s["qs_read"], NT * n + NT)
                A(qn[:], qn[:], ACT.Exp, scale=-0.5, bias=(biases[:, 1:2] if n < H else 0.0)).then_inc(s["qr_ready"], 1)

            b = N_QKV
            act.wait_ge(s["blk_done"], b + 1)
            high(b + 2, b + 2, 0)
            for n in range(NT):
                last = A(abT[:, n * TW:n * TW + TW], bank3(b % 2, n)[0:16], ACT.Copy)
            last.then_inc(side_free[b % 2], 1)
            for j in range(4):
                for k in range(3):
                    b = U_CONV + 3 * j + k
                    act.wait_ge(s["blk_done"], b + 1)
                    high(b + 2, b + 2, 0)
                    if k == 0:
                        if j:
                            act.wait_ge(s["yc_out1"], 16 * j)
                        for n in range(NT):
                            last = A(ccb[:, n * TW:n * TW + TW], bank3(b % 2, n), ACT.Copy)
                        last.then_inc(side_free[b % 2], 1)
                    if k == 2:
                        act.wait_ge(side_free[b % 2], b // 2 + 1)
                        act.wait_ge(s["qkv_done"], N_QKV)
                        if j:
                            act.wait_ge(s["yc_out0"], 16 * j)
                        A(ycH[:], ccb[:], ACT.Copy).then_inc(s["yc_high"], 1)
                    if 0 <= b - B_NORM < 2 * H:
                        norm_qk(b - B_NORM)
            for g in range(N_GATE):
                b = U_GATE + g
                act.wait_ge(s["blk_done"], b + 1)
                high(b + 2, b + 2, 0)
                if g == 0:
                    act.wait_ge(s["yc_out0"], 16 * 4)
                    act.wait_ge(s["yc_low"], 4)
                if g:
                    act.wait_ge(side_free[(b - 1) % 2], (b - 1) // 2 + 1)
                for n in range(NT):
                    last = A(tb[:, n * TW:n * TW + TW], bank3(b % 2, n), ACT.Tanh, scale=0.5)
                last.then_inc(s["tanh_done"], 1)

            act.wait_ge(s["abt_ready"], 1)
            act.wait_ge(s["tanh_done"], N_QKV + N_GATE)
            act.wait_ge(side_free[(N_Z - 1) % 2], (N_Z - 1) // 2 + 1)
            ab = ps[:, 6, 0:TT_ * 16].rearrange("p (t c) -> p t c", c=16)
            A(gA[:], ab[:, :, 0:8], ACT.Exp, scale=-1.0).then_inc(s["g_act"], 1)
            act.wait_ge(s["g_dve"], 2)
            A(gL[:], gA[:], ACT.Ln)
            A(gC[:], gC[:], ACT.Exp, scale=-1.0).then_inc(s["g_act"], 1)
            act.wait_ge(s["g_act"], 2)
            A(gC[:], gC[:], ACT.Ln, bias=biases[:, 2:3])
            A(cst[:, C_ALOG:C_ALOG + 8], cst[:, C_ALOG:C_ALOG + 8], ACT.Exp).then_inc(s["g_act"], 1)
            act.wait_ge(s["g_pe"], 1)

            def gp(k):
                return ps[:, 7, 72 * k:72 * k + 72].rearrange("p (t d h) -> p t d h", d=2, h=H)

            def field(f):
                return SC[:, :, :, f:f + 4]

            v4 = lambda t: t[:].rearrange("p t (d h) -> p t d h", d=2)
            act.wait_ge(s["g_dve"], 5)
            A(field(GG), gp(0), ACT.Copy)
            A(field(NG), gp(0), ACT.Copy, scale=-1.0)
            A(v4(gB), gp(0), ACT.Exp)
            A(field(KE), gp(1), ACT.Exp)
            A(field(CD0), gp(2), ACT.Exp)
            A(field(CD1), gp(3), ACT.Exp).then_inc(s["g_act"], 1)

            delta_act(act)

            act.wait_ge(SEM["dve", True], TT_ * N_STEP["dve", True])
            for h in range(H):
                A(osq[:, h, :], oT[:, h, :], ACT.Square).then_inc(s["o_sq"], 1)
            for h in range(H):
                act.wait_ge(s["o_st"], h + 1)
                for n in range(NT):
                    last = A(ors[:, h, n * TW:n * TW + TW], bank3(h % 2, n), ACT.Ln, scale=1.0 / P,
                             bias=biases[:, 0:1])
                last.then_inc(s["o_ln"], 1)
            for h in range(H):
                act.wait_ge(s["o_ln"], h + 1)
                A(ors[:, h, :], ors[:, h, :], ACT.Exp, scale=-0.5).then_inc(s["o_rs"], 1)
            for h in range(H):
                act.wait_ge(s["o_m"], h + 1)
                A(hH[:, 4 + h, :], oT[:, h, :], ACT.Copy).then_inc(s["mixH"], 1)

            for b in range(U_OUT, U_FFN):
                act.wait_ge(s["blk_done"], b + 1)
                high(b + 2, b + 2, 0)
                square(1, b - U_OUT, sq2, ss2)
            norm_rstd(1, rstd2, 1)
            norm_high(1, ub2, 3)

            gs = G[:, 0:GS].rearrange("p (r c) -> p r c", c=GRID + 2)
            gc = G[:, GS:GS + ZC]
            act.wait_ge(s["ffn_init"], 1)

            def gt_block(f, side):
                if not isinstance(f, int) or f:
                    act.wait_ge(s["fc_done"], f)
                evac_rows(side, gs, gc, 1).then_inc(side_free[side], 1)

            def gelu(f, f4):
                act.wait_ge(s["fc_done"], f + 1)
                A(fa[:, f4 % 2, :], fa[:, f4 % 2, :], ACT.Gelu_apprx_tanh).then_inc(s["gelu_done"], 1)

            def p_high(f, f4, slot, side, nfree):
                act.wait_ge(side_free[side], nfree)
                A(pH[:, slot, :], fa[:, f4 % 2, :], ACT.Copy).then_inc(s["pH_ready"], 1)

            act.wait_ge(s["blk_done"], B_FFN + 1)
            high(U_FFN + 2, U_FFN + 2, 0)
            gt_block(0, B_FFN % 2)
            with act.Fori(0, GROUPS) as g:
                ub0, b0 = U_FFN + 1, B_FFN + 1
                for f in range(4):
                    act.wait_ge(s["blk_done"], g * 16 + (b0 + 2 * f + 1))
                    high(g * 12 + (ub0 + 2 * f + 2), ub0 + 2 * f + 2, g * 3)
                    gelu(g * 4 + f, f)
                    gt_block(g * 4 + (f + 1), (b0 + 2 * f) % 2)
                    act.wait_ge(s["blk_done"], g * 16 + (b0 + 2 * f + 2))
                    high(g * 12 + (ub0 + 2 * f + 3), ub0 + 2 * f + 3, g * 3)
                    p_high(g * 4 + f, f, f, (b0 + 2 * f + 1) % 2, g * 8 + ((b0 + 2 * f + 1) // 2 + 1))
                for j in range(4):
                    act.wait_ge(s["blk_done"], g * 16 + (b0 + 8 + 2 * j + 2))
                    high(g * 12 + (ub0 + 8 + j + 2), ub0 + 8 + j + 2, g * 3)
            f0 = 4 * GROUPS
            act.wait_ge(s["blk_done"], B_TAIL + 1)
            high(U_TAIL + 2, U_TAIL + 2, 0)
            gelu(f0, f0)
            gt_block(f0 + 1, B_TAIL % 2)
            act.wait_ge(s["blk_done"], B_TAIL + 2)
            high(U_TAIL + 3, U_TAIL + 3, 0)
            p_high(f0, f0, 0, (B_TAIL + 1) % 2, (B_TAIL + 1) // 2 + 1)
            gelu(f0 + 1, f0 + 1)
            act.wait_ge(s["blk_done"], B_TAIL + 3)
            high(U_TAIL + 4, U_TAIL + 4, 0)
            p_high(f0 + 1, f0 + 1, 1, (B_TAIL + 2) % 2, (B_TAIL + 2) // 2 + 1)
            for b in range(KT):
                square(2, b, sq3, ss3)
            norm_rstd(2, rstd3, 1)

        @block.vector
        def _(dve):
            V = nc.vector
            V.memset(biases[:, 0:1], EPS)
            V.memset(biases[:, 1:2], -0.5 * float(np.log(P)))
            V.memset(biases[:, 2:3], 1.0).then_inc(s["bias_set"], 1)
            dve.wait_ge(s["cst_in"], 16)
            V.tensor_scalar(wqk[:], cst[:, C_QK:C_QK + 36], 0.5, None, ALU.mult)
            V.tensor_scalar(onw[:], cst[:, C_ON:C_ON + 1], 0.5, None, ALU.mult).then_inc(s["oz"], 1)
            dve.wait_ge(s["act_step"], 1)
            dve.wait_ge(s["oz"], 1)
            for k, col in enumerate((C_C, C_CC)):
                last = V.scalar_tensor_tensor(scT[:, :, k], scT[:, :, k], 1.0, cst[:, col:col + KT], ALU.add, ALU.mult)
            last.then_inc(s["sc_ready"], 1)
            dve.wait_ge(s["sc_ready"], 1)
            V.tensor_scalar(scT[:], scT[:], 0.5, None, ALU.mult).then_inc(s["sc_ready"], 1)

            def add_bias(lo, hi, n):
                dve.wait_ge(s["modps_ready"], hi)
                V.tensor_tensor(mod[:, 8 * lo:8 * hi, :],
                                ps[:, 3, 16 * lo:16 * hi].rearrange("p (b k) -> p b k", k=2),
                                cst[:, C_BADA + 8 * lo:C_BADA + 8 * hi].unsqueeze(2).broadcast_to([P, 8 * (hi - lo), 2]),
                                ALU.add).then_inc(s["mod_ready"], 1)
                dve.wait_ge(s["mod_ready"], n)

            def scale_of(dst, row, col):
                V.scalar_tensor_tensor(dst[:], mod[:, 8 * row:8 * row + 8, :], 1.0,
                                       cst[:, col:col + 8].unsqueeze(2).broadcast_to([P, 8, 2]),
                                       ALU.add, ALU.mult).then_inc(s["mod_ready"], 1)

            def norm_apply(k, scl, ubuf, rs, shift):
                dve.wait_ge(s["rstd_ready"], k + 1)

                def u_of(b):
                    if b >= 2:
                        dve.wait_ge(s["hL_ready"], 8 * k + b - 1)
                    for which, (lo, hi) in enumerate(((0, LAT), (LAT, T))):
                        last = V.scalar_tensor_tensor(ubuf[:, b % 2, lo:hi], X[:, b, lo:hi], scl[:, b, which:which + 1],
                                                      rs[:, lo:hi], ALU.mult, ALU.mult)
                    last.then_inc(s["u_ready"], 1)
                u_of(0)
                for b in range(KT):
                    if b + 1 < KT:
                        u_of(b + 1)
                    dve.wait_ge(s["hH_ready"], 8 * k + b + 1)
                    dve.wait_ge(s["u_ready"], 8 * k + b + 1)
                    for which, (lo, hi) in enumerate(((0, LAT), (LAT, T))):
                        last = V.scalar_tensor_tensor(hL[:, b, lo:hi], ubuf[:, b % 2, lo:hi],
                                                      mod[:, shift * 8 + b, which:which + 1],
                                                      hH[:, b, lo:hi].bitcast(F32), ALU.add, ALU.subtract)
                    last.then_inc(s["hL_ready"], 1)

            def add_square(k, b, sqb, total):
                dve.wait_ge(s["sq_ready"], 8 * k + b + 1)
                if b > 1:
                    dve.wait_ge(s["sq_used"], 7 * k + b - 1)
                V.tensor_tensor(total[:], total[:], sqb[:, b % 2, :], ALU.add).then_inc(s["sq_used"], 1)

            for b in range(1, KT):
                add_square(0, b, sq, ss)
            add_bias(0, 2, 1)
            scale_of(sc1, 1, C_N1)
            dve.wait_ge(s["mod_ready"], 2)
            norm_apply(0, sc1, ub, rstd, 0)
            add_bias(2, 6, 3)
            scale_of(sc2, 4, C_N2)
            dve.wait_ge(s["hL_ready"], 8)
            V.memset(zp[:], 0.0).then_inc(s["z_init"], 1)

            zs = zp[:, 0:ZS].rearrange("p (r c) -> p r c", c=GRID + 2)
            zc = zp[:, ZS:ZS + ZC]
            step = Tally(s["dve_step"])
            acs = acc[:, 0:LAT].rearrange("p (r c) -> p r c", c=GRID)
            def conv3(chain, w, done):
                for tap, first in ((1, True), (0, False), (2, False)):
                    for dst, src in ((acs, zs[:, :, tap:tap + GRID]), (acc[:, LAT:T], zc[:, tap:tap + CTX])):
                        if first:
                            last = V.tensor_scalar(dst, src, w(tap), None, ALU.mult)
                        else:
                            last = V.scalar_tensor_tensor(dst, src, w(tap), dst, ALU.mult, ALU.add)
                    if tap != 2:
                        chain.inc(last)
                        dve.wait_ge(chain.sem, chain.value())
                last.then_inc(done, 1)

            def qkv_block(b, b4, chain):
                dve.wait_ge(side_free[b4 % 2], b4 // 2 + 1 if isinstance(b, int) else chain.i * 2 + b4 // 2 + 1)
                if b4:
                    dve.wait_ge(s["qkv_done"], b)
                col = (lambda t: wqk[:, t * 12 + b:t * 12 + b + 1]) if isinstance(b, int) else \
                    (lambda t: wqk[:, bass.ds(b + t * 12, 1)])
                conv3(chain, col, s["conv_done"])
                dve.wait_ge(s["tanh_done"], b + 1)
                dst = QKV[:, b, :] if isinstance(b, int) else QKV[:, bass.ds(b, 1), :]
                src = (lambda t: t[:]) if isinstance(b, int) else (lambda t: t[:].unsqueeze(1))
                V.scalar_tensor_tensor(dst, src(tb), 1.0, src(acc), ALU.add, ALU.mult).then_inc(s["qkv_done"], 1)

            chain = Tally(s["conv_step"])
            for b in range(4):
                qkv_block(b, b, chain)
            with dve.Fori(1, 3) as i:
                chain.enter(i - 1, 8)
                for u in range(4):
                    qkv_block(i * 4 + u, 4 + u, chain)
                chain.leave(2)
            def norm_qk(b):
                n = b - B_NORM - 1
                if 0 <= n < 2 * H:
                    dve.wait_ge(s["qr_ready"], n + 1)
                    V.tensor_tensor(QKV[:, n, :], QKV[:, n, :], qn[:], ALU.mult).then_inc(s["qm_done"], 1)

            for j in range(4):
                b = U_CONV + 3 * j
                dve.wait_ge(s["qkv_done"], N_QKV)
                norm_qk(b)
                dve.wait_ge(side_free[b % 2], b // 2 + 1)
                b += 1
                dve.wait_ge(s["blk_done"], b + 1)
                dve.wait_ge(s["conv_done"], N_QKV + j)
                per = TW // GRID
                for n in range(NT):
                    rows = min(per, ROWS - n * per)
                    V.tensor_tensor(zs[:, n * per:n * per + rows, 1:GRID + 1],
                                    bank3(b % 2, n)[:, 0:rows * GRID].rearrange("p (r c) -> p r c", c=GRID),
                                    ccb[:, n * TW:n * TW + rows * GRID].rearrange("p (r c) -> p r c", c=GRID), ALU.mult)
                V.tensor_tensor(zc[:, 1:CTX + 1], bank3(b % 2, NT - 1)[:, TW - CTX:TW], ccb[:, LAT:T],
                                ALU.mult).then_inc(side_free[b % 2], 1)
                dve.wait_ge(side_free[b % 2], b // 2 + 1)
                dve.wait_ge(s["qkv_done"], N_QKV)
                if j:
                    dve.wait_ge(side_free[(b - 2) % 2], (b - 2) // 2 + 1)
                norm_qk(b)
                conv3(chain, lambda t: cst[:, C_CA + 4 * t + j:C_CA + 4 * t + j + 1], s["conv_done"])
                b += 1
                dve.wait_ge(s["blk_done"], b + 1)
                dve.wait_ge(s["conv_done"], N_QKV + j + 1)
                for n in range(NT):
                    last = V.tensor_tensor(ccb[:, n * TW:n * TW + TW], bank3(b % 2, n), acc[:, n * TW:n * TW + TW],
                                           ALU.mult)
                last.then_inc(side_free[b % 2], 1)
                norm_qk(b)
            for g in range(N_GATE):
                b = U_GATE + g
                dve.wait_ge(s["tanh_done"], N_QKV + g + 1)
                if g:
                    dve.wait_ge(s["gate_out"], 16 * g)
                else:
                    dve.wait_ge(side_free[(b - 1) % 2], (b - 1) // 2 + 1)
                for n in range(NT):
                    last = V.scalar_tensor_tensor(acc[:, n * TW:n * TW + TW], tb[:, n * TW:n * TW + TW], 1.0,
                                                  bank3(b % 2, n), ALU.add, ALU.mult)
                last.then_inc(side_free[b % 2], 1)

            ab = ps[:, 6, 0:TT_ * 16].rearrange("p (t c) -> p t c", c=16)
            dve.wait_ge(s["g_act"], 1)
            b8 = lambda col: cst[:, col:col + 8].unsqueeze(1).broadcast_to([P, TT_, 8])
            V.tensor_tensor(gB[:], ab[:, :, 8:16], b8(C_DTB), ALU.add).then_inc(s["g_dve"], 1)
            dve.wait_ge(s["g_dve"], 1)
            V.scalar_tensor_tensor(gC[:], gB[:], -1.0, gB[:], ALU.mult, ALU.max)
            V.tensor_scalar(gA[:], gA[:], 1.0, None, ALU.add).then_inc(s["g_dve"], 1)
            dve.wait_ge(s["g_dve"], 2)
            dve.wait_ge(s["g_act"], 3)
            V.reciprocal(gA[:], gA[:])
            V.scalar_tensor_tensor(la[:], gB[:], 0.0, gC[:], ALU.max, ALU.add).then_inc(s["g_dve"], 1)
            dve.wait_ge(s["g_dve"], 3)
            V.scalar_tensor_tensor(la[:], la[:], -1.0, b8(C_ALOG), ALU.mult, ALU.mult).then_inc(s["g_dve"], 1)
            dve.wait_ge(s["g_dve"], 4)
            v4 = lambda t: t[:].rearrange("p t (d h) -> p t d h", d=2)

            def field(f):
                return SC[:, :, :, f:f + 4]
            V.tensor_copy(field(BT), v4(gA)).then_inc(s["g_dve"], 1)
            dve.wait_ge(s["g_act"], 4)
            V.tensor_tensor(field(BG), v4(gA), v4(gB), ALU.mult)
            V.tensor_tensor(field(GE), field(GG), v4(gL), ALU.subtract).then_inc(s["sc_tab"], 1)
            dve.wait_ge(s["gate_out"], 16 * N_GATE)
            V.memset(oT[:], 0.0).then_inc(s["oz"], 1)
            dve.wait_ge(s["oz"], 2)
            delta_dve(dve)
            dve.wait_ge(SEM["dve", True], TT_ * N_STEP["dve", True])

            dve.wait_ge(s["gt_in"], 16)
            for h in range(H):
                dve.wait_ge(s["o_rs"], h + 1)
                step.inc(V.tensor_tensor(oT[:, h, :], oT[:, h, :], ors[:, h, :], ALU.mult))
                dve.wait_ge(s["dve_step"], step.value())
                V.scalar_tensor_tensor(oT[:, h, :], oT[:, h, :], onw[:, 0:1], og[:, h, :], ALU.mult,
                                       ALU.mult).then_inc(s["o_m"], 1)

            def residual(b, side, ob, gate):
                xs = (lambda lo, hi: X[:, ob, lo:hi])
                for n in range(NT):
                    lo, hi = n * TW, min((n + 1) * TW, LAT)
                    last = V.scalar_tensor_tensor(xs(lo, hi), bank3(side, n)[:, 0:hi - lo], mod[:, gate * 8 + ob, 0:1],
                                                  xs(lo, hi), ALU.mult, ALU.add)
                last = V.scalar_tensor_tensor(xs(LAT, T), bank3(side, NT - 1)[:, TW - CTX:TW],
                                              mod[:, gate * 8 + ob, 1:2], xs(LAT, T), ALU.mult, ALU.add)
                last.then_inc(side_free[side], 1)

            dve.wait_ge(s["x2_in"], 16)
            for ob in range(KT):
                b = U_OUT + ob
                dve.wait_ge(s["blk_done"], b + 1)
                residual(b, b % 2, ob, 2)
                if ob > 1:
                    add_square(1, ob - 1, sq2, ss2)
            add_square(1, KT - 1, sq2, ss2)
            dve.wait_ge(side_free[(U_FFN - 1) % 2], (U_FFN - 1) // 2 + 1)
            norm_apply(1, sc2, ub2, rstd2, 3)
            dve.wait_ge(s["hL_ready"], 16)
            V.memset(G[:], 0.0).then_inc(s["ffn_init"], 1)

            gs = G[:, 0:GS].rearrange("p (r c) -> p r c", c=GRID + 2)
            gc = G[:, GS:GS + ZC]
            fch = Tally(s["dve_step"])
            fch.n = step.n

            def conv9(f, f4, side, nfree):
                dve.wait_ge(side_free[side], nfree)
                dst = fa[:, f4 % 2, 0:LAT].rearrange("p (r c) -> p r c", c=GRID)
                dctx = fa[:, f4 % 2, LAT:T]
                w = (lambda t: cst[:, C_FFN + FB * t + f:C_FFN + FB * t + f + 1]) if isinstance(f, int) else \
                    (lambda t: cst[:, bass.ds(f + (C_FFN + FB * t), 1)])
                first = True
                for dy in range(3):
                    for dx in range(3):
                        src = gs[:, dy:dy + ROWS, dx:dx + GRID]
                        if first:
                            V.tensor_scalar(dst, src, w(3 * dy + dx), None, ALU.mult) if dy != 1 else None
                            last = V.tensor_scalar(dctx, gc[:, 0:CTX], w(3), None, ALU.mult)
                            first = False
                        else:
                            last = V.scalar_tensor_tensor(dst, src, w(3 * dy + dx), dst, ALU.mult, ALU.add)
                            if dy == 1 and dx:
                                last = V.scalar_tensor_tensor(dctx, gc[:, dx:dx + CTX], w(3 + dx), dctx,
                                                              ALU.mult, ALU.add)
                        if (dy, dx) == (2, 2):
                            last.then_inc(s["fc_done"], 1)
                        else:
                            fch.inc(last)
                            dve.wait_ge(s["dve_step"], fch.value())

            def product(f, f4, side, ndone):
                dve.wait_ge(s["gelu_done"], f + 1)
                dve.wait_ge(s["blk_done"], ndone)
                for n in range(NT):
                    last = V.tensor_tensor(fa[:, f4 % 2, n * TW:n * TW + TW], fa[:, f4 % 2, n * TW:n * TW + TW],
                                           bank3(side, n), ALU.mult)
                last.then_inc(side_free[side], 1)

            conv9(0, 0, B_FFN % 2, B_FFN // 2 + 1)

            def group(g, dyn):
                b0 = B_FFN + 1
                for f in range(4):
                    fi = g * 4 + f
                    bg = b0 + 2 * f
                    if dyn or f:
                        dve.wait_ge(s["pL_ready"], g * 4 + f)
                    conv9(g * 4 + (f + 1), f + 1, bg % 2, g * 8 + (bg // 2 + 1))
                    product(fi, f, (bg + 1) % 2, g * 16 + (bg + 2))
                for ob in range(KT):
                    b = b0 + 8 + ob
                    dve.wait_ge(s["blk_done"], g * 16 + (b + 1))
                    residual(b, b % 2, ob, 5)
            group(0, False)
            with dve.Fori(1, GROUPS) as g:
                fch.enter(g - 1, 32)
                group(g, True)
                fch.leave(GROUPS - 1)
            f0 = 4 * GROUPS
            dve.wait_ge(s["pL_ready"], f0)
            conv9(f0 + 1, f0 + 1, B_TAIL % 2, B_TAIL // 2 + 1)
            product(f0, f0, (B_TAIL + 1) % 2, B_TAIL + 2)
            product(f0 + 1, f0 + 1, (B_TAIL + 2) % 2, B_TAIL + 3)
            for ob in range(KT):
                b = B_TAIL + 3 + ob
                dve.wait_ge(s["blk_done"], b + 1)
                residual(b, b % 2, ob, 5)
                if ob > 1:
                    add_square(2, ob - 1, sq3, ss3)
            add_square(2, KT - 1, sq3, ss3)
            dve.wait_ge(side_free[(B_TAIL + 10) % 2], (B_TAIL + 10) // 2 + 1)
            dve.wait_ge(s["rstd_ready"], 3)
            for b in range(KT):
                if b >= 2:
                    dve.wait_ge(s[f"y_out{b % 2}"], 16 * (b // 2))
                V.scalar_tensor_tensor(yb[:, b % 2, :], X[:, b, :], cst[:, C_NF + b:C_NF + b + 1], rstd3[:],
                                       ALU.mult, ALU.mult).then_inc(s["y_ready"], 1)

        @block.tensor
        def _(pe):
            M = nc.tensor.matmul

            def ada(m):
                for kt in range(KT):
                    u = 8 * m + kt
                    pe.wait_ge(raw_in[u % RAW], (u // RAW + 1) * 16)
                    for j in range(2):
                        last = M(ps[0:2, 4 + 2 * (m % 2) + j, :], scT[:, kt, :], raw[:, u % RAW, 512 * j:512 * j + 512],
                                 start=(kt == 0), stop=(kt == KT - 1))
                    last.then_inc(s["ada_used"], 1)

            def turn(m):
                pe.wait_ge(s["modrow_ready"], m + 1)
                for b in range(KT):
                    last = M(ps[:, 3, 16 * m + 2 * b:16 * m + 2 * b + 2], modrow[:, m % 2, P * b:P * b + P],
                             mat("ident")[0:2, 0:2], start=True, stop=True)
                last.then_inc(s["modps_ready"], 1)

            def stats(k, total, side):
                pe.wait_ge(s["sq_used"], 7 * k + 7)
                for n in range(NT):
                    last = M(bank3(side, n), mat("ones"), total[:, n * TW:n * TW + TW], start=True, stop=True)
                last.then_inc(s["st_done"], 1)

            pe.wait_ge(s["sc_ready"], 2)
            ada(0)
            ada(1)
            turn(0)
            turn(1)
            stats(0, ss, 0)
            for m in range(2, 6):
                ada(m)
                if m >= 3:
                    turn(m - 1)
            turn(5)
            pe.wait_ge(s["mod_ready"], 3)

            def product_step(side, k, kts, left, right):
                rh, rl = right(k)
                for w, lo in ((wH, False), (wL, True)):
                    lhs = left(w, k)
                    for n in range(NT):
                        c = slice(n * TW, n * TW + TW)
                        last = M(bank3(side, n), lhs, rh[:, c], start=(k == 0 and not lo),
                                 stop=(lo and k == kts - 1))
                        if not lo:
                            M(bank3(side, n), lhs, rl[:, c], start=False, stop=False)
                return last

            def product_block(side, kts, left, right, ready):
                for k in range(kts):
                    ready(k)
                    last = product_step(side, k, kts, left, right)
                last.then_inc(s["blk_done"], 1)

            def h_of(k):
                return hH[:, k, :], hL[:, k, :]

            def w_of(u4):
                return lambda w, k: w[:, u4 % 2, k * P:k * P + P]

            def model_block(u, u4, free, ready):
                pe.wait_ge(s["wl_ready"], u + 1)
                if free[1] is not None:
                    pe.wait_ge(side_free[free[0]], free[1])
                product_block(free[0], KT, w_of(u4), h_of, ready)

            def model_pair(u, b, ready):
                for k in range(KT):
                    ready(k)
                    for o in range(2):
                        if k == 0:
                            pe.wait_ge(s["wl_ready"], u + o + 1)
                            if b + o >= 2:
                                pe.wait_ge(side_free[(b + o) % 2], (b + o) // 2)
                        last = product_step((b + o) % 2, k, KT, w_of(u + o), h_of)
                        if k == KT - 1:
                            last.then_inc(s["blk_done"], 1)

            no_wait = lambda k: None
            h1_ready = lambda k: pe.wait_ge(s["hL_ready"], k + 1)
            model_pair(0, 0, h1_ready)
            for u in (2, 3):
                model_block(u, u, (u % 2, u // 2), no_wait)
            units(pe, 4, B_NORM, lambda u, u4, i: model_block(u, u4, (u4 % 2, i * 2 + u4 // 2), no_wait))
            model_block(B_NORM, B_NORM, (B_NORM % 2, B_NORM // 2), no_wait)

            def norm_qk(k, n, base):
                if k not in (4, 5, 6):
                    return
                j = k - 4
                m = NT * n + j
                if j == 0:
                    pe.wait_ge(s["qs_ready"], base + (n + 1))
                if n or j == 2 or not isinstance(base, int):
                    pe.wait_ge(s["qs_read"], base * NT + (m - 1))
                M(ps[:, 6 + m % 2, 0:TW], mat("ones"), qn[:, j * TW:j * TW + TW], start=True,
                  stop=True).then_inc(s["qs_done"], 1)

            for half in range(2):
                for v in range(4):
                    n = 4 * half + v
                    u = B_NORM + 1 + n
                    model_block(u, u, (u % 2, u // 2), lambda k, n=n: norm_qk(k, n, 0))
            units(pe, B_NORM + 1 + 2 * H, N_Z, lambda u, u4, i: model_block(u, u4, (u4 % 2, i * 2 + u4 // 2), no_wait))
            pe.wait_ge(side_free[N_QKV % 2], N_QKV // 2 + 1)
            for t in range(TT_):
                last = M(ps[:, 6, 16 * t:16 * t + 16], abT[:, t * P:t * P + P], mat("ident")[0:16, 0:16],
                         start=True, stop=True)
            last.then_inc(s["abt_ready"], 1)
            pe.wait_ge(s["g_dve"], 4)
            for d in range(2):
                for k, m in enumerate((("UI", "LS"), ("LI", "US"))[d]):
                    M(ps[:, 7, 72 * k:72 * k + 72].rearrange("p (t c) -> p t c", c=8)[:, :, 4 * d:4 * d + 4],
                      mat(m), la[:, :, 4 * d:4 * d + 4], start=True, stop=True)
            for k in range(2):
                last = M(ps[:, 7, 144 + 72 * k:216 + 72 * k], mat(f"CB{k}"), la[:].rearrange("p t c -> p (t c)"),
                         start=True, stop=True)
            last.then_inc(s["g_pe"], 1)

            delta_pe(pe)

            for h in range(H):
                pe.wait_ge(s["o_sq"], h + 1)
                if h >= 2:
                    pe.wait_ge(s["o_ln"], h - 1)
                for n in range(NT):
                    last = M(bank3(h % 2, n), mat("ones"), osq[:, h, n * TW:n * TW + TW], start=True, stop=True)
                last.then_inc(s["o_st"], 1)
            pe.wait_ge(s["o_ln"], H)

            def mix_ready(k):
                if k < 4:
                    pe.wait_ge(s[f"yH_in{k // 2}"], 16)
                    pe.wait_ge(s[f"yL_in{k // 2}"], 16)
                else:
                    pe.wait_ge(s["mixL"], k - 3)
            model_pair(U_OUT, U_OUT, mix_ready)
            for u in range(U_OUT + 2, U_FFN):
                model_block(u, u, (u % 2, u // 2), no_wait)
            pe.wait_ge(side_free[1], (B_FFN - 2) // 2 + 1)
            stats(1, ss2, 1)
            pe.wait_ge(s["rstd_ready"], 2)
            model_pair(U_FFN, B_FFN, lambda k: pe.wait_ge(s["hL_ready"], 9 + k))

            def p_of(k):
                return pH[:, k, :], pL[:, k, :]

            def down(u, u4, b, bdyn, fis, width, p0, first):
                left = lambda o: lambda w, k: w[:, u4 % 2, (k * width + o) * P:(k * width + o) * P + P]
                pe.wait_ge(s["wl_ready"], u + 1)
                if first:
                    pe.wait_ge(s["pL_ready"], p0 + (fis - 1))
                    for o in range(2):
                        pe.wait_ge(side_free[(b + o) % 2], bdyn + (b + o) // 2)
                        for k in range(fis - 1):
                            product_step((b + o) % 2, k, fis, left(o), p_of)
                    pe.wait_ge(s["pL_ready"], p0 + fis)
                    for o in range(2):
                        product_step((b + o) % 2, fis - 1, fis, left(o), p_of).then_inc(s["blk_done"], 1)
                for o in range(2 if first else 0, width):
                    pe.wait_ge(side_free[(b + o) % 2], bdyn + (b + o) // 2)
                    product_block((b + o) % 2, fis, left(o), p_of, no_wait)

            with pe.Fori(0, GROUPS) as g:
                for k in range(1, 8):
                    u, b = U_FFN + 1 + k, B_FFN + 1 + k
                    model_block(g * 12 + u, u, (b % 2, g * 8 + b // 2), no_wait)
                for j in range(4):
                    u, b = U_FFN + 9 + j, B_FFN + 9 + 2 * j
                    down(g * 12 + u, u, b, g * 8, 4, 2, g * 4, j == 0)
                u, b = U_FFN + 13, B_FFN + 17
                model_block(g * 12 + u, u, (b % 2, g * 8 + b // 2), no_wait)
            for k in range(1, 3):
                model_block(U_TAIL + k, U_TAIL + k, ((B_TAIL + k) % 2, (B_TAIL + k) // 2), no_wait)
            for j in range(2):
                down(U_TAIL + 3 + j, U_TAIL + 3 + j, B_TAIL + 3 + 4 * j, 0, 2, 4, 4 * GROUPS, j == 0)
            pe.wait_ge(side_free[1], (B_TAIL + 9) // 2 + 1)
            stats(2, ss3, 1)


def kernel(x_prompt, x_sample, state_deltanet, c, c_ctx, w_ada, b_ada, norm1_w, w_in, conv_a_w, qkv_conv_w,
           a_log, dt_bias, o_norm_w, w_out, norm2_w, w_up, ffn_conv_w, w_down, final_norm_w):
    import concourse.bacc as bacc
    from concourse.bass_utils import run_bass_kernel_spmd

    f = lambda a: np.asarray(a, dtype=np.float32)
    cols = lambda a: f(a).reshape(-1, P).T
    mats, preds, ind = constants()
    rep = lambda a: np.broadcast_to(f(a).reshape(1, -1), (P, 2 * H))
    const = np.ascontiguousarray(np.concatenate([
        cols(b_ada), cols(norm1_w), cols(norm2_w), cols(final_norm_w), cols(conv_a_w), cols(qkv_conv_w),
        cols(o_norm_w), cols(c), cols(c_ctx), cols(ffn_conv_w), rep(dt_bias), rep(a_log), ind, mats], 1))
    assert const.shape[1] == N_CONST
    tok = np.concatenate([f(x_sample)[0], f(x_prompt)[0]], 0)
    xT = np.ascontiguousarray(tok.T.reshape(KT, P, T).transpose(1, 0, 2))
    s0 = np.ascontiguousarray(f(state_deltanet)[0, 0].transpose(2, 0, 1, 3))

    def unit(w):
        k, n = w.shape
        return w.reshape(k // P, P, n).transpose(1, 0, 2).reshape(P, -1)

    wa, wi, wo, wu, wd = (f(a)[0] for a in (w_ada, w_in, w_out, w_up, w_down))
    cw = D // 2
    us = [wa[k * P:k * P + P, m * D:m * D + D] for m in range(6) for k in range(KT)]
    blk = lambda lo: unit(wi[:, lo:lo + P])
    q0 = 3 * cw
    us += [blk(q0 + b * P) for b in range(N_QKV)]
    g0 = q0 + 3 * H * P
    ab0 = g0 + H * P
    us.append(unit(np.concatenate([wi[:, ab0:ab0 + 4 * H], wi[:, ab0 - P + 4 * H:ab0]], 1)))
    for j in range(4):
        us += [blk(cw + j * P), blk(2 * cw + j * P), blk(j * P)]
    us += [blk(g0 + b * P) for b in range(N_GATE)]
    us += [unit(wo[:, b * P:b * P + P]) for b in range(KT)]
    gt = lambda b: unit(wu[:, DFF + b * P:DFF + b * P + P])
    up = lambda b: unit(wu[:, b * P:b * P + P])
    us.append(gt(0))
    for g in range(GROUPS):
        for b in range(4 * g, 4 * g + 4):
            us += [gt(b + 1), up(b)]
        us += [unit(wd[4 * g * P:4 * (g + 1) * P, j * 256:j * 256 + 256]) for j in range(4)]
    b = 4 * GROUPS
    us += [gt(b + 1), up(b), up(b + 1)]
    us += [unit(wd[b * P:(b + 2) * P, j * 512:j * 512 + 512]) for j in range(2)]
    assert len(us) == N_UNITS
    wts = np.stack(us)

    nc = bacc.Bacc("TRN2", target_bir_lowering=False, num_devices=1)
    ins = {"const": const, "preds": preds.reshape(P, -1, Q), "xT": xT, "s0": s0, "wts": wts}
    dts = {"preds": I32}
    args = [nc.dram_tensor(k, v.shape, dts.get(k, F32), kind="ExternalInput").ap() for k, v in ins.items()]
    y = nc.dram_tensor("y", (P, KT, T), F32, kind="ExternalOutput").ap()
    st = nc.dram_tensor("st", (P, 2, H, P), F32, kind="ExternalOutput").ap()
    yc = nc.dram_tensor("yc", (P, 8, T), F32R, kind="Internal").ap()
    gd = nc.dram_tensor("gd", (P, 4, T), F32, kind="Internal").ap()
    build(nc, *args, y, st, yc, gd)
    r = run_bass_kernel_spmd(nc, [ins], core_ids=[0]).results[0]
    yt = r["y"].transpose(1, 0, 2).reshape(D, T).T
    return (np.ascontiguousarray(yt[LAT:])[None], np.ascontiguousarray(yt[:LAT])[None],
            np.ascontiguousarray(r["st"].transpose(1, 2, 0, 3))[None, None])
```

```python
import numpy as np

import concourse.bass as bass
from concourse import mybir
from concourse.alu_op_type import AluOpType as ALU

F32 = mybir.dt.float32
F32R = mybir.dt.float32r
I32 = mybir.dt.int32
ACT = mybir.ActivationFunctionType

P = 128
D = 1024
KT = D // P
LAT, CTX = 1024, 128
T = LAT + CTX
TW = 384
NT = T // TW
GRID = 64
ROWS = LAT // GRID
H = 4
TT_ = T // P
CH = 64
DFF = 2816
FB = DFF // P
EPS = 1e-6

C_BADA, C_N1, C_N2, C_NF, C_CA, C_QK, C_ON, C_C, C_CC, C_FFN = 0, 48, 56, 64, 72, 84, 120, 121, 129, 137
C_DTB = C_FFN + 9 * FB
C_ALOG = C_DTB + 2 * H
C_IND = C_ALOG + 2 * H
C_MAT = C_IND + 2
MATS = ["ident", "ones", "UI", "LI", "US", "LS", "CB0", "CB1", "E0", "E1", "I0", "I1", "D32", "OU", "OL", "SW"]
C_SUB = C_MAT + len(MATS) * P
Q = 32
N_CONST = C_SUB + 3 * Q
LEVELS = (2, 4, 8, 16)
BIG = 1e30

N_ADA = 48
N_QKV, N_AB, N_CONV, N_GATE = 12, 1, 12, 4
N_Z = N_QKV + N_AB + N_CONV + N_GATE
N_OUT = 8
GROUPS = 5
RAW = 4
U_CONV = N_QKV + N_AB
U_GATE = U_CONV + N_CONV
U_OUT = N_Z
U_FFN = U_OUT + N_OUT
U_TAIL = U_FFN + 1 + 12 * GROUPS
N_SPLIT = U_TAIL + 5
B_FFN = U_FFN
B_TAIL = B_FFN + 1 + 16 * GROUPS
B_NORM = 16
N_UNITS = N_ADA + N_SPLIT


def constants():
    p, f = np.meshgrid(np.arange(P), np.arange(P), indexing="ij")
    same = (p // CH) == (f // CH)
    m = {"ident": p == f, "ones": p >= 0, "UI": same & (p <= f), "LI": same & (p >= f),
         "US": same & (p < f), "LS": same & (p > f), "CB0": p < CH, "CB1": p >= CH}
    m["E0"], m["E1"] = (np.where(m[k], 0.0, BIG) for k in ("LS", "US"))
    m["I0"], m["I1"] = (np.where(m[k], 0.0, -BIG) for k in ("UI", "LI"))
    m["D32"] = p // Q == f // Q
    m["SW"] = f == (p + CH) % P
    m["OU"], m["OL"] = m["US"] & ~m["D32"], m["LS"] & ~m["D32"]

    def level(s):
        return ((p // s) % 2 == 1) & (f // s == p // s - 1)

    def compact(x):
        return np.concatenate([x[q:q + Q, q:q + Q] for q in range(0, P, Q)], 0)
    sub = [compact(p == f), -1.0 * compact(level(1)), -1.0 * compact(level(1).T)]
    mats = np.concatenate([m[k].astype(np.float32) for k in MATS] + [x.astype(np.float32) for x in sub], 1)
    preds = np.concatenate([compact(x).astype(np.int32) for s in LEVELS for x in (level(s), level(s).T)], 1)
    ind = np.stack([np.arange(P) < CH, np.arange(P) >= CH], 1).astype(np.float32)
    return mats, preds, ind


class Tally:

    def __init__(self, sem):
        self.sem, self.n, self.i, self.per, self.n0 = sem, 0, None, 0, 0

    def inc(self, ins):
        ins.then_inc(self.sem, 1)
        self.n += 1
        return self.n

    def value(self, n=None):
        n = self.n if n is None else n
        return n if self.i is None else self.i * self.per + n

    def enter(self, i, per):
        self.i, self.per, self.n0 = i, per, self.n

    def leave(self, count):
        assert self.n - self.n0 == self.per, (self.n - self.n0, self.per)
        self.n = self.n0 + count * self.per
        self.i = None


def build(nc, const, preds, xT, s0, wts, y_out, s_out, yc_d, g_d):
    BLK = T * 4
    at = [16512]

    def place(name, shape, dt, off=None):
        n = 4
        for s in shape[1:]:
            n *= s
        if off is None:
            off = at[0]
            at[0] += (n + 31) // 32 * 32
        return nc.alloc_sbuf_tensor_at(name, shape, dt, offset=off)

    cst = place("cst", [P, N_CONST], F32)
    prd = place("prd", [P, 2 * len(LEVELS), Q], I32)
    mod = place("mod", [P, 48, 2], F32)
    sc1 = place("sc1", [P, KT, 2], F32)
    sc2 = place("sc2", [P, KT, 2], F32)
    scT = place("scT", [P, KT, 2], F32)
    wqk = place("wqk", [P, 36], F32)
    onw = place("onw", [P, 1], F32)
    biases = place("biases", [P, 3], F32)
    dots = place("dots", [P, 160], F32)
    raw = place("raw", [P, RAW, D], F32)
    wH = place("wH", [P, 2, D], F32R)
    wL = place("wL", [P, 2, D], F32R)
    R0 = at[0]

    def blk(n):
        return R0 + n * BLK

    assert blk(35) < 229344
    hH = place("hH", [P, KT, T], F32R, blk(0))
    hL = place("hL", [P, KT, T], F32R, blk(8))
    X = place("X", [P, KT, T], F32, blk(16))
    QKV = place("QKV", [P, 12, T], F32, blk(16))
    sq = place("sq", [P, 2, T], F32, blk(28))
    rstd = place("rstd", [P, T], F32, blk(30))
    ub = place("ub", [P, 2, T], F32, blk(31))
    ss = place("ss", [P, T], F32, blk(15))
    ZS, ZC = ROWS * (GRID + 2), CTX + 2
    zp = place("zp", [P, ZS + ZC], F32, blk(28))
    acc = place("acc", [P, T], F32, blk(30))
    ccb = place("ccb", [P, T], F32, blk(31))
    tb = place("tb", [P, T], F32, blk(32))
    abT = place("abT", [2 * 2 * H, T], F32, blk(33))
    modrow = place("modrow", [2, 2, D], F32, blk(33))
    ycH = place("ycH", [P, T], F32R, blk(32))
    ycL = place("ycL", [P, T], F32R, blk(31))
    qn = place("qn", [P, T], F32, blk(34))
    oT = place("oT", [P, H, T], F32, blk(28))
    off = [blk(35)]

    def tail_place(name, shape, dt=F32):
        n = 4
        for s in shape[1:]:
            n *= s
        o = off[0]
        off[0] += n
        assert off[0] <= blk(35) or o >= blk(35) and off[0] <= 229344, name
        return place(name, shape, dt, o)

    SC = tail_place("SC", [P, TT_, 2, 32])
    la = tail_place("la", [P, TT_, 8])
    gA = tail_place("gA", [P, TT_, 8])
    gB = tail_place("gB", [P, TT_, 8])
    gC = tail_place("gC", [P, TT_, 8])
    gL = tail_place("gL", [P, TT_, 8])
    off[0] = blk(32)
    dl = []
    doff = [blk(0), blk(16)]

    def dplace(name, shape):
        n = 4
        for s in shape[1:]:
            n *= s
        o = doff[0]
        doff[0] += n
        assert doff[0] <= doff[1], name
        return place(name, shape, F32, o)

    for d in range(2):
        b = {}
        b["qkv"] = dplace(f"dqkv{d}", [P, 12, P])
        for nm in ("R1", "R2", "A", "AT", "AT32", "TT", "kbg", "ke", "PT", "U", "QS", "vnew"):
            b[nm] = dplace(f"{nm}{d}", [P, H, P])
        b["WQ"] = dplace(f"WQ{d}", [P, H, 2, P])
        for nm in ("Sa", "Sb"):
            b[nm] = tail_place(f"{nm}{d}", [P, H, P])
        b["QE"], b["Xf"], b["vb"] = b["kbg"], b["A"], b["R1"]
        for nm in ("T", "Tt", "X"):
            b[nm] = dplace(f"{nm}{d}", [P, H, Q])
        b["sc"] = dplace(f"sc_{d}", [P, 32])
        b["cd"] = dplace(f"cd{d}", [P, 8])
        dl.append(b)
    osq = place("osq", [P, H, T], F32, blk(4))
    ors = place("ors", [P, H, T], F32, blk(12))
    og = place("og", [P, H, T], F32, blk(24))
    pH = place("pH", [P, 4, T], F32R, blk(24))
    pL = place("pL", [P, 4, T], F32R, blk(28))
    GS = (ROWS + 2) * (GRID + 2)
    G = place("G", [P, GS + ZC], F32, blk(32))
    fa = place("fa", [P, 2, T], F32, blk(32) + ((GS + ZC) * 4 + 31) // 32 * 32)
    sq2 = place("sq2", [P, 2, T], F32, blk(24))
    rstd2 = place("rstd2", [P, T], F32, blk(26))
    ub2 = place("ub2", [P, 2, T], F32, blk(27))
    ss2 = place("ss2", [P, T], F32, blk(29))
    ss3 = place("ss3", [P, T], F32, blk(5))
    sq3 = place("sq3", [P, 2, T], F32, blk(0))
    rstd3 = place("rstd3", [P, T], F32, blk(2))

    ps = nc.alloc_psum_tensor("ps", [P, 8, 512], F32)

    def mat(name):
        k = C_MAT + MATS.index(name) * P
        return cst[:, k:k + P]

    def bank3(side, n):
        return ps[:, 3 * side + n, 0:TW]

    names = ("cst_in mat_in prd_in x_in0 x_in1 x_in2 x_in3 s0_in0 s0_in1 st_out0 st_out1 bias_set z_init ffn_init oz "
             "wh_ready wl_ready ada_used modrow_ready modps_ready mod_ready qs_ready qs_done qs_read qr_ready qm_done sc_ready sq_ready "
             "sq_used sq_last st_done rstd_ready u_ready hH_ready hL_ready blk_done side_free0 side_free1 conv_step "
             "conv_done tanh_done qkv_done yc_out0 yc_out1 yc_high yc_low gate_out gate_last abt_ready g_act g_dve g_pe sc_tab pre_pe pre_act pre_dve "
             "pre_pool scan_pe scan_act scan_dve scan_pool x2_in yH_in0 yH_in1 yL_in0 yL_in1 gt_in o_sq o_st o_ln o_rs o_m mixH mixL fc_done gelu_done "
             "pH_ready pL_ready pL_last y_ready dve_step act_step").split()
    s = {n: nc.alloc_semaphore(n) for n in names}
    raw_in = [nc.alloc_semaphore(f"raw_in{k}") for k in range(RAW)]
    y_sent = [nc.alloc_semaphore(f"y_sent{b}") for b in range(KT)]
    side_free = [s["side_free0"], s["side_free1"]]

    dot = [0]

    def plain(eng):
        dot[0] += 1
        o = dots[0:1, dot[0]:dot[0] + 1]
        if eng is nc.gpsimd:
            nc.gpsimd.tensor_tensor(o, biases[0:1, 0:1], biases[0:1, 0:1], ALU.add)
        else:
            nc.vector.memset(o, 0.0)

    def units(eng, lo, hi, body):
        n = (hi - lo) // 4
        if n > 1:
            with eng.Fori(0, n) as i:
                for u in range(4):
                    body(i * 4 + (lo + u), lo + u, i)
        else:
            n = 0
        for w in range(lo + 4 * n, hi):
            body(w, w, 0)

    def landed(w4, i):
        return (i + (w4 // RAW + 1)) * 16

    ORDER = {
        "pe": ["gb", "WS0", "kk", "DS0", "qkT", "trA", "WS1", "x0", "DS1", "O",
               "y0", "trk", "x1", "y1", "x2", "y2", "x3", "y3", "x4", "trv", "yt", "u", "wT"],
        "act": ["eg", "e1", "OQ0", "e2", "nc", "at", "xc0", "OQ1", "kbg", "xc1", "ke", "xc2", "xc3", "uc", "wc"],
        "dve": ["cp", "g1", "VN0", "g2", "a", "SU0", "at32", "t0", "t1", "VN1", "tr", "ex", "SU1", "OA", "pt",
                "cp0", "tr0", "ex0", "cp1", "tr1", "ex1", "cp2", "tr2", "ex2", "cp3", "tr3", "ex3", "xf", "vb", "ca"],
        "pool": ["CD", "sc", "qd", "off"],
    }
    STEP, N_STEP = {}, {}
    for e, order in ORDER.items():
        for scan in (False, True):
            part = [n for n in order if n.isupper() == scan]
            N_STEP[e, scan] = 2 * len(part)
            STEP.update({(e, n, d): 2 * k + d + 1 for k, n in enumerate(part) for d in range(2)})
    SEM = {(e, scan): s[("scan_" if scan else "pre_") + e] for e in ORDER for scan in (False, True)
           if N_STEP[e, scan]}

    with nc.Block() as block:

        @block.sync
        def _(sp):
            sp.dma_start(cst[:, 0:C_MAT], const[:, 0:C_MAT]).then_inc(s["cst_in"], 16)

            def load(w, w4, i):
                sp.dma_start(raw[:, w4 % RAW, :], wts[w]).then_inc(raw_in[w4 % RAW], 16)

            for w in range(RAW):
                load(w, w, 0)
            sp.dma_start(cst[:, C_MAT:N_CONST], const[:, C_MAT:N_CONST]).then_inc(s["mat_in"], 16)

            def after_ada(w, w4, i):
                sp.wait_ge(s["ada_used"], w - RAW + 1)
                load(w, w4, i)

            def after_split(w, w4, i):
                sp.wait_ge(s["wl_ready"], w - RAW - N_ADA + 1)
                load(w, w4, i)

            units(sp, RAW, 12, after_ada)
            for q in range(4):
                sp.dma_start(X[:, 2 * q:2 * q + 2, :], xT[:, 2 * q:2 * q + 2, :]).then_inc(s[f"x_in{q}"], 16)
                units(sp, 12 + 4 * q, 16 + 4 * q, after_ada)
            units(sp, 28, N_ADA + RAW, after_ada)
            ahead = N_ADA + U_OUT + 2 + RAW
            units(sp, N_ADA + RAW, ahead, after_split)
            for d in range(2):
                sp.wait_ge(SEM["dve", False], (TT_ - 1) * N_STEP["dve", False] + STEP["dve", "cp", d])
            sp.dma_start(og[:], g_d).then_inc(s["gt_in"], 16)
            sp.dma_start(X[:], xT).then_inc(s["x2_in"], 16)
            sp.wait_ge(SEM["dve", True], TT_ * N_STEP["dve", True])
            for d in range(2):
                sp.dma_start(s_out[:, d, :, :], dl[d]["Sa"][:]).then_inc(s[f"st_out{d}"], 16)
            units(sp, ahead, N_UNITS, after_split)
            for b in range(0, KT, 2):
                sp.wait_ge(s["y_ready"], b + 1)
                sp.dma_start(y_out[:, b, :], X[:, b, :]).then_inc(y_sent[b], 16)
            for b in range(KT):
                sp.wait_ge(y_sent[b], 16)
            for d in range(2):
                sp.wait_ge(s[f"st_out{d}"], 16)

        def delta_run(eng, me, stage, ahead_of_scan=None, between=None):
            def run(tile, parts):
                for name in ORDER[me]:
                    scan = name.isupper()
                    if scan not in parts:
                        continue
                    t = tile if scan else (tile[0], tile[1] + 1)
                    for d in range(2):
                        def after(e, of, dd, back=0):
                            if isinstance(t[0], int) and t[1] < back:
                                return
                            n = N_STEP[e, of.isupper()]
                            eng.wait_ge(SEM[e, of.isupper()], t[0] * n + ((t[1] - back) * n + STEP[e, of, dd]))
                        stage(name, d, t, after).then_inc(SEM[me, scan], 1)
            run((0, -1), (False,))
            if ahead_of_scan:
                ahead_of_scan()
            run((0, 0), (False, True))
            with eng.Fori(1, TT_ - 2) as i:
                run((i, 0), (False, True))
            run((0, TT_ - 2), (False, True))
            if between:
                between()
            run((0, TT_ - 1), (True,))

        def is_context(t):
            return isinstance(t[0], int) and t[1] == TT_ - 1

        def place_of(t, d):
            i, o = t
            if isinstance(i, int):
                return o if o == TT_ - 1 or d == 0 else TT_ - 2 - o
            return i + o if d == 0 else (TT_ - 2 - o) - i

        def cols_of(t, d, lo, n):
            x = place_of(t, d)
            return slice(x * P + lo, x * P + lo + n) if isinstance(x, int) else bass.ds(x * P + lo, n)

        def at_of(x):
            return slice(x, x + 1) if isinstance(x, int) else bass.ds(x, 1)

        def bh(ap):
            return ap.unsqueeze(1).broadcast_to([P, H, ap.shape[-1]])

        def bc(ap, n=P):
            return ap.unsqueeze(2).broadcast_to([P, H, n])

        def heads(k):
            return ps[:, k, :].rearrange("p (h n) -> p h n", h=H)

        def small(k):
            first = ps[:, k, 0:1]
            return bass.AP(first.tensor, first.offset, [first.ap[0], [P + Q, H], [1, Q]])

        def blocks(ap):
            return ap.rearrange("p h (b n) -> p h b n", n=Q)

        def spread(ap):
            return ap.unsqueeze(2).broadcast_to([P, H, P // Q, Q])

        def mask4(m):
            return mat(m).rearrange("p (b n) -> p b n", n=Q).unsqueeze(1).broadcast_to([P, H, P // Q, Q])

        def rows(k, d):
            c = k if d == 0 else 1 - k
            return c, slice(CH * c, CH * c + CH)

        GG, NG, GE, BG, BT, KE, CD0, CD1 = range(0, 32, 4)

        def delta_pool(pool):
            gp = nc.gpsimd

            def stage(name, d, t, after):
                b = dl[d]
                if name == "sc":
                    after("dve", "vb", d, 1)
                    after("act", "ke", d, 1)
                    plain(pool)
                    return gp.tensor_copy(b["sc"][:].unsqueeze(1), SC[:, at_of(place_of(t, d)), d, :])
                if name == "CD":
                    after("dve", "SU1", d, 1)
                    plain(pool)
                    return gp.tensor_copy(b["cd"][:].unsqueeze(1), SC[:, at_of(place_of(t, d)), d, CD0:CD0 + 8])
                if name == "qd":
                    after("act", "eg", d)
                    after("dve", "cp", d)
                    after("pe", "WS1", d, 1)
                    for c in range(2):
                        own, other = slice(CH * c, CH * c + CH), slice(CH - CH * c, P - CH * c)
                        last = gp.tensor_tensor(b["WQ"][:, :, c, other], b["QE"][:, :, own], b["qkv"][:, 0:H, own],
                                                ALU.mult)
                    return last
                after("act", "at", d)
                return gp.tensor_tensor(b["AT"][:], b["AT"][:], bh(mat(("OU", "OL")[d])), ALU.mult)
            pool.wait_ge(s["sc_tab"], 1)

            def ahead_of_scan():
                for d in range(2):
                    pool.dma_start(dl[d]["Sa"][:], s0[:, d, :, :]).then_inc(s[f"s0_in{d}"], 16)
            delta_run(pool, "pool", stage, ahead_of_scan)

        def delta_act(act):
            A = nc.scalar.activation
            act.wait_ge(s["qkv_done"], N_QKV)
            act.wait_ge(side_free[(N_Z - 1) % 2], (N_Z - 1) // 2 + 1)

            def stage(name, d, t, after):
                b = dl[d]
                sc = b["sc"]
                P0, P1, S0, S1 = range(4 * d, 4 * d + 4)
                if name == "eg":
                    after("pe", "gb", d)
                    after("pe", "wT", d, 1)
                    return A(b["QE"][:], heads(P0), ACT.Exp)
                if name in ("e1", "e2"):
                    r, scale, f = (b["R1"], -1.0, GE) if name == "e1" else (b["R2"], 1.0, NG)
                    after("dve", "g1" if name == "e1" else "g2", d)
                    for h in range(H):
                        last = A(r[:, h, :], r[:, h, :], ACT.Exp, scale=scale, bias=sc[:, f + h:f + h + 1])
                    return last
                if name == "nc":
                    after("dve", "a", d)
                    after("pe", "y3", d, 1)
                    for q in range(0, P, Q):
                        last = A(b["X"][q:q + Q], b["A"][q:q + Q, :, q:q + Q], ACT.Copy)
                    return last
                if name == "at":
                    after("dve", "at32", d)
                    after("pe", "x4", d, 1)
                    return A(b["AT"][:], heads(P1), ACT.Copy, scale=-1.0)
                if name == "kbg":
                    after("pe", "trk", d)
                    after("pool", "qd", d)
                    for h in range(H):
                        last = A(b["kbg"][:, h, :], ps[:, P0, h * P:h * P + P], ACT.Copy, scale=sc[:, BG + h:BG + h + 1])
                    return last
                if name == "ke":
                    after("pe", "DS1", d, 1)
                    for h in range(H):
                        last = A(b["ke"][:, h, :], ps[:, P0, h * P:h * P + P], ACT.Copy, scale=sc[:, KE + h:KE + h + 1])
                    return last
                if name[:2] == "xc":
                    after("pe", "x" + name[2:], d)
                    return A(b["X"][:], small(P1), ACT.Copy, scale=-1.0)
                if name == "uc":
                    after("pe", "u", d)
                    after("dve", "VN1", d, 1)
                    return A(b["U"][:], heads(P0), ACT.Copy)
                if name[:2] == "OQ":
                    k = int(name[2])
                    after("dve", f"VN{k}", d)
                    if k == 0:
                        after("pe", "O", d, 1)
                    _, other = rows(1 - k, d)
                    return A(b["QS"][other], heads(S1)[other], ACT.Copy)
                after("pe", "wT", d)
                after("pe", "WS1", d, 1)
                for c in range(2):
                    own = slice(CH * c, CH * c + CH)
                    last = A(b["WQ"][:, :, c, own], heads(P1)[:, :, own], ACT.Copy)
                return last
            delta_run(act, "act", stage)

        def delta_dve(dve):
            V = nc.vector
            dve.wait_ge(s["prd_in"], 16)

            def stage(name, d, t, after):
                b = dl[d]
                sc = b["sc"]
                P0, P1, S0, S1 = range(4 * d, 4 * d + 4)
                if name == "cp":
                    after("pe", "trv", d, 1)
                    after("pool", "qd", d, 1)
                    plain(dve)
                    return V.tensor_copy(b["qkv"][:], QKV[:, :, cols_of(t, d, 0, P)])
                if name == "g1":
                    after("act", "eg", d)
                    after("pe", "u", d, 1)
                    return V.tensor_tensor(b["R1"][:], heads(P0), bh(mat(f"E{d}")), ALU.add)
                if name == "g2":
                    after("dve", "pt", d, 1)
                    return V.tensor_tensor(b["R2"][:], heads(P0), bh(mat(f"I{d}")), ALU.add)
                if name == "a":
                    after("pe", "kk", d)
                    after("act", "e1", d)
                    after("pe", "yt", d, 1)
                    return V.tensor_tensor(b["A"][:], heads(P1), b["R1"][:], ALU.mult)
                if name == "pt":
                    after("pe", "qkT", d)
                    after("act", "e2", d)
                    after("pe", "O", d, 1)
                    return V.tensor_tensor(b["PT"][:], heads(P0), b["R2"][:], ALU.mult)
                if name == "at32":
                    after("pe", "trA", d)
                    after("pe", "x3", d, 1)
                    return V.tensor_tensor(b["AT32"][:], heads(P1), bh(mat("D32")), ALU.mult)
                if name == "t0":
                    after("act", "nc", d)
                    after("pe", "x4", d, 1)
                    after("dve", "tr3", d, 1)
                    k = C_SUB + Q * (1 + d)
                    return V.tensor_tensor(b["T"][:], b["X"][:], bh(cst[:, k:k + Q]), ALU.mult)
                if name == "t1":
                    after("dve", "t0", d)
                    return V.tensor_tensor(b["T"][:], b["T"][:], bh(cst[:, C_SUB:C_SUB + Q]), ALU.add)
                if name[:2] == "tr":
                    if name == "tr":
                        after("dve", "t1", d)
                        after("dve", "ex3", d, 1)
                    else:
                        after("dve", "cp" + name[2:], d)
                        after("dve", "ex" + ("" if name == "tr0" else str(int(name[2]) - 1)), d)
                    return V.transpose(b["Tt"][:].rearrange("p h n -> p (h n)"), b["T"][:].rearrange("p h n -> p (h n)"))
                if name[:2] == "ex":
                    after("dve", "tr" + name[2:], d)
                    if name == "ex":
                        after("pe", "u", d, 1)
                        after("pe", "wT", d, 1)
                    else:
                        after("pe", "y" + name[2:], d)
                    return V.tensor_tensor(blocks(b["TT"][:]), spread(b["Tt"][:]), mask4("D32"), ALU.mult)
                if name[:2] == "cp" and name != "cp":
                    l = int(name[2])
                    after("pe", f"y{l}", d)
                    after("dve", "tr" if l == 0 else f"tr{l - 1}", d)
                    plain(dve)
                    return V.copy_predicated(b["T"][:], bh(prd[:, 2 * l + d, :]), small(P1))
                if name == "vb":
                    after("pe", "trv", d)
                    after("dve", "a", d)
                    return V.tensor_tensor(b["vb"][:], heads(P0), bc(sc[:, BT:BT + 4]), ALU.mult)
                if name == "xf":
                    after("pe", "x4", d)
                    after("pe", "trA", d)
                    return V.tensor_tensor(blocks(b["Xf"][:]), spread(small(P1)), mask4(("OL", "OU")[d]), ALU.mult)
                if name == "ca":
                    after("pe", "yt", d)
                    after("dve", "ex3", d)
                    return V.tensor_tensor(b["TT"][:], b["TT"][:], heads(P1), ALU.add)
                if name == "OA":
                    after("pe", "O", d)
                    after("dve", "OA", 1 - d, 1 - d)
                    plain(dve)
                    oc = cols_of(t, d, 0, P)
                    return V.tensor_tensor(oT[:, :, oc], oT[:, :, oc], heads(S1), ALU.add)
                k = int(name[2])
                c, r = rows(k, d)
                cur, new = (b["Sa"], b["Sb"]) if k == 0 else (b["Sb"], b["Sa"])
                if name[:2] == "VN":
                    after("pe", f"WS{k}", d)
                    after("act", "uc", d)
                    if k == 0:
                        after("pe", "O", d, 1)
                    return V.tensor_tensor(b["vnew"][r], b["U"][r], heads(S1)[r], ALU.subtract)
                if name[:2] == "SU":
                    after("pe", f"DS{k}", d)
                    if k:
                        after("dve", "SU0", d)
                    else:
                        after("dve", "SU1", d, 1)
                        if is_context(t):
                            dve.wait_ge(s["oz"], 3)
                    after("pool", "CD", d)
                    for h in range(H):
                        last = V.scalar_tensor_tensor(new[:, h, :], cur[:, h, :], b["cd"][:, 4 * c + h:4 * c + h + 1],
                                                      ps[:, S0, h * P:h * P + P], ALU.mult, ALU.add)
                    return last

            def ahead_of_scan():
                dve.wait_ge(s["gate_out"], 16 * (N_GATE - 1))
                dve.wait_ge(s["gate_last"], 16)
                V.memset(oT[:], 0.0).then_inc(s["oz"], 1)
                dve.wait_ge(s["oz"], 2)

            def between():
                for d in range(2):
                    dve.wait_ge(SEM["dve", True], (TT_ - 1) * N_STEP["dve", True])
                    dve.wait_ge(SEM["pe", True], (TT_ - 1) * N_STEP["pe", True])
                V.memset(dl[0]["Sa"][:], 0.0)
                V.memset(dl[1]["Sa"][:], 0.0).then_inc(s["oz"], 1)
            delta_run(dve, "dve", stage, ahead_of_scan, between)

        def delta_pe(pe):
            M = nc.tensor.matmul

            def stage(name, d, t, after):
                b = dl[d]
                P0, P1, S0, S1 = range(4 * d, 4 * d + 4)

                def four(k, left, right, rows=slice(0, P)):
                    for h in range(H):
                        last = M(ps[:, k, h * P:h * P + P], left[rows, h, :],
                                 right[rows, h, :], start=True, stop=True)
                    return last

                def four_small(k, left, right):
                    for h in range(H):
                        last = M(ps[:, k, h * P:h * P + P], left[:, h, :], right.rearrange("p h n -> p (h n)"),
                                 start=True, stop=True)
                    return last

                def turn(k, x, h0=0):
                    for h in range(H):
                        last = nc.tensor.transpose(ps[:, k, h * P:h * P + P], x[:, h0 + h, :], mat("ident"))
                    return last
                q, k_ = b["qkv"][:, 0:H, :], b["qkv"][:, H:2 * H, :]
                if name == "gb":
                    after("pool", "sc", d)
                    after("act", "uc", d, 1)
                    for h in range(H):
                        last = nc.tensor.transpose(ps[:, P0, h * P:h * P + P],
                                                   b["sc"][:, GG + h:GG + h + 1].broadcast_to([P, P]), mat("ident"))
                    return last
                if name == "kk":
                    after("dve", "cp", d)
                    after("act", "wc", d, 1)
                    return four(P1, k_, k_)
                if name == "qkT":
                    after("dve", "g2", d)
                    return four(P0, k_, q)
                if name == "trA":
                    after("dve", "a", d)
                    return turn(P1, b["A"])
                if name == "trk":
                    after("dve", "pt", d)
                    return turn(P0, b["qkv"], H)
                if name == "trv":
                    after("act", "ke", d)
                    return turn(P0, b["qkv"], 2 * H)
                if name == "x4":
                    after("dve", "cp3", d)
                    after("pool", "off", d)
                    return four_small(P1, b["AT"], b["T"])
                if name[0] == "x":
                    after("dve", "t1" if name == "x0" else f"cp{int(name[1]) - 1}", d)
                    if name == "x0":
                        after("act", "at", d)
                    return four_small(P1, b["AT32"], b["T"])
                if name == "yt":
                    after("dve", "xf", d)
                    after("dve", "ex3", d)
                    return four(P1, b["Xf"], b["TT"])
                if name[0] == "y":
                    l = int(name[1])
                    after("act", f"xc{l}", d)
                    after("dve", "ex" if l == 0 else f"ex{l - 1}", d)
                    return four_small(P1, b["TT"], b["X"])
                if name == "u":
                    after("dve", "ca", d)
                    after("dve", "vb", d)
                    return four(P0, b["TT"], b["vb"])
                if name == "wT":
                    after("act", "kbg", d)
                    return four(P1, b["kbg"], b["TT"])
                if name == "O":
                    after("act", "OQ1", d)
                    after("dve", "pt", d)
                    for h in range(H):
                        out = ps[:, S1, h * P:h * P + P]
                        M(out, b["QS"][:, h, :], mat("SW"), start=True, stop=False)
                        last = M(out, b["vnew"][:, h, :], b["PT"][:, h, :], start=False, stop=True)
                    return last
                k = int(name[-1])
                c, r = rows(k, d)
                cur = b["Sa"] if k == 0 else b["Sb"]
                if name[:2] == "WS":
                    after("act", "wc", d)
                    after("pool", "qd", d)
                    if k == 0:
                        after("dve", "SU1", d, 1)
                        after("dve", "OA", d, 1)
                        if isinstance(t[0], int) and t[1] == 0:
                            pe.wait_ge(s[f"s0_in{d}"], 16)
                        if is_context(t):
                            pe.wait_ge(s["oz"], 3)
                    else:
                        after("dve", "SU0", d)
                        after("act", "OQ0", d)
                    return four(S1, b["WQ"][:, :, c, :], cur)
                after("dve", f"VN{k}", d)
                after("act", "ke", d)
                return four(S0, b["ke"], b["vnew"], rows=r)
            delta_run(pe, "pe", stage)

        @block.gpsimd
        def _(pool):
            pool.dma_start(prd[:], preds).then_inc(s["prd_in"], 16)

            def low(u, u4):
                pool.wait_ge(s["wh_ready"], u + 1)
                nc.gpsimd.tensor_tensor(wL[:, u4 % 2, :], raw[:, u4 % RAW, :],
                                        wH[:, u4 % 2, :].bitcast(F32), ALU.subtract).then_inc(s["wl_ready"], 1)

            low(0, 0)
            low(1, 1)
            units(pool, 2, U_CONV + 2, lambda u, u4, i: low(u, u4))
            for j in range(4):
                for k in range(3):
                    w = U_CONV + 3 * j + k
                    low(w + 2, w + 2)
                pool.wait_ge(s["yc_high"], j + 1)
                nc.gpsimd.tensor_tensor(ycL[:], ccb[:], ycH[:].bitcast(F32), ALU.subtract).then_inc(s["yc_low"], 1)
                pool.dma_start(yc_d[:, j, :], ycH[:]).then_inc(s["yc_out0"], 16)
                pool.wait_ge(s["yc_low"], j + 1)
                pool.dma_start(yc_d[:, 4 + j, :], ycL[:]).then_inc(s["yc_out1"], 16)
            for g in range(N_GATE):
                w = U_GATE + g
                low(w + 2, w + 2)
                if g < N_GATE - 1:
                    pool.wait_ge(side_free[w % 2], w // 2 + 1)
                    pool.dma_start(g_d[:, g, :], acc[:]).then_inc(s["gate_out"], 16)

            delta_pool(pool)
            for (e, scan), sem in SEM.items():
                pool.wait_ge(sem, TT_ * N_STEP[e, scan])
            for j in range(2):
                pool.dma_start(hH[:, 2 * j:2 * j + 2, :], yc_d[:, 2 * j:2 * j + 2, :]).then_inc(s[f"yH_in{j}"], 16)
                pool.dma_start(hL[:, 2 * j:2 * j + 2, :], yc_d[:, 4 + 2 * j:6 + 2 * j, :]).then_inc(s[f"yL_in{j}"], 16)
            for h in range(H):
                pool.wait_ge(s["mixH"], h + 1)
                nc.gpsimd.tensor_tensor(hL[:, 4 + h, :], oT[:, h, :], hH[:, 4 + h, :].bitcast(F32),
                                        ALU.subtract).then_inc(s["mixL"], 1)
            units(pool, U_OUT + 2, U_FFN + 2, lambda u, u4, i: low(u, u4))

            def p_low(f, slot, cnt):
                pool.wait_ge(s["pH_ready"], cnt)
                nc.gpsimd.tensor_tensor(pL[:, slot, :], fa[:, f % 2, :], pH[:, slot, :].bitcast(F32),
                                        ALU.subtract).then_inc(s["pL_ready"], 1)

            low(U_FFN + 2, U_FFN + 2)
            with pool.Fori(0, GROUPS) as g:
                u0 = U_FFN + 1
                for f in range(4):
                    low(g * 12 + (u0 + 2 * f + 2), u0 + 2 * f + 2)
                    low(g * 12 + (u0 + 2 * f + 3), u0 + 2 * f + 3)
                    if f < 3:
                        p_low(f, f, g * 4 + (f + 1))
                for j in range(4):
                    low(g * 12 + (u0 + 8 + j + 2), u0 + 8 + j + 2)
            for u in range(U_TAIL + 2, N_SPLIT - 1):
                low(u, u)
            p_low(0, 0, 4 * GROUPS + 1)
            low(N_SPLIT - 1, N_SPLIT - 1)

        @block.scalar
        def _(act):
            A = nc.scalar.activation
            act.wait_ge(s["cst_in"], 16)
            act.wait_ge(s["bias_set"], 1)
            for k, col in enumerate((C_C, C_CC)):
                last = A(scT[:, :, k], cst[:, col:col + KT], ACT.Tanh, scale=0.5)
            last.then_inc(s["act_step"], 1)

            def ada_rows(m):
                act.wait_ge(s["ada_used"], 8 * m + 8)
                if m >= 2:
                    act.wait_ge(s["modps_ready"], m - 1)
                for j in range(2):
                    last = A(modrow[:, m % 2, 512 * j:512 * j + 512], ps[0:2, 4 + 2 * (m % 2) + j, :], ACT.Copy)
                last.then_inc(s["modrow_ready"], 1)

            astep = Tally(s["act_step"])
            astep.n = 1

            def square(k, b, sqb, total):
                if k == 0:
                    act.wait_ge(s[f"x_in{b // 2}"], 16)
                else:
                    xb = (U_OUT, B_TAIL + 3)[k - 1] + b
                    act.wait_ge(side_free[xb % 2], xb // 2 + 1)
                if b >= 3:
                    act.wait_ge(s["sq_used"], 6 * k + b - 2)
                if b < KT - 1:
                    A(sqb[:, b % 2, :] if b else total[:], X[:, b, :], ACT.Square).then_inc(s["sq_ready"], 1)
                else:
                    for n in range(NT):
                        c = slice(n * TW, n * TW + TW)
                        A(sqb[:, b % 2, c], X[:, b, c], ACT.Square).then_inc(s["sq_last"], 1)

            def norm_rstd(k, rs, side):
                for n in range(NT):
                    act.wait_ge(s["st_done"], NT * k + n + 1)
                    last = A(rs[:, n * TW:n * TW + TW], bank3(side, n), ACT.Ln, scale=1.0 / D, bias=biases[:, 0:1])
                astep.inc(last)
                act.wait_ge(s["act_step"], astep.value())
                A(rs[:], rs[:], ACT.Exp, scale=-0.5).then_inc(s["rstd_ready"], 1)

            def norm_high(k, ubuf, shift):
                act.wait_ge(s["mod_ready"], 2)
                for b in range(KT):
                    act.wait_ge(s["u_ready"], 8 * k + b + 1)
                    A(hH[:, b, 0:LAT], ubuf[:, b % 2, 0:LAT], ACT.Identity, bias=mod[:, shift * 8 + b, 0:1])
                    A(hH[:, b, LAT:T], ubuf[:, b % 2, LAT:T], ACT.Identity,
                      bias=mod[:, shift * 8 + b, 1:2]).then_inc(s["hH_ready"], 1)

            ada_rows(0)
            ada_rows(1)
            for b in range(KT):
                square(0, b, sq, ss)
                if b == 3:
                    ada_rows(2)
            ada_rows(3)
            norm_rstd(0, rstd, 0)
            norm_high(0, ub, 0)
            ada_rows(4)
            ada_rows(5)

            def high(u, u4, i):
                act.wait_ge(raw_in[u4 % RAW], landed(u4 + N_ADA, i))
                A(wH[:, u4 % 2, :], raw[:, u4 % RAW, :], ACT.Copy).then_inc(s["wh_ready"], 1)

            high(0, 0, 0)
            high(1, 1, 0)

            def evac_rows(side, dst_s, dst_c, row):
                per = TW // GRID
                for n in range(NT):
                    rows = min(per, ROWS - n * per)
                    A(dst_s[:, row + n * per:row + n * per + rows, 1:GRID + 1],
                      bank3(side, n)[:, 0:rows * GRID].rearrange("p (r c) -> p r c", c=GRID), ACT.Copy)
                return A(dst_c[:, 1:CTX + 1], bank3(side, NT - 1)[:, LAT - (NT - 1) * TW:TW], ACT.Copy)

            zs = zp[:, 0:ZS].rearrange("p (r c) -> p r c", c=GRID + 2)
            zc = zp[:, ZS:ZS + ZC]

            act.wait_ge(s["z_init"], 1)

            def qkv_block(b, b4, i):
                act.wait_ge(s["blk_done"], b + 1)
                high(b + 2, b4 + 2, i)
                if b4:
                    act.wait_ge(s["conv_done"], b)
                evac_rows(b4 % 2, zs, zc, 0).then_inc(side_free[b4 % 2], 1)
                act.wait_ge(s["conv_done"], b + 1)
                if b4:
                    act.wait_ge(s["qkv_done"], b)
                A(tb[:], acc[:], ACT.Tanh).then_inc(s["tanh_done"], 1)

            for b in range(4):
                qkv_block(b, b, 0)
            with act.Fori(1, 3) as i:
                for u in range(4):
                    qkv_block(i * 4 + u, 4 + u, i - 1)

            def norm_qk(n):
                act.wait_ge(s["qkv_done"], N_QKV)
                if n:
                    act.wait_ge(s["qm_done"], n)
                A(qn[:], QKV[:, n, :], ACT.Square).then_inc(s["qs_ready"], 1)
                for j in range(NT):
                    act.wait_ge(s["qs_done"], NT * n + (j + 1 if j < 1 else NT))
                    A(qn[:, j * TW:j * TW + TW], ps[:, 6 + (NT * n + j) % 2, 0:TW], ACT.Ln,
                      bias=biases[:, 0:1]).then_inc(s["qs_read"], 1)
                act.wait_ge(s["qs_read"], NT * n + NT)
                A(qn[:], qn[:], ACT.Exp, scale=-0.5, bias=(biases[:, 1:2] if n < H else 0.0)).then_inc(s["qr_ready"], 1)

            b = N_QKV
            act.wait_ge(s["blk_done"], b + 1)
            high(b + 2, b + 2, 0)
            for n in range(NT):
                last = A(abT[:, n * TW:n * TW + TW], bank3(b % 2, n)[0:16], ACT.Copy)
            last.then_inc(side_free[b % 2], 1)
            for j in range(4):
                for k in range(3):
                    b = U_CONV + 3 * j + k
                    act.wait_ge(s["blk_done"], b + 1)
                    high(b + 2, b + 2, 0)
                    if k == 0:
                        if j:
                            act.wait_ge(s["yc_out1"], 16 * j)
                        for n in range(NT):
                            last = A(ccb[:, n * TW:n * TW + TW], bank3(b % 2, n), ACT.Copy)
                        last.then_inc(side_free[b % 2], 1)
                    if k == 2:
                        act.wait_ge(side_free[b % 2], b // 2 + 1)
                        act.wait_ge(s["qkv_done"], N_QKV)
                        if j:
                            act.wait_ge(s["yc_out0"], 16 * j)
                        A(ycH[:], ccb[:], ACT.Copy).then_inc(s["yc_high"], 1)
                    if 0 <= b - B_NORM < 2 * H:
                        norm_qk(b - B_NORM)
            def table_exps():
                act.wait_ge(s["abt_ready"], 1)
                ab = ps[:, 6, 0:TT_ * 16].rearrange("p (t c) -> p t c", c=16)
                A(gA[:], ab[:, :, 0:8], ACT.Exp, scale=-1.0).then_inc(s["g_act"], 1)
                act.wait_ge(s["g_dve"], 2)
                A(gL[:], gL[:], ACT.Exp, scale=-1.0)
                A(gC[:], gC[:], ACT.Exp, scale=-1.0).then_inc(s["g_act"], 1)
                act.wait_ge(s["g_act"], 2)
                A(gC[:], gC[:], ACT.Ln, bias=biases[:, 2:3])
                A(gL[:], gL[:], ACT.Ln, bias=biases[:, 2:3])
                A(cst[:, C_ALOG:C_ALOG + 8], cst[:, C_ALOG:C_ALOG + 8], ACT.Exp).then_inc(s["g_act"], 1)

            def table_fields():
                act.wait_ge(s["g_pe"], 1)

                def gp(k):
                    return ps[:, 7, 72 * k:72 * k + 72].rearrange("p (t d h) -> p t d h", d=2, h=H)

                def field(f):
                    return SC[:, :, :, f:f + 4]

                v4 = lambda t: t[:].rearrange("p t (d h) -> p t d h", d=2)
                act.wait_ge(s["g_dve"], 5)
                A(field(GG), gp(0), ACT.Copy)
                A(field(NG), gp(0), ACT.Copy, scale=-1.0)
                A(v4(gB), gp(0), ACT.Exp)
                A(field(KE), gp(1), ACT.Exp)
                A(field(CD0), gp(2), ACT.Exp)
                A(field(CD1), gp(3), ACT.Exp).then_inc(s["g_act"], 1)

            for g in range(N_GATE):
                b = U_GATE + g
                act.wait_ge(s["blk_done"], b + 1)
                high(b + 2, b + 2, 0)
                if g == 0:
                    act.wait_ge(s["yc_out0"], 16 * 4)
                    act.wait_ge(s["yc_low"], 4)
                if g:
                    act.wait_ge(side_free[(b - 1) % 2], (b - 1) // 2 + 1)
                for n in range(NT):
                    last = A(tb[:, n * TW:n * TW + TW], bank3(b % 2, n), ACT.Tanh, scale=0.5)
                last.then_inc(s["tanh_done"], 1)
                if g == 0:
                    table_exps()
                if g == 2:
                    table_fields()

            act.wait_ge(side_free[(N_Z - 1) % 2], (N_Z - 1) // 2 + 1)
            act.dma_start(g_d[:, N_GATE - 1, :], acc[:]).then_inc(s["gate_last"], 16)

            delta_act(act)

            act.wait_ge(SEM["dve", True], TT_ * N_STEP["dve", True])
            for h in range(H):
                A(osq[:, h, :], oT[:, h, :], ACT.Square).then_inc(s["o_sq"], 1)
            for h in range(H):
                act.wait_ge(s["o_st"], h + 1)
                for n in range(NT):
                    last = A(ors[:, h, n * TW:n * TW + TW], bank3(h % 2, n), ACT.Ln, scale=1.0 / P,
                             bias=biases[:, 0:1])
                last.then_inc(s["o_ln"], 1)
            for h in range(H):
                act.wait_ge(s["o_ln"], h + 1)
                A(ors[:, h, :], ors[:, h, :], ACT.Exp, scale=-0.5).then_inc(s["o_rs"], 1)
            for h in range(H):
                act.wait_ge(s["o_m"], h + 1)
                A(hH[:, 4 + h, :], oT[:, h, :], ACT.Copy).then_inc(s["mixH"], 1)

            for b in range(U_OUT, U_FFN):
                act.wait_ge(s["blk_done"], b + 1)
                high(b + 2, b + 2, 0)
                square(1, b - U_OUT, sq2, ss2)
            norm_rstd(1, rstd2, 1)
            norm_high(1, ub2, 3)

            gs = G[:, 0:GS].rearrange("p (r c) -> p r c", c=GRID + 2)
            gc = G[:, GS:GS + ZC]
            act.wait_ge(s["ffn_init"], 1)

            def gt_block(f, side):
                if not isinstance(f, int) or f:
                    act.wait_ge(s["fc_done"], f)
                evac_rows(side, gs, gc, 1).then_inc(side_free[side], 1)

            def gelu(f, f4):
                act.wait_ge(s["fc_done"], f + 1)
                A(fa[:, f4 % 2, :], fa[:, f4 % 2, :], ACT.Gelu_apprx_tanh).then_inc(s["gelu_done"], 1)

            def p_high(f, f4, slot, side, nfree):
                act.wait_ge(side_free[side], nfree)
                A(pH[:, slot, :], fa[:, f4 % 2, :], ACT.Copy).then_inc(s["pH_ready"], 1)

            act.wait_ge(s["blk_done"], B_FFN + 1)
            high(U_FFN + 2, U_FFN + 2, 0)
            gt_block(0, B_FFN % 2)
            with act.Fori(0, GROUPS) as g:
                ub0, b0 = U_FFN + 1, B_FFN + 1
                for f in range(4):
                    act.wait_ge(s["blk_done"], g * 16 + (b0 + 2 * f + 1))
                    high(g * 12 + (ub0 + 2 * f + 2), ub0 + 2 * f + 2, g * 3)
                    gelu(g * 4 + f, f)
                    gt_block(g * 4 + (f + 1), (b0 + 2 * f) % 2)
                    act.wait_ge(s["blk_done"], g * 16 + (b0 + 2 * f + 2))
                    high(g * 12 + (ub0 + 2 * f + 3), ub0 + 2 * f + 3, g * 3)
                    p_high(g * 4 + f, f, f, (b0 + 2 * f + 1) % 2, g * 8 + ((b0 + 2 * f + 1) // 2 + 1))
                for j in range(4):
                    act.wait_ge(s["blk_done"], g * 16 + (b0 + 8 + 2 * j + 2))
                    high(g * 12 + (ub0 + 8 + j + 2), ub0 + 8 + j + 2, g * 3)
            f0 = 4 * GROUPS
            act.wait_ge(s["blk_done"], B_TAIL + 1)
            high(U_TAIL + 2, U_TAIL + 2, 0)
            gelu(f0, f0)
            gt_block(f0 + 1, B_TAIL % 2)
            act.wait_ge(s["blk_done"], B_TAIL + 2)
            high(U_TAIL + 3, U_TAIL + 3, 0)
            p_high(f0, f0, 0, (B_TAIL + 1) % 2, (B_TAIL + 1) // 2 + 1)
            gelu(f0 + 1, f0 + 1)
            act.wait_ge(s["blk_done"], B_TAIL + 3)
            high(U_TAIL + 4, U_TAIL + 4, 0)
            p_high(f0 + 1, f0 + 1, 1, (B_TAIL + 2) % 2, (B_TAIL + 2) // 2 + 1)
            for b in range(KT):
                square(2, b, sq3, ss3)
            norm_rstd(2, rstd3, 1)
            for b in range(1, KT, 2):
                act.wait_ge(s["y_ready"], b + 1)
                act.dma_start(y_out[:, b, :], X[:, b, :]).then_inc(y_sent[b], 16)

        @block.vector
        def _(dve):
            V = nc.vector
            V.memset(biases[:, 0:1], EPS)
            V.memset(biases[:, 1:2], -0.5 * float(np.log(P)))
            V.memset(biases[:, 2:3], 1.0).then_inc(s["bias_set"], 1)
            dve.wait_ge(s["cst_in"], 16)
            V.tensor_scalar(wqk[:], cst[:, C_QK:C_QK + 36], 0.5, None, ALU.mult)
            V.tensor_scalar(onw[:], cst[:, C_ON:C_ON + 1], 0.5, None, ALU.mult).then_inc(s["oz"], 1)
            dve.wait_ge(s["act_step"], 1)
            dve.wait_ge(s["oz"], 1)
            for k, col in enumerate((C_C, C_CC)):
                last = V.scalar_tensor_tensor(scT[:, :, k], scT[:, :, k], 1.0, cst[:, col:col + KT], ALU.add, ALU.mult)
            last.then_inc(s["sc_ready"], 1)
            dve.wait_ge(s["sc_ready"], 1)
            V.tensor_scalar(scT[:], scT[:], 0.5, None, ALU.mult).then_inc(s["sc_ready"], 1)

            def add_bias(lo, hi, n):
                dve.wait_ge(s["modps_ready"], hi)
                V.tensor_tensor(mod[:, 8 * lo:8 * hi, :],
                                ps[:, 3, 16 * lo:16 * hi].rearrange("p (b k) -> p b k", k=2),
                                cst[:, C_BADA + 8 * lo:C_BADA + 8 * hi].unsqueeze(2).broadcast_to([P, 8 * (hi - lo), 2]),
                                ALU.add).then_inc(s["mod_ready"], 1)
                dve.wait_ge(s["mod_ready"], n)

            def scale_of(dst, row, col):
                V.scalar_tensor_tensor(dst[:], mod[:, 8 * row:8 * row + 8, :], 1.0,
                                       cst[:, col:col + 8].unsqueeze(2).broadcast_to([P, 8, 2]),
                                       ALU.add, ALU.mult).then_inc(s["mod_ready"], 1)

            def norm_apply(k, scl, ubuf, rs, shift):
                dve.wait_ge(s["rstd_ready"], k + 1)

                def u_of(b):
                    if b >= 2:
                        dve.wait_ge(s["hL_ready"], 8 * k + b - 1)
                    for which, (lo, hi) in enumerate(((0, LAT), (LAT, T))):
                        last = V.scalar_tensor_tensor(ubuf[:, b % 2, lo:hi], X[:, b, lo:hi], scl[:, b, which:which + 1],
                                                      rs[:, lo:hi], ALU.mult, ALU.mult)
                    last.then_inc(s["u_ready"], 1)
                u_of(0)
                for b in range(KT):
                    if b + 1 < KT:
                        u_of(b + 1)
                    dve.wait_ge(s["hH_ready"], 8 * k + b + 1)
                    dve.wait_ge(s["u_ready"], 8 * k + b + 1)
                    for which, (lo, hi) in enumerate(((0, LAT), (LAT, T))):
                        last = V.scalar_tensor_tensor(hL[:, b, lo:hi], ubuf[:, b % 2, lo:hi],
                                                      mod[:, shift * 8 + b, which:which + 1],
                                                      hH[:, b, lo:hi].bitcast(F32), ALU.add, ALU.subtract)
                    last.then_inc(s["hL_ready"], 1)

            def add_square(k, b, sqb, total):
                dve.wait_ge(s["sq_ready"], 7 * k + b + 1)
                if b > 1:
                    dve.wait_ge(s["sq_used"], 6 * k + b - 1)
                V.tensor_tensor(total[:], total[:], sqb[:, b % 2, :], ALU.add).then_inc(s["sq_used"], 1)

            add_bias(0, 2, 1)
            scale_of(sc1, 1, C_N1)
            for b in range(1, KT - 1):
                add_square(0, b, sq, ss)
            dve.wait_ge(s["mod_ready"], 2)
            norm_apply(0, sc1, ub, rstd, 0)
            add_bias(2, 6, 3)
            scale_of(sc2, 4, C_N2)
            dve.wait_ge(s["hL_ready"], 8)
            V.memset(zp[:], 0.0).then_inc(s["z_init"], 1)

            zs = zp[:, 0:ZS].rearrange("p (r c) -> p r c", c=GRID + 2)
            zc = zp[:, ZS:ZS + ZC]
            step = Tally(s["dve_step"])
            acs = acc[:, 0:LAT].rearrange("p (r c) -> p r c", c=GRID)
            def conv3(chain, w, done):
                for tap, first in ((1, True), (0, False), (2, False)):
                    for dst, src in ((acs, zs[:, :, tap:tap + GRID]), (acc[:, LAT:T], zc[:, tap:tap + CTX])):
                        if first:
                            last = V.tensor_scalar(dst, src, w(tap), None, ALU.mult)
                        else:
                            last = V.scalar_tensor_tensor(dst, src, w(tap), dst, ALU.mult, ALU.add)
                    if tap != 2:
                        chain.inc(last)
                        dve.wait_ge(chain.sem, chain.value())
                last.then_inc(done, 1)

            def qkv_block(b, b4, chain):
                dve.wait_ge(side_free[b4 % 2], b4 // 2 + 1 if isinstance(b, int) else chain.i * 2 + b4 // 2 + 1)
                if b4:
                    dve.wait_ge(s["qkv_done"], b)
                col = (lambda t: wqk[:, t * 12 + b:t * 12 + b + 1]) if isinstance(b, int) else \
                    (lambda t: wqk[:, bass.ds(b + t * 12, 1)])
                conv3(chain, col, s["conv_done"])
                dve.wait_ge(s["tanh_done"], b + 1)
                dst = QKV[:, b, :] if isinstance(b, int) else QKV[:, bass.ds(b, 1), :]
                src = (lambda t: t[:]) if isinstance(b, int) else (lambda t: t[:].unsqueeze(1))
                V.scalar_tensor_tensor(dst, src(tb), 1.0, src(acc), ALU.add, ALU.mult).then_inc(s["qkv_done"], 1)

            chain = Tally(s["conv_step"])
            for b in range(4):
                qkv_block(b, b, chain)
            with dve.Fori(1, 3) as i:
                chain.enter(i - 1, 8)
                for u in range(4):
                    qkv_block(i * 4 + u, 4 + u, chain)
                chain.leave(2)
            def norm_qk(b):
                n = b - B_NORM - 1
                if 0 <= n < 2 * H:
                    dve.wait_ge(s["qr_ready"], n + 1)
                    V.tensor_tensor(QKV[:, n, :], QKV[:, n, :], qn[:], ALU.mult).then_inc(s["qm_done"], 1)

            for j in range(4):
                b = U_CONV + 3 * j
                dve.wait_ge(s["qkv_done"], N_QKV)
                norm_qk(b)
                dve.wait_ge(side_free[b % 2], b // 2 + 1)
                b += 1
                dve.wait_ge(s["blk_done"], b + 1)
                dve.wait_ge(s["conv_done"], N_QKV + j)
                per = TW // GRID
                for n in range(NT):
                    rows = min(per, ROWS - n * per)
                    V.tensor_tensor(zs[:, n * per:n * per + rows, 1:GRID + 1],
                                    bank3(b % 2, n)[:, 0:rows * GRID].rearrange("p (r c) -> p r c", c=GRID),
                                    ccb[:, n * TW:n * TW + rows * GRID].rearrange("p (r c) -> p r c", c=GRID), ALU.mult)
                V.tensor_tensor(zc[:, 1:CTX + 1], bank3(b % 2, NT - 1)[:, TW - CTX:TW], ccb[:, LAT:T],
                                ALU.mult).then_inc(side_free[b % 2], 1)
                dve.wait_ge(side_free[b % 2], b // 2 + 1)
                dve.wait_ge(s["qkv_done"], N_QKV)
                if j:
                    dve.wait_ge(side_free[(b - 2) % 2], (b - 2) // 2 + 1)
                norm_qk(b)
                conv3(chain, lambda t: cst[:, C_CA + 4 * t + j:C_CA + 4 * t + j + 1], s["conv_done"])
                b += 1
                dve.wait_ge(s["blk_done"], b + 1)
                dve.wait_ge(s["conv_done"], N_QKV + j + 1)
                for n in range(NT):
                    last = V.tensor_tensor(ccb[:, n * TW:n * TW + TW], bank3(b % 2, n), acc[:, n * TW:n * TW + TW],
                                           ALU.mult)
                last.then_inc(side_free[b % 2], 1)
                norm_qk(b)
            v4 = lambda t: t[:].rearrange("p t (d h) -> p t d h", d=2)

            def field(f):
                return SC[:, :, :, f:f + 4]

            def table_alpha():
                ab = ps[:, 6, 0:TT_ * 16].rearrange("p (t c) -> p t c", c=16)
                dve.wait_ge(s["g_act"], 1)
                b8 = lambda col: cst[:, col:col + 8].unsqueeze(1).broadcast_to([P, TT_, 8])
                V.tensor_copy(gL[:], ab[:, :, 0:8])
                V.tensor_tensor(gB[:], ab[:, :, 8:16], b8(C_DTB), ALU.add).then_inc(s["g_dve"], 1)
                dve.wait_ge(s["g_dve"], 1)
                V.scalar_tensor_tensor(gC[:], gB[:], -1.0, gB[:], ALU.mult, ALU.max)
                V.scalar_tensor_tensor(gL[:], gL[:], -1.0, gL[:], ALU.mult, ALU.max)
                V.tensor_scalar(gA[:], gA[:], 1.0, None, ALU.add).then_inc(s["g_dve"], 1)
                dve.wait_ge(s["g_dve"], 2)
                dve.wait_ge(s["g_act"], 3)
                V.reciprocal(gA[:], gA[:])
                V.scalar_tensor_tensor(gL[:], ab[:, :, 0:8], 0.0, gL[:], ALU.min, ALU.subtract)
                V.scalar_tensor_tensor(la[:], gB[:], 0.0, gC[:], ALU.max, ALU.add).then_inc(s["g_dve"], 1)
                dve.wait_ge(s["g_dve"], 3)
                V.scalar_tensor_tensor(la[:], la[:], -1.0, b8(C_ALOG), ALU.mult, ALU.mult).then_inc(s["g_dve"], 1)
                dve.wait_ge(s["g_dve"], 4)
                V.tensor_copy(field(BT), v4(gA)).then_inc(s["g_dve"], 1)

            def table_fields():
                dve.wait_ge(s["g_act"], 4)
                V.tensor_tensor(field(BG), v4(gA), v4(gB), ALU.mult)
                V.tensor_tensor(field(GE), field(GG), v4(gL), ALU.add).then_inc(s["sc_tab"], 1)

            for g in range(N_GATE):
                b = U_GATE + g
                dve.wait_ge(s["tanh_done"], N_QKV + g + 1)
                if g:
                    dve.wait_ge(s["gate_out"], 16 * g)
                else:
                    dve.wait_ge(side_free[(b - 1) % 2], (b - 1) // 2 + 1)
                for n in range(NT):
                    last = V.scalar_tensor_tensor(acc[:, n * TW:n * TW + TW], tb[:, n * TW:n * TW + TW], 1.0,
                                                  bank3(b % 2, n), ALU.add, ALU.mult)
                last.then_inc(side_free[b % 2], 1)
                if g == 0:
                    table_alpha()
                if g == 2:
                    table_fields()

            delta_dve(dve)
            dve.wait_ge(SEM["dve", True], TT_ * N_STEP["dve", True])

            dve.wait_ge(s["gt_in"], 16)
            for h in range(H):
                dve.wait_ge(s["o_rs"], h + 1)
                step.inc(V.tensor_tensor(oT[:, h, :], oT[:, h, :], ors[:, h, :], ALU.mult))
                dve.wait_ge(s["dve_step"], step.value())
                V.scalar_tensor_tensor(oT[:, h, :], oT[:, h, :], onw[:, 0:1], og[:, h, :], ALU.mult,
                                       ALU.mult).then_inc(s["o_m"], 1)

            def residual(b, side, ob, gate):
                xs = (lambda lo, hi: X[:, ob, lo:hi])
                for n in range(NT):
                    lo, hi = n * TW, min((n + 1) * TW, LAT)
                    last = V.scalar_tensor_tensor(xs(lo, hi), bank3(side, n)[:, 0:hi - lo], mod[:, gate * 8 + ob, 0:1],
                                                  xs(lo, hi), ALU.mult, ALU.add)
                last = V.scalar_tensor_tensor(xs(LAT, T), bank3(side, NT - 1)[:, TW - CTX:TW],
                                              mod[:, gate * 8 + ob, 1:2], xs(LAT, T), ALU.mult, ALU.add)
                last.then_inc(side_free[side], 1)

            dve.wait_ge(s["x2_in"], 16)
            for ob in range(KT):
                b = U_OUT + ob
                if ob > 1:
                    add_square(1, ob - 1, sq2, ss2)
                dve.wait_ge(s["blk_done"], b + 1)
                residual(b, b % 2, ob, 2)
            dve.wait_ge(side_free[(U_FFN - 1) % 2], (U_FFN - 1) // 2 + 1)
            norm_apply(1, sc2, ub2, rstd2, 3)
            dve.wait_ge(s["hL_ready"], 16)
            V.memset(G[:], 0.0).then_inc(s["ffn_init"], 1)

            gs = G[:, 0:GS].rearrange("p (r c) -> p r c", c=GRID + 2)
            gc = G[:, GS:GS + ZC]
            fch = Tally(s["dve_step"])
            fch.n = step.n

            def conv9(f, f4, side, nfree, beside=None):
                dve.wait_ge(side_free[side], nfree)
                dst = fa[:, f4 % 2, 0:LAT].rearrange("p (r c) -> p r c", c=GRID)
                dctx = fa[:, f4 % 2, LAT:T]
                w = (lambda t: cst[:, C_FFN + FB * t + f:C_FFN + FB * t + f + 1]) if isinstance(f, int) else \
                    (lambda t: cst[:, bass.ds(f + (C_FFN + FB * t), 1)])
                first = True
                for dy in range(3):
                    for dx in range(3):
                        src = gs[:, dy:dy + ROWS, dx:dx + GRID]
                        if first:
                            V.tensor_scalar(dst, src, w(3 * dy + dx), None, ALU.mult)
                            last = V.tensor_scalar(dctx, gc[:, 0:CTX], w(3), None, ALU.mult)
                            first = False
                        else:
                            last = V.scalar_tensor_tensor(dst, src, w(3 * dy + dx), dst, ALU.mult, ALU.add)
                            if dy == 1 and dx:
                                last = V.scalar_tensor_tensor(dctx, gc[:, dx:dx + CTX], w(3 + dx), dctx,
                                                              ALU.mult, ALU.add)
                        if (dy, dx) == (2, 2):
                            last.then_inc(s["fc_done"], 1)
                        else:
                            fch.inc(last)
                            if beside and 3 * dy + dx in beside:
                                beside[3 * dy + dx]()
                            dve.wait_ge(s["dve_step"], fch.value())

            def product(f, f4, side, ndone):
                dve.wait_ge(s["gelu_done"], f + 1)
                dve.wait_ge(s["blk_done"], ndone)
                for n in range(NT):
                    last = V.tensor_tensor(fa[:, f4 % 2, n * TW:n * TW + TW], fa[:, f4 % 2, n * TW:n * TW + TW],
                                           bank3(side, n), ALU.mult)
                last.then_inc(side_free[side], 1)

            def p_low(f4, slot, nhigh):
                dve.wait_ge(s["pH_ready"], nhigh)
                V.tensor_tensor(pL[:, slot, :], fa[:, f4 % 2, :], pH[:, slot, :].bitcast(F32),
                                ALU.subtract).then_inc(s["pL_last"], 1)

            conv9(0, 0, B_FFN % 2, B_FFN // 2 + 1)

            def group(g, dyn):
                b0 = B_FFN + 1
                for f in range(4):
                    fi = g * 4 + f
                    bg = b0 + 2 * f
                    if f:
                        dve.wait_ge(s["pL_ready"], g * 3 + f)
                    elif dyn:
                        dve.wait_ge(s["pL_last"], g)
                    beside = {5: lambda: product(fi, f, (bg + 1) % 2, g * 16 + (bg + 2))}
                    if f == 3:
                        beside[6] = lambda: p_low(3, 3, g * 4 + 4)
                    conv9(g * 4 + (f + 1), f + 1, bg % 2, g * 8 + (bg // 2 + 1), beside)
                for ob in range(KT):
                    b = b0 + 8 + ob
                    dve.wait_ge(s["blk_done"], g * 16 + (b + 1))
                    residual(b, b % 2, ob, 5)
            group(0, False)
            with dve.Fori(1, GROUPS) as g:
                fch.enter(g - 1, 32)
                group(g, True)
                fch.leave(GROUPS - 1)
            f0 = 4 * GROUPS
            dve.wait_ge(s["pL_last"], GROUPS)
            conv9(f0 + 1, f0 + 1, B_TAIL % 2, B_TAIL // 2 + 1,
                  {5: lambda: product(f0, f0, (B_TAIL + 1) % 2, B_TAIL + 2)})
            product(f0 + 1, f0 + 1, (B_TAIL + 2) % 2, B_TAIL + 3)
            p_low(f0 + 1, 1, f0 + 2)
            for ob in range(KT):
                b = B_TAIL + 3 + ob
                if ob == KT - 1:
                    add_square(2, KT - 2, sq3, ss3)
                dve.wait_ge(s["blk_done"], b + 1)
                residual(b, b % 2, ob, 5)
                if 1 < ob < KT - 1:
                    add_square(2, ob - 1, sq3, ss3)
            dve.wait_ge(side_free[(B_TAIL + 10) % 2], (B_TAIL + 10) // 2 + 1)
            dve.wait_ge(s["rstd_ready"], 3)
            for b in range(KT):
                V.scalar_tensor_tensor(X[:, b, :], X[:, b, :], cst[:, C_NF + b:C_NF + b + 1], rstd3[:],
                                       ALU.mult, ALU.mult).then_inc(s["y_ready"], 1)

        @block.tensor
        def _(pe):
            M = nc.tensor.matmul

            def ada(m):
                for kt in range(KT):
                    u = 8 * m + kt
                    pe.wait_ge(raw_in[u % RAW], (u // RAW + 1) * 16)
                    for j in range(2):
                        last = M(ps[0:2, 4 + 2 * (m % 2) + j, :], scT[:, kt, :], raw[:, u % RAW, 512 * j:512 * j + 512],
                                 start=(kt == 0), stop=(kt == KT - 1))
                    last.then_inc(s["ada_used"], 1)

            def turn(m):
                pe.wait_ge(s["modrow_ready"], m + 1)
                for b in range(KT):
                    last = M(ps[:, 3, 16 * m + 2 * b:16 * m + 2 * b + 2], modrow[:, m % 2, P * b:P * b + P],
                             mat("ident")[0:2, 0:2], start=True, stop=True)
                last.then_inc(s["modps_ready"], 1)

            def stats(k, total, last_sq, side):
                pe.wait_ge(s["sq_used"], 6 * k + 6)
                for n in range(NT):
                    M(bank3(side, n), mat("ones"), total[:, n * TW:n * TW + TW], start=True, stop=False)
                for n in range(NT):
                    pe.wait_ge(s["sq_last"], NT * k + n + 1)
                    M(bank3(side, n), mat("ones"), last_sq[:, n * TW:n * TW + TW], start=False,
                      stop=True).then_inc(s["st_done"], 1)

            pe.wait_ge(s["sc_ready"], 2)
            ada(0)
            ada(1)
            pe.wait_ge(s["mat_in"], 16)
            turn(0)
            turn(1)
            ada(2)
            ada(3)
            pe.wait_ge(s["mod_ready"], 1)
            turn(2)
            turn(3)
            stats(0, ss, sq[:, 1, :], 0)
            ada(4)
            ada(5)
            turn(4)
            turn(5)
            pe.wait_ge(s["mod_ready"], 3)

            def product_step(side, k, kts, left, right):
                rh, rl = right(k)
                for w, lo in ((wH, False), (wL, True)):
                    lhs = left(w, k)
                    for n in range(NT):
                        c = slice(n * TW, n * TW + TW)
                        last = M(bank3(side, n), lhs, rh[:, c], start=(k == 0 and not lo),
                                 stop=(lo and k == kts - 1))
                        if not lo:
                            M(bank3(side, n), lhs, rl[:, c], start=False, stop=False)
                return last

            def product_block(side, kts, left, right, ready):
                for k in range(kts):
                    ready(k)
                    last = product_step(side, k, kts, left, right)
                last.then_inc(s["blk_done"], 1)

            def h_of(k):
                return hH[:, k, :], hL[:, k, :]

            def w_of(u4):
                return lambda w, k: w[:, u4 % 2, k * P:k * P + P]

            def model_block(u, u4, free, ready):
                pe.wait_ge(s["wl_ready"], u + 1)
                if free[1] is not None:
                    pe.wait_ge(side_free[free[0]], free[1])
                product_block(free[0], KT, w_of(u4), h_of, ready)

            def model_pair(u, b, ready):
                for k in range(KT):
                    ready(k)
                    for o in range(2):
                        if k == 0:
                            pe.wait_ge(s["wl_ready"], u + o + 1)
                            if b + o >= 2:
                                pe.wait_ge(side_free[(b + o) % 2], (b + o) // 2)
                        last = product_step((b + o) % 2, k, KT, w_of(u + o), h_of)
                        if k == KT - 1:
                            last.then_inc(s["blk_done"], 1)

            no_wait = lambda k: None
            h1_ready = lambda k: pe.wait_ge(s["hL_ready"], k + 1)
            model_pair(0, 0, h1_ready)
            for u in (2, 3):
                model_block(u, u, (u % 2, u // 2), no_wait)
            units(pe, 4, B_NORM, lambda u, u4, i: model_block(u, u4, (u4 % 2, i * 2 + u4 // 2), no_wait))
            model_block(B_NORM, B_NORM, (B_NORM % 2, B_NORM // 2), no_wait)

            def norm_qk(k, n, base):
                if k not in (4, 5, 6):
                    return
                j = k - 4
                m = NT * n + j
                if j == 0:
                    pe.wait_ge(s["qs_ready"], base + (n + 1))
                if n or j == 2 or not isinstance(base, int):
                    pe.wait_ge(s["qs_read"], base * NT + (m - 1))
                M(ps[:, 6 + m % 2, 0:TW], mat("ones"), qn[:, j * TW:j * TW + TW], start=True,
                  stop=True).then_inc(s["qs_done"], 1)

            for half in range(2):
                for v in range(4):
                    n = 4 * half + v
                    u = B_NORM + 1 + n
                    model_block(u, u, (u % 2, u // 2), lambda k, n=n: norm_qk(k, n, 0))
            def table_turn():
                pe.wait_ge(side_free[N_QKV % 2], N_QKV // 2 + 1)
                pe.wait_ge(s["qs_read"], 2 * H * NT)
                for t in range(TT_):
                    last = M(ps[:, 6, 16 * t:16 * t + 16], abT[:, t * P:t * P + P], mat("ident")[0:16, 0:16],
                             start=True, stop=True)
                last.then_inc(s["abt_ready"], 1)

            def table_sums():
                pe.wait_ge(s["g_dve"], 4)
                for d in range(2):
                    for k, m in enumerate((("UI", "LS"), ("LI", "US"))[d]):
                        M(ps[:, 7, 72 * k:72 * k + 72].rearrange("p (t c) -> p t c", c=8)[:, :, 4 * d:4 * d + 4],
                          mat(m), la[:, :, 4 * d:4 * d + 4], start=True, stop=True)
                for k in range(2):
                    last = M(ps[:, 7, 144 + 72 * k:216 + 72 * k], mat(f"CB{k}"), la[:].rearrange("p t c -> p (t c)"),
                             start=True, stop=True)
                last.then_inc(s["g_pe"], 1)

            table = {(0, 4): table_turn, (2, 4): table_sums}
            for g in range(N_GATE):
                u = U_GATE + g
                model_block(u, u, (u % 2, u // 2), lambda k, g=g: table[g, k]() if (g, k) in table else None)

            for b in (N_Z - 2, N_Z - 1):
                pe.wait_ge(side_free[b % 2], b // 2 + 1)
            delta_pe(pe)

            for h in range(H):
                pe.wait_ge(s["o_sq"], h + 1)
                if h >= 2:
                    pe.wait_ge(s["o_ln"], h - 1)
                for n in range(NT):
                    last = M(bank3(h % 2, n), mat("ones"), osq[:, h, n * TW:n * TW + TW], start=True, stop=True)
                last.then_inc(s["o_st"], 1)
            pe.wait_ge(s["o_ln"], H)

            def mix_ready(k):
                if k < 4:
                    pe.wait_ge(s[f"yH_in{k // 2}"], 16)
                    pe.wait_ge(s[f"yL_in{k // 2}"], 16)
                else:
                    pe.wait_ge(s["mixL"], k - 3)
            model_pair(U_OUT, U_OUT, mix_ready)
            for u in range(U_OUT + 2, U_FFN):
                model_block(u, u, (u % 2, u // 2), no_wait)
            pe.wait_ge(side_free[(B_FFN - 2) % 2], (B_FFN - 2) // 2 + 1)
            stats(1, ss2, sq2[:, 1, :], 1)
            pe.wait_ge(s["rstd_ready"], 2)
            model_pair(U_FFN, B_FFN, lambda k: pe.wait_ge(s["hL_ready"], 9 + k))

            def p_of(k):
                return pH[:, k, :], pL[:, k, :]

            def down(u, u4, b, bdyn, fis, width, nlow, nlast, first):
                left = lambda o: lambda w, k: w[:, u4 % 2, (k * width + o) * P:(k * width + o) * P + P]
                pe.wait_ge(s["wl_ready"], u + 1)
                if first:
                    pe.wait_ge(s["pL_ready"], nlow)
                    for o in range(2):
                        pe.wait_ge(side_free[(b + o) % 2], bdyn + (b + o) // 2)
                        for k in range(fis - 1):
                            product_step((b + o) % 2, k, fis, left(o), p_of)
                    pe.wait_ge(s["pL_last"], nlast)
                    for o in range(2):
                        product_step((b + o) % 2, fis - 1, fis, left(o), p_of).then_inc(s["blk_done"], 1)
                for o in range(2 if first else 0, width):
                    pe.wait_ge(side_free[(b + o) % 2], bdyn + (b + o) // 2)
                    product_block((b + o) % 2, fis, left(o), p_of, no_wait)

            with pe.Fori(0, GROUPS) as g:
                for k in range(1, 8):
                    u, b = U_FFN + 1 + k, B_FFN + 1 + k
                    model_block(g * 12 + u, u, (b % 2, g * 8 + b // 2), no_wait)
                for j in range(4):
                    u, b = U_FFN + 9 + j, B_FFN + 9 + 2 * j
                    down(g * 12 + u, u, b, g * 8, 4, 2, g * 3 + 3, g + 1, j == 0)
                u, b = U_FFN + 13, B_FFN + 17
                model_block(g * 12 + u, u, (b % 2, g * 8 + b // 2), no_wait)
            for k in range(1, 3):
                model_block(U_TAIL + k, U_TAIL + k, ((B_TAIL + k) % 2, (B_TAIL + k) // 2), no_wait)
            for j in range(2):
                down(U_TAIL + 3 + j, U_TAIL + 3 + j, B_TAIL + 3 + 4 * j, 0, 2, 4, 3 * GROUPS + 1, GROUPS + 1, j == 0)
            pe.wait_ge(side_free[(B_TAIL + 9) % 2], (B_TAIL + 9) // 2 + 1)
            stats(2, ss3, sq3[:, 1, :], 1)


def kernel(x_prompt, x_sample, state_deltanet, c, c_ctx, w_ada, b_ada, norm1_w, w_in, conv_a_w, qkv_conv_w,
           a_log, dt_bias, o_norm_w, w_out, norm2_w, w_up, ffn_conv_w, w_down, final_norm_w):
    import concourse.bacc as bacc
    from concourse.bass_utils import run_bass_kernel_spmd

    f = lambda a: np.asarray(a, dtype=np.float32)
    cols = lambda a: f(a).reshape(-1, P).T
    mats, preds, ind = constants()
    rep = lambda a: np.broadcast_to(f(a).reshape(1, -1), (P, 2 * H))
    const = np.ascontiguousarray(np.concatenate([
        cols(b_ada), cols(norm1_w), cols(norm2_w), cols(final_norm_w), cols(conv_a_w), cols(qkv_conv_w),
        cols(o_norm_w), cols(c), cols(c_ctx), cols(ffn_conv_w), rep(dt_bias), rep(a_log), ind, mats], 1))
    assert const.shape[1] == N_CONST
    tok = np.concatenate([f(x_sample)[0], f(x_prompt)[0]], 0)
    xT = np.ascontiguousarray(tok.T.reshape(KT, P, T).transpose(1, 0, 2))
    s0 = np.ascontiguousarray(f(state_deltanet)[0, 0].transpose(2, 0, 1, 3))

    def unit(w):
        k, n = w.shape
        return w.reshape(k // P, P, n).transpose(1, 0, 2).reshape(P, -1)

    wa, wi, wo, wu, wd = (f(a)[0] for a in (w_ada, w_in, w_out, w_up, w_down))
    cw = D // 2
    us = [wa[k * P:k * P + P, m * D:m * D + D] for m in range(6) for k in range(KT)]
    blk = lambda lo: unit(wi[:, lo:lo + P])
    q0 = 3 * cw
    us += [blk(q0 + b * P) for b in range(N_QKV)]
    g0 = q0 + 3 * H * P
    ab0 = g0 + H * P
    us.append(unit(np.concatenate([wi[:, ab0:ab0 + 4 * H], wi[:, ab0 - P + 4 * H:ab0]], 1)))
    for j in range(4):
        us += [blk(cw + j * P), blk(2 * cw + j * P), blk(j * P)]
    us += [blk(g0 + b * P) for b in range(N_GATE)]
    us += [unit(wo[:, b * P:b * P + P]) for b in range(KT)]
    gt = lambda b: unit(wu[:, DFF + b * P:DFF + b * P + P])
    up = lambda b: unit(wu[:, b * P:b * P + P])
    us.append(gt(0))
    for g in range(GROUPS):
        for b in range(4 * g, 4 * g + 4):
            us += [gt(b + 1), up(b)]
        us += [unit(wd[4 * g * P:4 * (g + 1) * P, j * 256:j * 256 + 256]) for j in range(4)]
    b = 4 * GROUPS
    us += [gt(b + 1), up(b), up(b + 1)]
    us += [unit(wd[b * P:(b + 2) * P, j * 512:j * 512 + 512]) for j in range(2)]
    assert len(us) == N_UNITS
    wts = np.stack(us)

    nc = bacc.Bacc("TRN2", target_bir_lowering=False, num_devices=1)
    ins = {"const": const, "preds": preds.reshape(P, -1, Q), "xT": xT, "s0": s0, "wts": wts}
    dts = {"preds": I32}
    args = [nc.dram_tensor(k, v.shape, dts.get(k, F32), kind="ExternalInput").ap() for k, v in ins.items()]
    y = nc.dram_tensor("y", (P, KT, T), F32, kind="ExternalOutput").ap()
    st = nc.dram_tensor("st", (P, 2, H, P), F32, kind="ExternalOutput").ap()
    yc = nc.dram_tensor("yc", (P, 8, T), F32R, kind="Internal").ap()
    gd = nc.dram_tensor("gd", (P, 4, T), F32, kind="Internal").ap()
    build(nc, *args, y, st, yc, gd)
    r = run_bass_kernel_spmd(nc, [ins], core_ids=[0]).results[0]
    yt = r["y"].transpose(1, 0, 2).reshape(D, T).T
    return (np.ascontiguousarray(yt[LAT:])[None], np.ascontiguousarray(yt[:LAT])[None],
            np.ascontiguousarray(r["st"].transpose(1, 2, 0, 3))[None, None])
```
